# Optimizing a Trainium2 kernel written in Bass

```python
import math
import jax, jax.numpy as jnp
from jax import lax
import numpy as np

D_MODEL = 1024
BATCH = 1
SEQ = 256
DEPTH = 1

RMS_EPS = 1e-6
N_BRANCHES = 3
MIX_WIDTH = D_MODEL
ATT_HEAD_DIM = 64
ATT_HEADS = MIX_WIDTH // ATT_HEAD_DIM
BLOCK_Q = 128
SSD_HEAD_DIM = 64
SSD_HEADS = MIX_WIDTH // SSD_HEAD_DIM
SSD_GROUPS = 4
SSD_HEADS_PER_GROUP = SSD_HEADS // SSD_GROUPS
SSD_STATE = 128
SSD_CONV = 4
SSD_CHUNK = 128
SSD_CONV_DIM = MIX_WIDTH + 2 * SSD_GROUPS * SSD_STATE
ML_HEADS = 4
ML_HEAD_DIM = MIX_WIDTH // ML_HEADS
ML_CONV = 4
ML_CHUNK = 128
N_EXPERT_GROUPS = 8
EXPERTS_PER_GROUP = 8
N_EXPERTS = N_EXPERT_GROUPS * EXPERTS_PER_GROUP
TOP_K = 2
D_EXPERT = D_MODEL // 2
MOE_BLOCK = 128

SPLIT_SIZES = (
    MIX_WIDTH, MIX_WIDTH, MIX_WIDTH, ATT_HEADS,
    MIX_WIDTH, SSD_CONV_DIM, SSD_HEADS,
    MIX_WIDTH, MIX_WIDTH, MIX_WIDTH, ML_HEADS, ML_HEADS, MIX_WIDTH,
    N_BRANCHES * D_MODEL,
)
SPLIT_POINTS = tuple(int(v) for v in np.cumsum(SPLIT_SIZES)[:-1])
IN_WIDTH = int(sum(SPLIT_SIZES))

kernel_name = 'hybrid_fox_ssd_mlstm_hmoe'

def _rmsnorm(x, w):
    xf = x.astype(jnp.float32)
    y = xf * lax.rsqrt(jnp.mean(xf * xf, axis=-1, keepdims=True) + RMS_EPS)
    return (y * w.astype(jnp.float32)).astype(x.dtype)

def _group_rmsnorm(x, w, n_groups):
    shp = x.shape
    xg = x.reshape(shp[:-1] + (n_groups, shp[-1] // n_groups)).astype(jnp.float32)
    y = xg * lax.rsqrt(jnp.mean(xg * xg, axis=-1, keepdims=True) + RMS_EPS)
    return (y.reshape(shp) * w.astype(jnp.float32)).astype(x.dtype)

def _causal_depthwise_conv(x, w, b):
    K = w.shape[0]
    L = x.shape[1]
    xp = jnp.pad(x, ((0, 0), (K - 1, 0), (0, 0)))
    y = xp[:, 0:L] * w[0]
    for k in range(1, K):
        y = y + xp[:, k:k + L] * w[k]
    return y + b

def _forgetting_attention(q, k, v, f_logit):
    Bsz, L, _ = q.shape
    to_heads = lambda t: t.reshape(Bsz, L, ATT_HEADS, ATT_HEAD_DIM).transpose(0, 2, 1, 3)
    q, k, v = to_heads(q), to_heads(k), to_heads(v)
    F = jnp.cumsum(jax.nn.log_sigmoid(f_logit.astype(jnp.float32)), axis=1).transpose(0, 2, 1)
    scale = ATT_HEAD_DIM ** -0.5
    outs = []
    for blk in range(L // BLOCK_Q):
        s0, s1 = blk * BLOCK_Q, (blk + 1) * BLOCK_Q
        logits = jnp.einsum('bhqd,bhkd->bhqk', q[:, :, s0:s1], k[:, :, :s1],
                            preferred_element_type=jnp.float32) * scale
        logits = logits + F[:, :, s0:s1, None] - F[:, :, None, :s1]
        q_pos = s0 + jnp.arange(BLOCK_Q)
        k_pos = jnp.arange(s1)
        logits = jnp.where(k_pos[None, :] <= q_pos[:, None], logits, -jnp.inf)
        p = jax.nn.softmax(logits, axis=-1).astype(v.dtype)
        outs.append(jnp.einsum('bhqk,bhkd->bhqd', p, v[:, :, :s1]))
    o = jnp.concatenate(outs, axis=2)
    return o.transpose(0, 2, 1, 3).reshape(Bsz, L, MIX_WIDTH)

def _ssd_mixer(z, xbc, dt_raw, conv_w, conv_b, dt_bias, a_log, d_skip, norm_w):
    dtype = z.dtype
    Bsz, L, _ = z.shape
    nc, Q, G, Hg, P, N = L // SSD_CHUNK, SSD_CHUNK, SSD_GROUPS, SSD_HEADS_PER_GROUP, SSD_HEAD_DIM, SSD_STATE
    xbc = jax.nn.silu(_causal_depthwise_conv(xbc, conv_w, conv_b)).astype(jnp.float32)
    xs, Bm, Cm = jnp.split(xbc, (MIX_WIDTH, MIX_WIDTH + G * N), axis=-1)
    xs = xs.reshape(Bsz, nc, Q, G, Hg, P)
    Bm = Bm.reshape(Bsz, nc, Q, G, N)
    Cm = Cm.reshape(Bsz, nc, Q, G, N)
    dt = jax.nn.softplus(dt_raw.astype(jnp.float32) + dt_bias.astype(jnp.float32)).reshape(Bsz, nc, Q, G, Hg)
    A = -jnp.exp(a_log.astype(jnp.float32)).reshape(G, Hg)
    a_cum = jnp.cumsum(dt * A, axis=2)
    seg = a_cum[:, :, :, None] - a_cum[:, :, None, :]
    causal = jnp.tril(jnp.ones((Q, Q), dtype=bool))[:, :, None, None]
    decay = jnp.exp(jnp.where(causal, seg, -jnp.inf))
    cb = jnp.einsum('bcign,bcjgn->bcijg', Cm, Bm)
    w_ij = cb[..., None] * decay * dt[:, :, None]
    y_diag = jnp.einsum('bcijgh,bcjghp->bcighp', w_ij, xs)
    decay_to_end = jnp.exp(a_cum[:, :, -1:] - a_cum)
    states = jnp.einsum('bcjgn,bcjgh,bcjghp->bcghpn', Bm, decay_to_end * dt, xs)
    chunk_decay = jnp.exp(a_cum[:, :, -1])

    def step(s, inp):
        st, dec = inp
        return s * dec[..., None, None] + st, s

    init = jnp.zeros((Bsz, G, Hg, P, N), jnp.float32)
    _, prev = lax.scan(step, init, (jnp.moveaxis(states, 1, 0), jnp.moveaxis(chunk_decay, 1, 0)))
    prev = jnp.moveaxis(prev, 0, 1)
    y_off = jnp.einsum('bcign,bcghpn,bcigh->bcighp', Cm, prev, jnp.exp(a_cum))
    y = y_diag + y_off + xs * d_skip.astype(jnp.float32).reshape(G, Hg)[:, :, None]
    y = y.reshape(Bsz, L, MIX_WIDTH)
    y = y * jax.nn.silu(z.astype(jnp.float32))
    return _group_rmsnorm(y, norm_w, SSD_GROUPS).astype(dtype)

def _mlstm_mixer(q, k, v, i_raw, f_raw, o_raw, conv_w, conv_b, i_bias, f_bias, norm_w):
    dtype = q.dtype
    Bsz, L, _ = q.shape
    nc, Q, H, d = L // ML_CHUNK, ML_CHUNK, ML_HEADS, ML_HEAD_DIM
    qk = jax.nn.silu(_causal_depthwise_conv(jnp.concatenate([q, k], axis=-1), conv_w, conv_b))
    q, k = jnp.split(qk.astype(jnp.float32), 2, axis=-1)
    k = k * (d ** -0.5)
    chunked = lambda t: t.reshape(Bsz, nc, Q, H, d).transpose(1, 0, 3, 2, 4)
    gate_chunked = lambda t: t.reshape(Bsz, nc, Q, H).transpose(1, 0, 3, 2)
    qc, kc, vc = chunked(q), chunked(k), chunked(v.astype(jnp.float32))
    log_i = gate_chunked(i_raw.astype(jnp.float32) + i_bias.astype(jnp.float32))
    log_f = gate_chunked(jax.nn.log_sigmoid(f_raw.astype(jnp.float32) + f_bias.astype(jnp.float32)))
    causal = jnp.tril(jnp.ones((Q, Q), dtype=bool))

    def step(carry, inp):
        C, n, m = carry
        qb, kb, vb, ib, fb = inp
        b = jnp.cumsum(fb, axis=-1)
        g = b[..., -1]
        D = jnp.where(causal, b[..., :, None] - b[..., None, :] + ib[..., None, :], -jnp.inf)
        m_inter = b + m[..., None]
        m_t = jnp.maximum(m_inter, jnp.max(D, axis=-1))
        ws = jnp.exp(D - m_t[..., None]) * jnp.einsum('bhtd,bhsd->bhts', qb, kb)
        inter = jnp.exp(m_inter - m_t)
        num = jnp.einsum('bhts,bhsv->bhtv', ws, vb) + inter[..., None] * jnp.einsum('bhtd,bhdv->bhtv', qb, C)
        den = jnp.sum(ws, axis=-1) + inter * jnp.einsum('bhtd,bhd->bht', qb, n)
        h = num / jnp.maximum(jnp.abs(den), jnp.exp(-m_t))[..., None]
        e = g[..., None] - b + ib
        m_new = jnp.maximum(g + m, jnp.max(e, axis=-1))
        wk = jnp.exp(e - m_new[..., None])
        carry_scale = jnp.exp(g + m - m_new)
        C = carry_scale[..., None, None] * C + jnp.einsum('bhs,bhsd,bhsv->bhdv', wk, kb, vb)
        n = carry_scale[..., None] * n + jnp.einsum('bhs,bhsd->bhd', wk, kb)
        return (C, n, m_new), h

    init = (jnp.zeros((Bsz, H, d, d), jnp.float32), jnp.zeros((Bsz, H, d), jnp.float32),
            jnp.zeros((Bsz, H), jnp.float32))
    _, hs = lax.scan(step, init, (qc, kc, vc, log_i, log_f))
    hs = hs.transpose(1, 0, 3, 2, 4).reshape(Bsz, L, MIX_WIDTH)
    hs = _group_rmsnorm(hs, norm_w, ML_HEADS).astype(jnp.float32)
    return (jax.nn.sigmoid(o_raw.astype(jnp.float32)) * hs).astype(dtype)

def _hybrid_mixer(h, w_in, att_f_bias, ssd_conv_w, ssd_conv_b, ssd_dt_bias, ssd_a_log, ssd_d, ssd_norm_w,
                  ml_conv_w, ml_conv_b, ml_i_bias, ml_f_bias, ml_norm_w, gate_bias, w_branch, w_out):
    (a_q, a_k, a_v, a_f, s_z, s_xbc, s_dt, m_q, m_k, m_v, m_i, m_f, m_o, g_raw) = [
        h @ w for w in jnp.split(w_in, SPLIT_POINTS, axis=-1)]
    y_att = _forgetting_attention(a_q, a_k, a_v, a_f + att_f_bias)
    y_ssd = _ssd_mixer(s_z, s_xbc, s_dt, ssd_conv_w, ssd_conv_b, ssd_dt_bias, ssd_a_log, ssd_d, ssd_norm_w)
    y_ml = _mlstm_mixer(m_q, m_k, m_v, m_i, m_f, m_o, ml_conv_w, ml_conv_b, ml_i_bias, ml_f_bias, ml_norm_w)
    gates = jax.nn.sigmoid((g_raw + gate_bias).astype(jnp.float32)).astype(h.dtype)
    gates = gates.reshape(h.shape[:-1] + (N_BRANCHES, D_MODEL))
    u = (gates[..., 0, :] * (y_att @ w_branch[0])
         + gates[..., 1, :] * (y_ssd @ w_branch[1])
         + gates[..., 2, :] * (y_ml @ w_branch[2]))
    return u @ w_out

def _hier_moe(h, w_group, b_group, w_expert_router, b_expert_router, w_gate, w_up, w_down):
    dtype = h.dtype
    Bsz, L, D = h.shape
    N = Bsz * L
    xf = h.reshape(N, D)
    g_logits = (xf @ w_group + b_group).astype(jnp.float32)
    g_prob = jax.nn.softmax(g_logits, axis=-1)
    _, g_sel = lax.top_k(g_logits, 1)
    e_logits = (xf @ w_expert_router + b_expert_router).astype(jnp.float32)
    e_logits = e_logits.reshape(N, N_EXPERT_GROUPS, EXPERTS_PER_GROUP)
    e_in_group = jnp.take_along_axis(e_logits, g_sel[:, :, None], axis=1)[:, 0]
    top_v, top_i = lax.top_k(e_in_group, TOP_K)
    weights = jnp.take_along_axis(g_prob, g_sel, axis=1) * jax.nn.softmax(top_v, axis=-1)
    expert_id = g_sel * EXPERTS_PER_GROUP + top_i
    A = N * TOP_K
    flat_e = expert_id.reshape(A)
    flat_tok = jnp.repeat(jnp.arange(N, dtype=jnp.int32), TOP_K)
    flat_w = weights.reshape(A)
    order = jnp.argsort(flat_e)
    sorted_e = flat_e[order]
    counts = jnp.bincount(flat_e, length=N_EXPERTS)
    starts = jnp.cumsum(counts) - counts
    padded = ((counts + MOE_BLOCK - 1) // MOE_BLOCK) * MOE_BLOCK
    pend = jnp.cumsum(padded)
    pstart = pend - padded
    dest = pstart[sorted_e] + (jnp.arange(A) - starts[sorted_e])
    P = A + N_EXPERTS * MOE_BLOCK
    row_tok = jnp.full((P,), N, jnp.int32).at[dest].set(flat_tok[order])
    row_w = jnp.zeros((P,), jnp.float32).at[dest].set(flat_w[order])
    n_blk = P // MOE_BLOCK
    blk_e = jnp.minimum(jnp.searchsorted(pend, jnp.arange(n_blk) * MOE_BLOCK, side='right'), N_EXPERTS - 1)
    x_rows = jnp.concatenate([xf, jnp.zeros((1, D), dtype)], axis=0)[row_tok].reshape(n_blk, MOE_BLOCK, D)

    def expert_block(args):
        xb, e = args
        return (jax.nn.silu(xb @ w_gate[e]) * (xb @ w_up[e])) @ w_down[e]

    y_rows = lax.map(expert_block, (x_rows, blk_e)).reshape(P, D)
    y = jax.ops.segment_sum(y_rows.astype(jnp.float32) * row_w[:, None], row_tok, num_segments=N + 1)[:N]
    return y.astype(dtype).reshape(Bsz, L, D)

def setup_inputs(seed: int = 0) -> dict:
    key = jax.random.key(seed)
    ks = jax.random.split(key, 27)
    f32 = jnp.float32
    nrm = lambda k, shape, scale: jax.random.normal(k, shape, f32) * scale
    dt = jnp.exp(jax.random.uniform(ks[6], (DEPTH, SSD_HEADS), f32) * (math.log(0.1) - math.log(0.001))
                 + math.log(0.001))
    return {
        'x': jax.random.normal(ks[0], (BATCH, SEQ, D_MODEL), f32),
        'norm1_w': 1.0 + nrm(ks[1], (DEPTH, D_MODEL), 0.02),
        'w_in': nrm(ks[2], (DEPTH, D_MODEL, IN_WIDTH), D_MODEL ** -0.5),
        'att_f_bias': jax.random.uniform(ks[3], (DEPTH, ATT_HEADS), f32, 1.0, 4.0),
        'ssd_conv_w': nrm(ks[4], (DEPTH, SSD_CONV, SSD_CONV_DIM), SSD_CONV ** -0.5),
        'ssd_conv_b': nrm(ks[5], (DEPTH, SSD_CONV_DIM), 0.01),
        'ssd_dt_bias': dt + jnp.log(-jnp.expm1(-dt)),
        'ssd_a_log': jnp.log(jax.random.uniform(ks[7], (DEPTH, SSD_HEADS), f32, 1.0, 16.0)),
        'ssd_d': 1.0 + nrm(ks[8], (DEPTH, SSD_HEADS), 0.1),
        'ssd_norm_w': 1.0 + nrm(ks[9], (DEPTH, MIX_WIDTH), 0.02),
        'ml_conv_w': nrm(ks[10], (DEPTH, ML_CONV, 2 * MIX_WIDTH), ML_CONV ** -0.5),
        'ml_conv_b': nrm(ks[11], (DEPTH, 2 * MIX_WIDTH), 0.01),
        'ml_i_bias': nrm(ks[12], (DEPTH, ML_HEADS), 0.1),
        'ml_f_bias': jax.random.uniform(ks[13], (DEPTH, ML_HEADS), f32, 3.0, 6.0),
        'ml_norm_w': 1.0 + nrm(ks[14], (DEPTH, MIX_WIDTH), 0.02),
        'gate_bias': nrm(ks[15], (DEPTH, N_BRANCHES * D_MODEL), 0.01),
        'w_branch': nrm(ks[16], (DEPTH, N_BRANCHES, MIX_WIDTH, D_MODEL), MIX_WIDTH ** -0.5),
        'w_out': nrm(ks[17], (DEPTH, D_MODEL, D_MODEL), D_MODEL ** -0.5),
        'norm2_w': 1.0 + nrm(ks[18], (DEPTH, D_MODEL), 0.02),
        'w_group': nrm(ks[19], (DEPTH, D_MODEL, N_EXPERT_GROUPS), D_MODEL ** -0.5),
        'b_group': nrm(ks[20], (DEPTH, N_EXPERT_GROUPS), 0.01),
        'w_expert_router': nrm(ks[21], (DEPTH, D_MODEL, N_EXPERTS), D_MODEL ** -0.5),
        'b_expert_router': nrm(ks[22], (DEPTH, N_EXPERTS), 0.01),
        'w_gate': nrm(ks[23], (DEPTH, N_EXPERTS, D_MODEL, D_EXPERT), D_MODEL ** -0.5),
        'w_up': nrm(ks[24], (DEPTH, N_EXPERTS, D_MODEL, D_EXPERT), D_MODEL ** -0.5),
        'w_down': nrm(ks[25], (DEPTH, N_EXPERTS, D_EXPERT, D_MODEL), D_EXPERT ** -0.5),
        'final_norm_w': 1.0 + nrm(ks[26], (D_MODEL,), 0.02),
    }

def reference(x, norm1_w, w_in, att_f_bias, ssd_conv_w, ssd_conv_b, ssd_dt_bias, ssd_a_log, ssd_d, ssd_norm_w,
              ml_conv_w, ml_conv_b, ml_i_bias, ml_f_bias, ml_norm_w, gate_bias, w_branch, w_out, norm2_w,
              w_group, b_group, w_expert_router, b_expert_router, w_gate, w_up, w_down, final_norm_w):
    for layer in range(DEPTH):
        h = _rmsnorm(x, norm1_w[layer])
        x = x + _hybrid_mixer(h, w_in[layer], att_f_bias[layer], ssd_conv_w[layer], ssd_conv_b[layer],
                              ssd_dt_bias[layer], ssd_a_log[layer], ssd_d[layer], ssd_norm_w[layer],
                              ml_conv_w[layer], ml_conv_b[layer], ml_i_bias[layer], ml_f_bias[layer],
                              ml_norm_w[layer], gate_bias[layer], w_branch[layer], w_out[layer])
        h = _rmsnorm(x, norm2_w[layer])
        x = x + _hier_moe(h, w_group[layer], b_group[layer], w_expert_router[layer], b_expert_router[layer],
                          w_gate[layer], w_up[layer], w_down[layer])
    return _rmsnorm(x, final_norm_w)


_drawn_inputs = setup_inputs


def setup_inputs(seed=0):
    import zlib

    import numpy as np

    out = dict(_drawn_inputs(seed))
    spreads = {}
    factors = {'ssd_conv_b': 3.96,
     'ssd_norm_w': 3.338,
     'ml_conv_b': 8.0,
     'ml_i_bias': 200.0,
     'ml_norm_w': 4.357,
     'gate_bias': 5.796,
     'norm2_w': 3.332,
     'b_group': 5.055,
     'b_expert_router': 8.0,
     'final_norm_w': 21.794}
    for name, (base, spread) in spreads.items():
        noise = np.random.default_rng([zlib.crc32(name.encode()), seed]).standard_normal(out[name].shape)
        drawn = base * np.exp(spread * noise) if base else spread * noise
        out[name] = __import__('jax').numpy.asarray(drawn.astype(out[name].dtype))
    for name, factor in factors.items():
        out[name] = (out[name] * factor).astype(out[name].dtype)
    return out
```

```python
from contextlib import ExitStack

import concourse.bass as bass
from concourse import mybir

F32 = mybir.dt.float32
I32 = mybir.dt.int32
U32 = mybir.dt.uint32
ALU = mybir.AluOpType
ACT = mybir.ActivationFunctionType
AX_X = mybir.AxisListType.X

P = 128
EPS = 1e-6
MASKED = -1e30


def plan(D, W):
    blocks, units = [], []
    col = 0
    at = {}
    for name, width in (("aq", D), ("ak", D), ("av", D), ("af", 16), ("z", D), ("xbc", 2 * D), ("dt", 16),
                        ("mq", D), ("mk", D), ("mv", D), ("mi", 4), ("mf", 4), ("mo", D), ("g", 3 * D)):
        at[name] = col
        col += width
    assert col == W
    for name in ("aq", "ak", "av", "xbc", "z", "mq", "mk", "mv", "mo", "g", "br", "out"):
        width = {"xbc": 2 * D, "g": 3 * D, "br": 3 * D}.get(name, D)
        for b in range(width // 512):
            if name == "br":
                blocks.append(("br", b // 2, 512 * (b % 2)))
            elif name == "out":
                blocks.append(("out", 0, 512 * b))
            else:
                blocks.append(("in", 0, at[name] + 512 * b))
            n = len(blocks) - 1
            if name == "out":
                if b:
                    units += [(name, n - 1 + h, t, h) for t in range(2) for h in range(2)]
            elif name in ("av", "mv"):
                units += [(name, n, t, b) for t in range(2)]
            else:
                units += [(name, n, c, 4 * b + c) for c in range(4)]
    return blocks, units, at


def stages(units):
    first = {}
    for u, unit in enumerate(units):
        first.setdefault(unit[0], u)
    follow = [[] for _ in units]
    follow[1].append(("gates", 0))
    follow[4].append(("sums", 0))
    u0 = first["xbc"]
    for s in range(19):
        follow[u0 + s] += [(k, s - lag) for lag, k in enumerate(("fox_a", "fox_p", "fox_b", "fox_c"))
                           if 0 <= s - lag < 16]
    u0 = first["mq"]
    for s in range(24):
        if s < 8:
            follow[u0 + s] += [("ssd_x", s)] + ([("ssd_cb", s // 2)] if s % 2 else [])
        if 0 <= s - 6 < 16:
            follow[u0 + s] += [("ssd_a", s - 6)]
        if 0 <= s - 8 < 16:
            follow[u0 + s] += [("ssd_c", s - 8)]
    follow[first["g"]] += [("ssd_norm", 0)]
    for h in range(4):
        u = first["g"] + 2 + 5 * h
        follow[u] += [("ml_a", h)]
        follow[u + 2] += [("ml_b", h)]
        follow[u + 3] += [("ml_c", h)]
    follow[first["g"] + 22] += [("ml_norm", 0)]
    return follow, first


def build_trunk(nc, x, norm1_w, w_in, att_f_bias, ssd_conv_w, ssd_conv_b, ssd_dt_bias, ssd_a_log, ssd_d,
                ssd_norm_w, ml_conv_w, ml_conv_b, ml_i_bias, ml_f_bias, ml_norm_w, gate_bias, w_branch, w_out,
                norm2_w, w_group, b_group, w_expert_router, b_expert_router, w_gate, w_up, w_down,
                final_norm_w, out):
    D = x.shape[2]
    T = x.shape[1]
    NT = T // P
    KC = D // P
    NE = w_gate.shape[1]
    NG = w_group.shape[2]
    EG = NE // NG
    FE = w_gate.shape[3]
    HC = FE // P
    NR = NG + NE
    SLOT = 32
    assert (D, T, NE, NG, FE) == (1024, 256, 64, 8, 512)
    BLOCKS, UNITS, COL = plan(D, w_in.shape[2])
    FOLLOW, FIRST = stages(UNITS)
    NB = len(BLOCKS)
    RING = 3
    BANKS = 3
    NU = len(UNITS)
    LAST = {unit[1]: u for u, unit in enumerate(UNITS)}
    CONSTS = 23
    PAR_IN = 16 * 20
    SMALL_GL = 4
    ML_NEG, ML_W = 4, 4
    RV_RSTD, RV_H2T, RV_GSUB, RV_VD, RV_OHM, RV_POS, RV_ITC, RV_ITEMS = 2, (3, 5), 12, 22, 26, 35, 50, 60
    RA_H2, RA_LGT = (3, 4), 5
    FIN_SQ, FIN_OUT = (5, 10), (12, 14)

    ctx = ExitStack()
    with ctx:
        def sb(name, shape, dt=F32):
            return ctx.enter_context(nc.sbuf_tensor(name, shape, dt))

        def sem(name):
            return ctx.enter_context(nc.semaphore(name))

        xs = sb("xs", [P, NT, D])
        ring = sb("ring", [P, RING, KC, 512])
        r1 = sb("r1", [P, 12288])
        r2 = sb("r2", [P, 6144])
        zu = sb("zu", [P, KC, T])
        r3 = sb("r3", [P, 6144])
        cbm = sb("cbm", [P, 4, 384])
        ident = sb("ident", [P, P])
        tri = sb("tri", [P, P])
        stri = sb("stri", [P, P])
        ones = sb("ones", [P, P])
        mean = sb("mean", [P, P])
        mask01 = sb("mask01", [P, 384])
        mneg = sb("mneg", [P, 256])
        eps = sb("eps", [P, 1])
        pc = sb("pc", [P, 2, 104])
        prow = sb("prow", [104, 2, P])
        n2 = sb("n2", [P, KC])
        dsk = sb("dsk", [P, KC])
        wsm = sb("wsm", [P, KC, 40])
        bsm = sb("bsm", [P, 40])
        alog = sb("alog", [P, 16])
        sm = sb("sm", [P, NT, 40])
        smw = sb("smw", [P, 6, NT, 40])
        dtt = sb("dtt", [P, NT, 16])
        gl = sb("gl", [P, NT, 36])
        li = sb("li", [P, NT, 4])
        cum = sb("cum", [P, NT, 36])
        rn = sb("rn", [P, NT, 20])
        ss = sb("ss", [P, 8])
        work = sb("work", [P, 10, 384])
        acc = sb("acc", [P, 3, T])
        thb = sb("thb", [P, 3, T])
        mx = sb("mx", [P, 2, 2])
        nmx = sb("nmx", [P, 2, 2])
        rsum = sb("rsum", [P, 2, 2])
        rinv = sb("rinv", [P, 2, 2])
        mls = sb("mls", [P, 6, 2])
        tmpu = sb("tmpu", [P, 2, T])
        bigt = work[:, :, :].rearrange("p a b -> p (a b)")[:, 0:D]

        qT = r1[:, 0:2048].rearrange("p (c t) -> p c t", c=KC)
        kT = r1[:, 2048:4096].rearrange("p (c t) -> p c t", c=KC)
        vN = r1[:, 4096:6144].rearrange("p (t n) -> p t n", t=NT)
        moT = r1[:, 6144:8192].rearrange("p (c t) -> p c t", c=KC)
        hT = r1[:, 8192:10240].rearrange("p (c t) -> p c t", c=KC)
        hN = r1[:, 10240:12288].rearrange("p (t n) -> p t n", t=NT)
        xbcT = r2[:, 0:4096].rearrange("p (c t) -> p c t", c=2 * KC)
        xdt = r2[:, 4096:6144].rearrange("p (t n) -> p t n", t=NT)
        gT = r2[:, :].rearrange("p (c t) -> p c t", c=3 * KC)
        yT = r3[:, :].rearrange("p (b c t) -> p b c t", b=3, c=KC)
        h2p = r3[:, 0:2048].rearrange("p (t c d) -> p t c d", t=NT, c=KC)
        h2T = r3[:, 2048:4096].rearrange("p (c t) -> p c t", c=KC)
        posb = r3[:, 4096:4608]
        wb = r3[:, 4608:5120]
        comb = r3[:, 5120:5632].rearrange("p (j t) -> p j t", j=2)
        combt = r3[:, 5632:6144]
        wg_s = [r1[:, 0:4096].rearrange("p (c n) -> p c n", c=KC), ring[:, 0, :, :]]
        wu_s = [r1[:, 4096:8192].rearrange("p (c n) -> p c n", c=KC), ring[:, 1, :, :]]
        wd_s = [r1[:, 8192:12288].rearrange("p (c n) -> p c n", c=HC),
                ring[:, 2, :, :].rearrange("p a b -> p (a b)").rearrange("p (c n) -> p c n", c=HC)]
        xg = r2[:, 0:512].rearrange("p (c s) -> p c s", c=KC)
        gus = r2[:, 512:1024].rearrange("p (j n) -> p j n", j=2)
        tht = r2[:, 1024:1280].rearrange("p (j i s) -> p j i s", j=2, i=2)
        gt1 = r2[:, 1280:1536].rearrange("p (j i s) -> p j i s", j=2, i=2)
        actT = r2[:, 1536:1792].rearrange("p (j i s) -> p j i s", j=2, i=2)
        ysb = r2[:, 1792:2304].rearrange("p (j n) -> p j n", j=2)
        pick = r2[:, 2304:2432].rearrange("p (t s) -> p t s", t=2)
        tgt = r2[:, 2432:2496]
        fw = r2[:, 2560:2560 + D]
        wrt = sb("wrt", [P, KC, NR])
        brt = sb("brt", [NR, 1])
        lgT = r2[0:NR, 5200:5456]
        lg = r2[:, 3584:3728].rearrange("p (t n) -> p t n", t=NT)
        top = sb("top", [P, NT, 8])
        topi = sb("topi", [P, NT, 8], U32)
        rt = sb("rt", [P, 24, NT])
        ohg = sb("ohg", [P, NT, NG])
        egs = r2[:, 3728:3856].rearrange("p (t e g) -> p t e g", t=NT, e=EG)
        ein = sb("ein", [P, NT, EG])
        pe8 = sb("pe8", [P, NT, NG])
        eid = sb("eid", [P, NT, 2])
        ohe = r2[:, 3856:4112].rearrange("p (a e) -> p a e", e=NE)
        ohm = r2[:, 4368:4496].rearrange("p (a e) -> p a e", e=NE)
        rke = r2[:, 4112:4368].rearrange("p (a e) -> p a e", e=NE)
        rank = sb("rank", [P, NT * 2])
        pos = sb("pos", [P, NT * 2])
        wtok = sb("wtok", [P, NT, 2])
        iota = sb("iota", [P, P])
        thr = sb("thr", [P, 8])
        pmod = sb("pmod", [P, 1])
        pidx = sb("pidx", [P, 1])
        two = sb("two", [P, NE])
        cnt8 = r2[:, 4496:5008].rearrange("p (e b) -> p e b", b=8)
        nbk = r2[:, 5008:5200].rearrange("p (a e) -> p a e", e=NE)
        itc = sb("itc", [P, 8])
        base = sb("base", [P, P])
        eint = sb("eint", [P, P], I32)
        npair = sb("npair", [P, 1], I32)
        bcur = sb("bcur", [P, 2])
        bnxt = sb("bnxt", [P, 2])
        scol = sb("scol", [P, 2])

        bank = [ctx.enter_context(nc.psum_tensor(f"bank{i}", [P, 512], F32)) for i in range(8)]
        PJ = bank[0:3]
        SC = bank[3:5]
        TR = bank[5]
        OB = bank[6:8]
        ACCB = bank[0:4]
        GAB, GUB, TRB, DNB = bank[4:8]

        par_in = sem("par_in")
        x_in = sem("x_in")
        rt_in = sem("rt_in")
        w_in_sem = [sem(f"w_block{i}") for i in range(RING)]
        fw_in = sem("fw_in")
        x1_part = sem("x1_part")
        consts = sem("consts")
        dstep = sem("dstep")
        astep = sem("astep")
        x_sq = sem("x_sq")
        x_norm = sem("x_norm")
        h_turned = sem("h_turned")
        h_ready = sem("h_ready")
        par_turned = sem("par_turned")
        par_ready = sem("par_ready")
        small_done = sem("small_done")
        small_v = sem("small_v")
        small_a = sem("small_a")
        cum_done = sem("cum_done")
        cum_ready = sem("cum_ready")
        proj = sem("proj")
        kept = sem("kept")
        conv_pre = sem("conv_pre")
        conv_sum = sem("conv_sum")
        conv_tanh = sem("conv_tanh")
        conv_out = sem("conv_out")
        fox_scores = sem("fox_scores")
        fox_masked = sem("fox_masked")
        fox_negmax = sem("fox_negmax")
        fox_exp = sem("fox_exp")
        fox_probs = sem("fox_probs")
        fox_turned = sem("fox_turned")
        fox_pt = sem("fox_pt")
        fox_out = sem("fox_out")
        fox_y = sem("fox_y")
        z_tanh = sem("z_tanh")
        z_out = sem("z_out")
        ssd_turned = sem("ssd_turned")
        ssd_x = sem("ssd_x")
        ssd_cb = sem("ssd_cb")
        ssd_cbm = sem("ssd_cbm")
        ssd_bc = sem("ssd_bc")
        ssd_seg = sem("ssd_seg")
        ssd_exp = sem("ssd_exp")
        ssd_w = sem("ssd_w")
        ssd_out = sem("ssd_out")
        ssd_y = sem("ssd_y")
        nrm_sq = sem("nrm_sq")
        nrm_ms = sem("nrm_ms")
        nrm_rt = sem("nrm_rt")
        nrm_y = sem("nrm_y")
        ml_scores = sem("ml_scores")
        ml_neg = sem("ml_neg")
        ml_exp = sem("ml_exp")
        ml_w = sem("ml_w")
        ml_turned = sem("ml_turned")
        ml_pt = sem("ml_pt")
        ml_out = sem("ml_out")
        ml_y = sem("ml_y")
        g_ready = sem("g_ready")
        u_ready = sem("u_ready")
        x1_ready = sem("x1_ready")
        r_v = sem("r_v")
        r_a = sem("r_a")
        r_p = sem("r_p")
        gu_in = [sem(f"gu_in{j}") for j in range(2)]
        dn_in = [sem(f"dn_in{j}") for j in range(2)]
        picked = sem("picked")
        combined = sem("combined")
        gathered = sem("gathered")
        xg_ready = sem("xg_ready")
        gu_done = sem("gu_done")
        gu_copied = sem("gu_copied")
        hid_turned = sem("hid_turned")
        hid_tanh = sem("hid_tanh")
        hid_v = sem("hid_v")
        down_done = sem("down_done")
        y_copied = sem("y_copied")
        comb_done = sem("comb_done")
        pick_v = sem("pick_v")
        comb_v = sem("comb_v")
        acc_zero = sem("acc_zero")
        fin_v = sem("fin_v")
        fin_a = sem("fin_a")
        out_done = sem("out_done")

        lay = w_in[0]
        blk_src = {
            "in": lambda i, c: lay[:, c:c + 512],
            "br": lambda i, c: w_branch[0, i, :, c:c + 512],
            "out": lambda i, c: w_out[0, :, c:c + 512],
        }
        CONV = [u for u, unit in enumerate(UNITS) if unit[0] in ("xbc", "mq", "mk")]
        conv_no = {u: i for i, u in enumerate(CONV)}
        Z0 = FIRST["z"]
        G0 = FIRST["g"]
        BR0 = FIRST["br"]
        OUT0 = FIRST["out"]

        FREED, n = [], {}
        for kind, *_ in UNITS:
            s = {"xbc": conv_sum, "mq": conv_sum, "mk": conv_sum, "z": z_out, "br": u_ready, "out": x1_part}.get(kind, kept)
            n[s.name] = n.get(s.name, 0) + 1
            FREED.append((s, n[s.name]))

        block = ctx.enter_context(nc.Block())

        def load_expert(sp, e, j):
            sp.dma_start(wg_s[j], w_gate[0, e].rearrange("(p c) n -> p c n", p=P)).then_inc(gu_in[j], 16)
            sp.dma_start(wu_s[j], w_up[0, e].rearrange("(p c) n -> p c n", p=P)).then_inc(gu_in[j], 16)
            sp.dma_start(wd_s[j], w_down[0, e].rearrange("(c p) n -> p c n", p=P)).then_inc(dn_in[j], 16)

        @block.sync
        def _(sp):
            for t in range(NT):
                sp.dma_start(xs[:, t, :], x[0, t * P:(t + 1) * P, :]).then_inc(x_in, 16)
            for n, (kind, i, c) in enumerate(BLOCKS):
                if n >= RING:
                    sp.wait_ge(proj, LAST[n - RING] + 1)
                sp.dma_start(ring[:, n % RING, :, :],
                             blk_src[kind](i, c).rearrange("(c p) n -> p c n", p=P)).then_inc(w_in_sem[n % RING], 16)
                if n == UNITS[BR0][1] + RING:
                    sp.wait_ge(proj, BR0 + 1)
                    sp.wait_ge(nrm_y, 16)
                    load_expert(sp, 0, 0)
            sp.wait_ge(proj, NU)
            sp.wait_ge(u_ready, 24)
            sp.dma_start(fw, final_norm_w.rearrange("(a n) -> a n", a=1).to_broadcast([P, D])).then_inc(fw_in, 16)
            load_expert(sp, 1, 1)
            sp.wait_ge(r_v, RV_ITEMS)
            pairs = sp.value_load(npair[0:1, 0:1], min_val=1, max_val=P // 2 - 1)
            with sp.If(pairs > 1):
                with sp.Fori(1, pairs) as i:
                    for j in range(2):
                        e = sp.value_load(eint[0:1, bass.ds(2 * i + j, 1)], min_val=0, max_val=NE - 1)
                        sp.wait_ge(gu_done, 2 * i + (j - 1))
                        sp.dma_start(wg_s[j], w_gate[0, bass.ds(e, 1), :, :].rearrange(
                            "a (p c) n -> p (a c) n", p=P)).then_inc(gu_in[j], 16)
                        sp.dma_start(wu_s[j], w_up[0, bass.ds(e, 1), :, :].rearrange(
                            "a (p c) n -> p (a c) n", p=P)).then_inc(gu_in[j], 16)
                        sp.wait_ge(down_done, 2 * i + (j - 1))
                        sp.dma_start(wd_s[j], w_down[0, bass.ds(e, 1), :, :].rearrange(
                            "a (c p) n -> p (a c) n", p=P)).then_inc(dn_in[j], 16)
            for t in range(NT):
                sp.wait_ge(fin_v, FIN_OUT[t])
                sp.dma_start(out[0, t * P:(t + 1) * P, :], xs[:, t, :]).then_inc(out_done, 16)
            sp.wait_ge(out_done, 16 * NT)

        @block.gpsimd
        def _(pool):
            def aff(t, pattern, op, base_, mult, fill, inp=None):
                return pool.affine_select(out=t, in_=t if inp is None else inp, compare_op=op, fill=fill, base=base_,
                                          pattern=pattern, channel_multiplier=mult)
            pool.memset(ident[:, :], 0.0).then_inc(consts, 1)
            pool.memset(tri[:, :], 1.0).then_inc(consts, 1)
            pool.memset(stri[:, :], 1.0).then_inc(consts, 1)
            pool.memset(ones[:, :], 1.0).then_inc(consts, 1)
            pool.memset(mean[:, :], 1.0 / 256).then_inc(consts, 1)
            pool.memset(mask01[:, :], 1.0).then_inc(consts, 1)
            pool.memset(mneg[:, :], 0.0).then_inc(consts, 1)
            pool.memset(eps[:, :], EPS).then_inc(consts, 1)
            pool.memset(two[:, :], 0.0).then_inc(consts, 1)
            pool.iota(iota[:, :], [[1, P]], base=0, channel_multiplier=0,
                      allow_small_or_imprecise_dtypes=True).then_inc(consts, 1)
            pool.iota(thr[:, :], [[SLOT, 8]], base=0, channel_multiplier=0,
                      allow_small_or_imprecise_dtypes=True).then_inc(consts, 1)
            pool.iota(pidx[:, :], [[0, 1]], base=-2, channel_multiplier=1,
                      allow_small_or_imprecise_dtypes=True).then_inc(consts, 1)
            for q in range(4):
                pool.wait_ge(consts, 12 + q)
                pool.iota(pmod[32 * q:32 * q + 32, :], [[0, 1]], base=0, channel_multiplier=1,
                          allow_small_or_imprecise_dtypes=True).then_inc(consts, 1)
            pool.wait_ge(consts, 16)
            aff(ident[:, :], [[-1, P]], ALU.not_equal, 0, 1, 1.0).then_inc(consts, 1)
            aff(tri[:, :], [[1, P]], ALU.is_ge, 0, -1, 0.0).then_inc(consts, 1)
            aff(stri[:, :], [[1, P]], ALU.is_gt, 0, -1, 0.0).then_inc(consts, 1)
            aff(mask01[:, 0:P], [[1, P]], ALU.is_ge, 0, -1, 0.0).then_inc(consts, 1)
            aff(mask01[:, 256:384], [[1, P]], ALU.is_ge, 0, -1, 0.0).then_inc(consts, 1)
            aff(mneg[:, P:256], [[-1, P]], ALU.is_ge, 0, 1, MASKED).then_inc(consts, 1)
            pool.memset(two[:, 0:2], 1.0).then_inc(consts, 1)
        @block.tensor
        def _(pe):
            pe.wait_ge(consts, CONSTS)
            pe.wait_ge(par_in, PAR_IN)
            for i in range(2):
                mm = pe.transpose(SC[0][:, 104 * i:104 * i + 104], prow[:, i, :], ident[0:104, 0:104])
            mm.then_inc(par_turned, 1)
            for t in range(NT):
                pe.wait_ge(x_norm, t + 1)
                for c in range(KC):
                    b = OB[c // 4]
                    if t and c % 4 == 0:
                        pe.wait_ge(h_ready, 8 * (t - 1) + 4 * (c // 4) + 4)
                    pe.transpose(b[:, P * (c % 4):P * (c % 4) + P], hN[:, t, P * c:P * c + P],
                                 ident[:, :]).then_inc(h_turned, 1)
            pe.wait_ge(h_ready, 16)
            for u, (kind, n, part, chunk) in enumerate(UNITS):
                if kind == "br" and chunk % KC == 0:
                    b = chunk // KC
                    pe.wait_ge(*((fox_y, 8), (nrm_y, 8), (nrm_y, 16))[b])
                if kind == "out" and u == OUT0:
                    pe.wait_ge(u_ready, 24)
                pe.wait_ge(w_in_sem[n % RING], 16 * (n // RING + 1))
                if u >= BANKS:
                    pe.wait_ge(*FREED[u - BANKS])
                pj = PJ[u % BANKS]
                w = ring[:, n % RING, :, :]
                for c in range(KC):
                    f, l = c == 0, c == KC - 1
                    if kind in ("av", "mv", "out"):
                        src = zu if kind == "out" else hT
                        mm = pe.matmul(pj[:, :], src[:, c, P * part:P * part + P], w[:, c, :], start=f, stop=l)
                    else:
                        rhs = yT[:, chunk // KC, c, :] if kind == "br" else hT[:, c, :]
                        mm = pe.matmul(pj[:, 0:T], w[:, c, P * part:P * part + P], rhs, start=f, stop=l)
                mm.then_inc(proj, 1)
                for stage, h in FOLLOW[u]:
                    if stage == "gates":
                        for t in range(NT):
                            for c in range(KC):
                                mm = pe.matmul(TR[:, 40 * t:40 * t + 40], hT[:, c, P * t:P * t + P], wsm[:, c, :],
                                               start=(c == 0), stop=(c == KC - 1))
                            mm.then_inc(small_done, 1)
                    elif stage == "sums":
                        pe.wait_ge(small_v, SMALL_GL)
                        pe.matmul(TR[:, 128:164], tri[:, :], gl[:, 0, :], start=True, stop=True)
                        pe.matmul(TR[:, 192:228], ones[:, :], gl[:, 0, :], start=True, stop=False)
                        pe.matmul(TR[:, 192:228], tri[:, :], gl[:, 1, :], start=False, stop=True).then_inc(cum_done, 1)
                    elif stage == "fox_a":
                        s = SC[h % 2]
                        if h == 0:
                            pe.wait_ge(*FREED[FIRST["xbc"] - 1])
                            pe.wait_ge(cum_ready, 4)
                        if h >= 2:
                            pe.wait_ge(fox_masked, 2 * (h - 1))
                        q = slice(64 * (h % 2), 64 * (h % 2) + 64)
                        for lo, qs, nk in ((0, slice(P, T), T), (T, slice(0, P), P)):
                            pe.matmul(s[:, lo:lo + nk], qT[q, h // 2, qs], kT[q, h // 2, 0:nk], start=True, stop=False)
                            for t in range(nk // P):
                                mm = pe.matmul(s[:, lo + P * t:lo + P * t + P],
                                               rn[:, t, h:h + 1].to_broadcast([P, P]), ident[:, :],
                                               start=False, stop=(t == nk // P - 1))
                        mm.then_inc(fox_scores, 1)
                    elif stage == "fox_b":
                        pe.wait_ge(fox_probs, 2 * h + 2)
                        if h:
                            pe.wait_ge(fox_pt, h)
                        p = work[:, 2 + h % 2, :]
                        pe.transpose(TR[:, 0:P], p[:, T:384], ident[:, :])
                        pe.transpose(TR[:, P:T], p[:, 0:P], ident[:, :])
                        pe.transpose(TR[:, T:384], p[:, P:T], ident[:, :]).then_inc(fox_turned, 1)
                    elif stage == "fox_c":
                        pe.wait_ge(fox_pt, h + 1)
                        if h >= 4 and h % 2 == 0:
                            pe.wait_ge(fox_y, h // 2 - 1)
                        o = OB[(h // 2) % 2][64 * (h % 2):64 * (h % 2) + 64, :]
                        pt = work[:, 4 + h % 2, :]
                        pe.matmul(o[:, 0:T], vN[:, 0, 64 * h:64 * h + 64], pt[:, 0:T], start=True, stop=False)
                        pe.matmul(o[:, P:T], vN[:, 1, 64 * h:64 * h + 64], pt[:, T:384],
                                  start=False, stop=True).then_inc(fox_out, 1)
                    elif stage == "ssd_x":
                        if h == 0:
                            pe.wait_ge(fox_pt, 16)
                            pe.wait_ge(fox_y, 8)
                            pe.wait_ge(conv_out, 16)
                        elif h >= 2:
                            pe.wait_ge(ssd_x, h - 1)
                        for t in range(NT):
                            mm = pe.transpose((TR, OB[0])[h % 2][:, P * t:P * t + P],
                                              xbcT[:, h, P * t:P * t + P], ident[:, :])
                        mm.then_inc(ssd_turned, 1)
                    elif stage == "ssd_cb":
                        if h:
                            pe.wait_ge(ssd_cbm, h)
                        pe.matmul(OB[1][:, 0:T], xbcT[:, 8 + h, 0:P], xbcT[:, 12 + h, 0:T], start=True, stop=True)
                        pe.matmul(OB[1][:, T:384], xbcT[:, 8 + h, P:T], xbcT[:, 12 + h, P:T],
                                  start=True, stop=True).then_inc(ssd_cb, 1)
                    elif stage == "ssd_a":
                        s = SC[h % 2]
                        if h >= 2:
                            pe.wait_ge(ssd_seg, 2 * (h - 1))
                        else:
                            pe.wait_ge(fox_masked, 32)
                        for t in range(NT):
                            mm = pe.matmul(s[:, P * t:P * t + P], cum[:, t, 16 + h:17 + h].to_broadcast([P, P]),
                                           ident[:, :], start=True, stop=True)
                        mm.then_inc(ssd_bc, 1)
                    elif stage == "ssd_c":
                        pe.wait_ge(ssd_w, h + 1)
                        pe.wait_ge(ssd_x, h // 2 + 1)
                        if h == 0:
                            pe.wait_ge(ssd_x, 8)
                        elif h == 2:
                            pe.wait_ge(ssd_cbm, 4)
                        elif h % 2 == 0:
                            pe.wait_ge(ssd_y, 2 * (h // 2 - 1))
                        o = OB[(h // 2) % 2][64 * (h % 2):64 * (h % 2) + 64, :]
                        w2 = work[:, 4 + h % 2, :]
                        pe.matmul(o[:, 0:T], xdt[:, 0, 64 * h:64 * h + 64], w2[:, 0:T], start=True, stop=False)
                        pe.matmul(o[:, P:T], xdt[:, 1, 64 * h:64 * h + 64], w2[:, T:384],
                                  start=False, stop=True).then_inc(ssd_out, 1)
                    elif stage in ("ssd_norm", "ml_norm"):
                        k = 0 if stage == "ssd_norm" else 1
                        for g in range(4):
                            pe.wait_ge(nrm_sq, 4 * k + g + 1)
                            if g >= 2 or k:
                                pe.wait_ge(nrm_rt, 4 * k + g - 1)
                            if g < 2:
                                pe.wait_ge(*((ssd_y, 16), (ml_y, 8))[k])
                            o = OB[g % 2]
                            for i in range(2):
                                mm = pe.matmul(o[:, 0:T], mean[:, :], work[:, 6 + 2 * (g % 2) + i, 0:T],
                                               start=(i == 0), stop=(i == 1))
                            mm.then_inc(nrm_ms, 1)
                    elif stage == "ml_a":
                        if h == 0:
                            pe.wait_ge(*FREED[G0 - 1])
                            pe.wait_ge(conv_out, len(CONV))
                            pe.wait_ge(ssd_seg, 32)
                        else:
                            pe.wait_ge(ml_w, ML_W * h)
                        for lo, qs, nk in ((0, slice(P, T), T), (T, slice(0, P), P)):
                            for i in range(2):
                                pe.matmul(SC[0][:, lo:lo + nk], qT[:, 2 * h + i, qs], kT[:, 2 * h + i, 0:nk],
                                          start=(i == 0), stop=(i == 1))
                        for t in range(NT):
                            mm = pe.matmul(SC[1][:, P * t:P * t + P], rn[:, t, 16 + h:17 + h].to_broadcast([P, P]),
                                           ident[:, :], start=True, stop=True)
                        mm.then_inc(ml_scores, 1)
                    elif stage == "ml_b":
                        pe.wait_ge(ml_w, ML_W * (h + 1))
                        if h:
                            pe.wait_ge(ml_pt, h)
                        p = work[:, 2, :]
                        pe.transpose(TR[:, 0:P], p[:, T:384], ident[:, :])
                        pe.transpose(TR[:, P:T], p[:, 0:P], ident[:, :])
                        pe.transpose(TR[:, T:384], p[:, P:T], ident[:, :]).then_inc(ml_turned, 1)
                    elif stage == "ml_c":
                        pe.wait_ge(ml_pt, h + 1)
                        if h == 0:
                            pe.wait_ge(nrm_rt, 4)
                        else:
                            pe.wait_ge(ml_y, 2 * h)
                        pt = work[:, 4, :]
                        for i in range(2):
                            v = slice(256 * h + P * i, 256 * h + P * i + P)
                            pe.matmul(OB[i][:, 0:T], vN[:, 0, v], pt[:, 0:T], start=True, stop=False)
                            pe.matmul(OB[i][:, P:T], vN[:, 1, v], pt[:, T:384],
                                      start=False, stop=True).then_inc(ml_out, 1)

            for t in range(NT):
                for c in range(KC):
                    if c % 4 == 0:
                        pe.wait_ge(r_a, RA_H2[t])
                        if t:
                            pe.wait_ge(r_v, RV_H2T[0] + c // 4)
                    pe.transpose(SC[c // 4][:, P * (c % 4):P * (c % 4) + P], h2p[:, t, c, :], ident[:, :])\
                        .then_inc(r_p, 1)
            pe.wait_ge(r_v, RV_H2T[1] + 1)
            pe.wait_ge(rt_in, 64)
            for c in range(KC):
                mm = pe.matmul(TR[0:NR, 0:T], wrt[:, c, :], h2T[:, c, :], start=(c == 0), stop=(c == KC - 1))
            mm.then_inc(r_p, 1)
            pe.wait_ge(r_a, RA_LGT)
            for t in range(NT):
                mm = pe.transpose(OB[0][:, P * t:P * t + NR], lgT[:, P * t:P * t + P], ident[0:NR, 0:NR])
            mm.then_inc(r_p, 1)
            pe.wait_ge(r_v, RV_OHM)
            pe.matmul(OB[1][:, 0:NE], stri[:, :], ohm[:, 0, :], start=True, stop=True)
            pe.matmul(OB[1][:, NE:2 * NE], ones[:, :], ohm[:, 0, :], start=True, stop=False)
            pe.matmul(OB[1][:, NE:2 * NE], stri[:, :], ohm[:, 1, :], start=False, stop=True)
            pe.matmul(OB[1][:, 2 * NE:3 * NE], ones[:, :], ohm[:, 0, :], start=True, stop=False)
            pe.matmul(OB[1][:, 2 * NE:3 * NE], ones[:, :], ohm[:, 1, :], start=False, stop=True).then_inc(r_p, 1)
            pe.wait_ge(r_v, RV_POS)
            for dst, src in ((SC[0], pos[:, :].rearrange("p (t k) -> p t k", t=NT)), (SC[1], wtok)):
                for k in range(2):
                    for t in range(NT):
                        mm = pe.matmul(dst[:, T * k + P * t:T * k + P * t + P], src[:, t, k:k + 1].to_broadcast([P, P]),
                                       ident[:, :], start=True, stop=True)
            mm.then_inc(r_p, 1)
            pe.wait_ge(r_v, RV_ITC)
            for i in range(2):
                mm = pe.matmul(TR[:, P * i:P * i + P], itc[:, i:i + 1].to_broadcast([P, P]), ident[:, :],
                               start=True, stop=True)
            mm.then_inc(r_p, 1)

            pe.wait_ge(r_v, RV_ITEMS)
            pe.wait_ge(acc_zero, 1)
            for n in range(4):
                mm = pe.matmul(ACCB[n][:, :], ident[:, :], bigt[:, 0:512], start=True, stop=True)
            mm.then_inc(comb_done, 1)

            def gather():
                for c in range(KC):
                    for t in range(NT):
                        mm = pe.matmul(GAB[:, 64 * c:64 * c + 64], h2p[:, t, c, :], pick[:, t, :],
                                       start=(t == 0), stop=(t == NT - 1))
                mm.then_inc(gathered, 1)

            pe.wait_ge(picked, 1)
            gather()
            pairs = pe.value_load(npair[0:1, 0:1], min_val=1, max_val=P // 2 - 1)
            with pe.Fori(0, pairs) as i:
                for j in range(2):
                    gu = GUB[:, T * j:T * j + T]
                    pe.wait_ge(gu_in[j], 32 * i + 32)
                    if j == 0:
                        pe.wait_ge(xg_ready, i + 1)
                    for c in range(KC):
                        for g in range(4):
                            w = (wg_s[j] if g < 2 else wu_s[j])[:, c, T * (g % 2):T * (g % 2) + T]
                            mm = pe.matmul(gu[32 * g:32 * g + 32, :], xg[:, c, 32 * j:32 * j + 32], w,
                                           start=(c == 0), stop=(c == KC - 1))
                    mm.then_inc(gu_done, 1)
                    if j == 1:
                        pe.wait_ge(picked, i + 2)
                        gather()
                    pe.wait_ge(gu_copied, 2 * i + (j + 1))
                    for k in range(2):
                        mm = pe.transpose(TRB[:, T * j + P * k:T * j + P * k + P], gus[:, j, P * k:P * k + P],
                                          ident[:, :])
                    mm.then_inc(hid_turned, 1)
                    pe.wait_ge(hid_v, 4 * i + (2 * j + 2))
                    pe.wait_ge(dn_in[j], 16 * i + 16)
                    dn = DNB[:, T * j:T * j + T]
                    for c in range(HC):
                        a = actT[:, j, c % 2, 32 * (c // 2):32 * (c // 2) + 32]
                        for g in range(4):
                            mm = pe.matmul(dn[32 * g:32 * g + 32, :], a, wd_s[j][:, c, T * g:T * g + T],
                                           start=(c == 0), stop=(c == HC - 1))
                    mm.then_inc(down_done, 1)
                    pe.wait_ge(y_copied, 2 * i + (j + 1))
                    pe.wait_ge(combined, 2 * i + (j + 1))
                    for t in range(NT):
                        for g in range(4):
                            r = slice(32 * g, 32 * g + 32)
                            mm = pe.matmul(ACCB[g][:, T * t:T * t + T], comb[r, j, P * t:P * t + P], ysb[r, j, :],
                                           start=False, stop=True, skip_group_check=True)
                    mm.then_inc(comb_done, 1)
        @block.scalar
        def _(act):
            rows = ((0, 0, norm1_w[0], KC), (0, 8, ssd_conv_w[0].rearrange("k n -> (k n)"), 64),
                    (0, 72, ssd_conv_b[0], 16), (0, 88, ssd_norm_w[0], 8), (0, 96, ml_norm_w[0], 8),
                    (1, 0, ml_conv_w[0].rearrange("k n -> (k n)"), 64), (1, 64, ml_conv_b[0], 16),
                    (1, 80, gate_bias[0], 24))
            for i, r, src, n in rows:
                act.dma_start(prow[r:r + n, i, :], src.rearrange("(r p) -> r p", p=P)).then_inc(par_in, 16)
            act.dma_start(n2[:, :], norm2_w[0].rearrange("(p c) -> p c", p=P)).then_inc(par_in, 16)
            col = 0
            for name, n, bias in (("af", 16, att_f_bias), ("dt", 16, ssd_dt_bias), ("mi", 4, ml_i_bias),
                                  ("mf", 4, ml_f_bias)):
                act.dma_start(wsm[:, :, col:col + n],
                              lay[:, COL[name]:COL[name] + n].rearrange("(c p) n -> p c n", p=P)).then_inc(par_in, 16)
                act.dma_start(bsm[:, col:col + n], bias[0:1, :].to_broadcast([P, n])).then_inc(par_in, 16)
                col += n
            act.dma_start(alog[:, :], ssd_a_log[0:1, :].to_broadcast([P, 16])).then_inc(par_in, 16)
            for i in range(2):
                with nc.allow_non_contiguous_dma("eight values"):
                    act.dma_start(dsk[64 * i:64 * i + 64, :],
                                  ssd_d[0:1, :].rearrange("a (c two) -> a c two", two=2)[:, :, i]
                                  .to_broadcast([64, KC])).then_inc(par_in, 16)
            with nc.allow_non_contiguous_dma("router weights"):
                act.dma_start(wrt[:, :, 0:NG], w_group[0].rearrange("(p c) n -> p c n", p=P)).then_inc(rt_in, 16)
                act.dma_start(wrt[:, :, NG:NR], w_expert_router[0].rearrange("(p c) n -> p c n", p=P))\
                    .then_inc(rt_in, 16)
                act.dma_start(brt[0:NG, :], b_group.rearrange("a n -> n a")).then_inc(rt_in, 16)
                act.dma_start(brt[NG:NR, :], b_expert_router.rearrange("a n -> n a")).then_inc(rt_in, 16)
            act.wait_ge(consts, CONSTS)
            for t in range(NT):
                act.wait_ge(x_sq, t + 1)
                act.activation(ss[:, 2 + t:3 + t], ss[:, t:t + 1], ACT.Sqrt, bias=eps[:, :], scale=1.0 / D)\
                    .then_inc(astep, 1)
            act.wait_ge(par_ready, 3)

            def tanh_of(u):
                i = conv_no[u]
                act.wait_ge(conv_sum, i + 1)
                if i >= 3:
                    act.wait_ge(conv_out, i - 2)
                act.activation(thb[:, i % 3, :], acc[:, i % 3, :], ACT.Tanh).then_inc(conv_tanh, 1)

            for u, (kind, n, part, chunk) in enumerate(UNITS):
                pj = PJ[u % BANKS]
                if kind in ("aq", "ak", "av", "mv", "mo", "z", "g", "xbc", "mq", "mk"):
                    act.wait_ge(proj, u + 1)
                if kind == "aq":
                    act.activation(qT[:, chunk, :], pj[:, 0:T], ACT.Copy, scale=64 ** -0.5).then_inc(kept, 1)
                elif kind == "ak":
                    act.activation(kT[:, chunk, :], pj[:, 0:T], ACT.Copy).then_inc(kept, 1)
                elif kind in ("av", "mv"):
                    act.activation(vN[:, part, 512 * chunk:512 * chunk + 512], pj[:, :], ACT.Copy).then_inc(kept, 1)
                elif kind == "mo":
                    act.activation(moT[:, chunk, :], pj[:, 0:T], ACT.Tanh, scale=0.5).then_inc(kept, 1)
                elif kind == "z":
                    i = u - Z0
                    if i >= 2:
                        act.wait_ge(z_out, i - 1)
                    act.activation(work[:, 8 + i % 2, 0:T], pj[:, 0:T], ACT.Tanh, scale=0.5).then_inc(z_tanh, 1)
                elif kind == "g":
                    if u == G0:
                        act.wait_ge(ssd_y, 16)
                    act.activation(gT[:, chunk, :], pj[:, 0:T], ACT.Tanh, bias=pc[:, 1, 80 + chunk:81 + chunk],
                                   scale=0.5).then_inc(kept, 1)
                elif u in conv_no:
                    i = conv_no[u]
                    w0, b0, wi, ch = (8, 72, 0, chunk) if kind == "xbc" else (0, 64, 1, chunk + (8 if kind == "mk" else 0))
                    if i >= 3:
                        act.wait_ge(conv_out, i - 2)
                    act.activation(acc[:, i % 3, :], pj[:, 0:T], ACT.Identity, bias=pc[:, wi, b0 + ch:b0 + ch + 1],
                                   scale=pc[:, wi, w0 + 48 + ch:w0 + 49 + ch]).then_inc(conv_pre, 1)
                if u and u - 1 in conv_no:
                    tanh_of(u - 1)
                for stage, h in FOLLOW[u]:
                    if stage == "gates":
                        act.wait_ge(small_v, 2)
                        act.activation(smw[:, 1, :, :], smw[:, 0, :, :], ACT.Exp, scale=-1.0).then_inc(small_a, 1)
                        act.activation(alog[:, :], alog[:, :], ACT.Exp).then_inc(small_a, 1)
                        act.wait_ge(small_v, 3)
                        act.activation(smw[:, 3, :, :], smw[:, 2, :, :], ACT.Ln).then_inc(small_a, 1)
                    elif stage == "fox_a":
                        act.wait_ge(fox_negmax, h + 1)
                        if h >= 2:
                            act.wait_ge(fox_turned, h - 1)
                        b = h % 2
                        act.activation(work[:, 2 + b, 0:T], work[:, b, 0:T], ACT.Exp, bias=nmx[:, b, 1:2],
                                       accum_out=rsum[:, b, 1:2]).then_inc(fox_exp, 1)
                        act.activation(work[:, 2 + b, T:384], work[:, b, T:384], ACT.Exp, bias=nmx[:, b, 0:1],
                                       accum_out=rsum[:, b, 0:1]).then_inc(fox_exp, 1)
                    elif stage == "fox_b":
                        act.wait_ge(fox_turned, h + 1)
                        if h >= 2:
                            act.wait_ge(fox_out, h - 1)
                        act.activation(work[:, 4 + h % 2, :], TR[:, 0:384], ACT.Copy).then_inc(fox_pt, 1)
                    elif stage == "ssd_a":
                        act.wait_ge(ssd_seg, 2 * h + 2)
                        if h >= 2:
                            act.wait_ge(ssd_w, h - 1)
                        act.activation(work[:, 2 + h % 2, :], work[:, h % 2, :], ACT.Exp).then_inc(ssd_exp, 1)
                    elif stage in ("ssd_norm", "ml_norm"):
                        k = 0 if stage == "ssd_norm" else 1
                        if k == 0:
                            act.wait_ge(ssd_y, 16)
                            act.wait_ge(z_out, 8)
                        else:
                            act.wait_ge(ml_y, 8)
                        for g in range(5):
                            if g < 4:
                                if g >= 2:
                                    act.wait_ge(nrm_ms, 4 * k + g - 1)
                                act.activation(work[:, 6 + 2 * (g % 2):8 + 2 * (g % 2), 0:T],
                                               yT[:, 1 + k, 2 * g:2 * g + 2, :], ACT.Square).then_inc(nrm_sq, 1)
                            if g:
                                act.wait_ge(nrm_ms, 4 * k + g)
                                q = g - 1
                                if q >= 2 or k:
                                    act.wait_ge(nrm_y, 8 * k + 2 * (q - 1) if q >= 2 else 8)
                                act.activation(tmpu[:, q % 2, :], OB[q % 2][:, 0:T], ACT.Sqrt, bias=eps[:, :])\
                                    .then_inc(nrm_rt, 1)
                    elif stage == "ml_a":
                        act.wait_ge(ml_neg, ML_NEG * (h + 1))
                        act.activation(work[:, 1, 0:T], work[:, 0, 0:T], ACT.Exp, bias=mls[:, 1, 1:2]).then_inc(ml_exp, 1)
                        act.activation(work[:, 1, T:384], work[:, 0, T:384], ACT.Exp, bias=mls[:, 1, 0:1])\
                            .then_inc(ml_exp, 1)
                        act.activation(mls[:, 3, :], mls[:, 2, :], ACT.Exp).then_inc(ml_exp, 1)
                    elif stage == "ml_b":
                        act.wait_ge(ml_turned, h + 1)
                        if h:
                            act.wait_ge(ml_out, 2 * h)
                        act.activation(work[:, 4, :], TR[:, 0:384], ACT.Copy).then_inc(ml_pt, 1)

            n = 0
            for t in range(NT):
                act.wait_ge(x1_ready, t + 1)
                act.activation(ss[:, 2 + t:3 + t], ss[:, t:t + 1], ACT.Sqrt, bias=eps[:, :], scale=1.0 / D)\
                    .then_inc(r_a, 1)
            for t in range(NT):
                act.wait_ge(r_v, RV_RSTD)
                act.activation(h2p[:, t, :, :], xs[:, t, :].rearrange("q (p c) -> q c p", c=KC), ACT.Copy,
                               scale=ss[:, 4 + t:5 + t]).then_inc(r_a, 1)
            act.wait_ge(r_p, 17)
            act.wait_ge(rt_in, 64)
            act.activation(lgT, TR[0:NR, 0:T], ACT.Identity, bias=brt[:, :]).then_inc(r_a, 1)
            act.wait_ge(r_v, RV_GSUB)
            act.activation(pe8[:, :, :], pe8[:, :, :], ACT.Exp).then_inc(r_a, 1)
            act.wait_ge(r_v, RV_VD)
            act.activation(rt[:, 4, :], rt[:, 3, :], ACT.Exp).then_inc(r_a, 1)

            act.wait_ge(r_v, RV_ITEMS)
            pairs = act.value_load(npair[0:1, 0:1], min_val=1, max_val=P // 2 - 1)
            with act.Fori(0, pairs) as i:
                for j in range(2):
                    act.wait_ge(gu_done, 2 * i + (j + 1))
                    act.activation(gus[:, j, :], GUB[:, T * j:T * j + T], ACT.Copy).then_inc(gu_copied, 1)
                    act.wait_ge(hid_turned, 2 * i + (j + 1))
                    act.activation(tht[:, j, :, :], TRB[:, T * j:T * j + T].rearrange("p (i s) -> p i s", i=2)[:, :, 0:64],
                                   ACT.Tanh, scale=0.5).then_inc(hid_tanh, 1)
                    act.wait_ge(down_done, 2 * i + (j + 1))
                    act.activation(ysb[:, j, :], DNB[:, T * j:T * j + T], ACT.Copy).then_inc(y_copied, 1)
            for t in range(NT):
                act.wait_ge(fin_v, FIN_SQ[t])
                act.activation(ss[:, 2 + t:3 + t], ss[:, t:t + 1], ACT.Sqrt, bias=eps[:, :], scale=1.0 / D)\
                    .then_inc(fin_a, 1)

        @block.vector
        def _(dve):
            steps = 0

            def step(ins):
                nonlocal steps
                steps += 1
                ins.then_inc(dstep, 1)
                dve.wait_ge(dstep, steps)

            def recip_rms(t):
                step(dve.reciprocal(ss[:, 4 + t:5 + t], ss[:, 2 + t:3 + t]))

            for t in range(NT):
                dve.wait_ge(x_in, 32)
                dve.tensor_tensor_reduce(bigt, xs[:, t, :], xs[:, t, :], 1.0, 0.0, ALU.mult, ALU.add,
                                         ss[:, t:t + 1]).then_inc(x_sq, 1)
                dve.wait_ge(x_sq, t + 1)
            dve.wait_ge(par_turned, 1)
            dve.tensor_copy(pc[:, 0, :], SC[0][:, 0:104]).then_inc(par_ready, 1)
            dve.tensor_scalar(pc[:, 1, :], SC[0][:, 104:208], 0.5, None, ALU.mult).then_inc(par_ready, 1)
            dve.wait_ge(par_ready, 2)
            dve.tensor_scalar(pc[:, 0, 8:88], pc[:, 0, 8:88], 0.5, None, ALU.mult).then_inc(par_ready, 1)
            dve.wait_ge(par_ready, 3)
            step(dve.tensor_scalar(pc[:, 0, 96:104], pc[:, 0, 96:104], 0.5, None, ALU.mult))
            for t in range(NT):
                dve.wait_ge(astep, t + 1)
                recip_rms(t)
                dve.tensor_scalar(hN[:, t, :], xs[:, t, :], ss[:, 4 + t:5 + t], None, ALU.mult).then_inc(x_norm, 1)
            for t in range(NT):
                for c in range(KC):
                    dve.wait_ge(h_turned, 8 * t + 4 * (c // 4) + 4)
                    dve.tensor_scalar(hT[:, c, P * t:P * t + P], OB[c // 4][:, P * (c % 4):P * (c % 4) + P],
                                      pc[:, 0, c:c + 1], None, ALU.mult).then_inc(h_ready, 1)
            def silu_of(u):
                i = conv_no[u]
                kind, n, part, chunk = UNITS[u]
                dve.wait_ge(conv_tanh, i + 1)
                dst = {"xbc": xbcT, "mq": qT, "mk": kT}[kind]
                dve.scalar_tensor_tensor(dst[:, chunk, :], thb[:, i % 3, :], 1.0, acc[:, i % 3, :], ALU.add, ALU.mult)\
                    .then_inc(conv_out, 1)

            def ssd_weights(h):
                b = h % 2
                dve.wait_ge(ssd_exp, h + 1)
                dve.wait_ge(ssd_cbm, h // 4 + 1)
                if h >= 2:
                    dve.wait_ge(ssd_out, h - 1)
                dve.tensor_tensor(work[:, 4 + b, :], work[:, 2 + b, :], cbm[:, h // 4, :], ALU.mult).then_inc(ssd_w, 1)

            for u, (kind, n, part, chunk) in enumerate(UNITS):
                pj = PJ[u % BANKS]
                if u in conv_no:
                    i = conv_no[u]
                    wi, w0, ch = (0, 8, chunk) if kind == "xbc" else (1, 0, chunk + (8 if kind == "mk" else 0))
                    dve.wait_ge(conv_pre, i + 1)
                    a = acc[:, i % 3, :]
                    for back in (1, 2, 3):
                        k = w0 + 16 * (3 - back) + ch
                        ins = dve.scalar_tensor_tensor(a[:, back:T], pj[:, 0:T - back], pc[:, wi, k:k + 1], a[:, back:T],
                                                       ALU.mult, ALU.add)
                        if back < 3:
                            step(ins)
                    ins.then_inc(conv_sum, 1)
                elif kind == "z":
                    i = u - Z0
                    dve.wait_ge(z_tanh, i + 1)
                    dve.scalar_tensor_tensor(zu[:, chunk, :], work[:, 8 + i % 2, 0:T], 1.0, pj[:, 0:T], ALU.add, ALU.mult)\
                        .then_inc(z_out, 1)
                elif kind == "br":
                    b, oc = divmod(chunk, KC)
                    dve.wait_ge(proj, u + 1)
                    if u == BR0:
                        dve.wait_ge(nrm_y, 8)
                    gate = gT[:, chunk, :]
                    if b == 0:
                        dve.scalar_tensor_tensor(zu[:, oc, :], gate, 1.0, pj[:, 0:T], ALU.add, ALU.mult)\
                            .then_inc(u_ready, 1)
                    else:
                        dve.wait_ge(u_ready, u - BR0 - 1)
                        step(dve.scalar_tensor_tensor(tmpu[:, u % 2, :], gate, 1.0, pj[:, 0:T], ALU.add, ALU.mult))
                        dve.tensor_tensor(zu[:, oc, :], zu[:, oc, :], tmpu[:, u % 2, :], ALU.add).then_inc(u_ready, 1)
                elif kind == "out":
                    dve.wait_ge(proj, u + 1)
                    xo = xs[:, part, 512 * chunk:512 * chunk + 512]
                    dve.scalar_tensor_tensor(xo, pj[:, :], 0.5, xo, ALU.mult, ALU.add).then_inc(x1_part, 1)
                    dve.wait_ge(x1_part, u - OUT0 + 1)
                if u and u - 1 in conv_no:
                    silu_of(u - 1)
                for stage, h in FOLLOW[u]:
                    if stage == "gates":
                        dve.wait_ge(small_done, 2)
                        dve.tensor_tensor(sm[:, :, :], TR[:, 0:80].rearrange("p (t n) -> p t n", t=NT),
                                          bsm[:, None, :].to_broadcast([P, NT, 40]), ALU.add).then_inc(small_v, 1)
                        dve.wait_ge(small_v, 1)
                        dve.scalar_tensor_tensor(smw[:, 0, :, :], sm[:, :, :], -1.0, sm[:, :, :], ALU.mult, ALU.max)\
                            .then_inc(small_v, 1)
                        dve.wait_ge(small_a, 1)
                        dve.tensor_scalar(smw[:, 2, :, :], smw[:, 1, :, :], 1.0, None, ALU.add).then_inc(small_v, 1)
                        dve.wait_ge(small_v, 3)
                        step(dve.scalar_tensor_tensor(smw[:, 4, :, :], smw[:, 2, :, :], -1.0, smw[:, 1, :, :], ALU.add, ALU.subtract))
                        dve.wait_ge(small_a, 3)
                        step(dve.tensor_tensor(smw[:, 5, :, :], smw[:, 3, :, :], smw[:, 4, :, :], ALU.subtract))
                        softplus = smw[:, 5, :, :]
                        step(dve.scalar_tensor_tensor(dtt[:, :, :], sm[:, :, 16:32], 0.0, softplus[:, :, 16:32], ALU.max, ALU.add))
                        step(dve.scalar_tensor_tensor(gl[:, :, 0:16], sm[:, :, 0:16], 0.0, softplus[:, :, 0:16],
                                                      ALU.min, ALU.subtract))
                        step(dve.scalar_tensor_tensor(gl[:, :, 32:36], sm[:, :, 36:40], 0.0, softplus[:, :, 36:40],
                                                      ALU.min, ALU.subtract))
                        dve.scalar_tensor_tensor(gl[:, :, 16:32], dtt[:, :, :], -1.0, alog[:, None, :].to_broadcast([P, NT, 16]),
                                                 ALU.mult, ALU.mult).then_inc(small_v, 1)
                    elif stage == "sums":
                        dve.wait_ge(cum_done, 1)
                        for t in range(NT):
                            dve.tensor_copy(cum[:, t, :], TR[:, 128 + 64 * t:164 + 64 * t]).then_inc(cum_ready, 1)
                        dve.wait_ge(cum_ready, 2)
                        dve.tensor_scalar(rn[:, :, 0:16], cum[:, :, 0:16], -1.0, None, ALU.mult).then_inc(cum_ready, 1)
                        dve.tensor_tensor(rn[:, :, 16:20], sm[:, :, 32:36], cum[:, :, 32:36], ALU.subtract).then_inc(cum_ready, 1)
                    elif stage == "fox_a":
                        b = h % 2
                        dve.wait_ge(fox_scores, h + 1)
                        if h >= 2:
                            dve.wait_ge(fox_exp, 2 * (h - 1))
                        dve.tensor_tensor_reduce(work[:, b, 0:T], SC[b][:, 0:T], mneg[:, :], 1.0, -3e38,
                                                 ALU.add, ALU.max, mx[:, b, 1:2]).then_inc(fox_masked, 1)
                        dve.tensor_tensor_reduce(work[:, b, T:384], SC[b][:, T:384], mneg[:, P:T], 1.0, -3e38,
                                                 ALU.add, ALU.max, mx[:, b, 0:1]).then_inc(fox_masked, 1)
                        dve.wait_ge(fox_masked, 2 * h + 2)
                        dve.tensor_scalar(nmx[:, b, :], mx[:, b, :], -1.0, None, ALU.mult).then_inc(fox_negmax, 1)
                    elif stage == "fox_p":
                        b = h % 2
                        dve.wait_ge(fox_exp, 2 * h + 2)
                        step(dve.reciprocal(rinv[:, b, :], rsum[:, b, :]))
                        p = work[:, 2 + b, :]
                        dve.tensor_scalar(p[:, 0:T], p[:, 0:T], rinv[:, b, 1:2], None, ALU.mult).then_inc(fox_probs, 1)
                        dve.tensor_scalar(p[:, T:384], p[:, T:384], rinv[:, b, 0:1], None, ALU.mult)\
                            .then_inc(fox_probs, 1)
                    elif stage == "fox_c" and h % 2:
                        dve.wait_ge(fox_out, h + 1)
                        dve.tensor_copy(yT[:, 0, h // 2, :], OB[(h // 2) % 2][:, 0:T]).then_inc(fox_y, 1)
                    elif stage == "ssd_x":
                        dve.wait_ge(ssd_turned, h + 1)
                        dve.tensor_tensor(
                            xdt[:, :, P * h:P * h + P].rearrange("p t (a d) -> p t a d", a=2),
                            (TR, OB[0])[h % 2][:, 0:T].rearrange("p (t a d) -> p t a d", t=NT, a=2),
                            dtt[:, :, 2 * h:2 * h + 2, None].to_broadcast([P, NT, 2, 64]), ALU.mult).then_inc(ssd_x, 1)
                    elif stage == "ssd_cb":
                        dve.wait_ge(ssd_cb, h + 1)
                        dve.tensor_tensor(cbm[:, h, :], OB[1][:, 0:384], mask01[:, :], ALU.mult).then_inc(ssd_cbm, 1)
                    elif stage == "ssd_a":
                        b = h % 2
                        dve.wait_ge(ssd_bc, h + 1)
                        if h >= 2:
                            dve.wait_ge(ssd_exp, h - 1)
                        dve.tensor_scalar(work[:, b, 0:T], SC[b][:, 0:T], cum[:, 0, 16 + h:17 + h], 0.0,
                                          ALU.subtract, ALU.min).then_inc(ssd_seg, 1)
                        dve.tensor_scalar(work[:, b, T:384], SC[b][:, P:T], cum[:, 1, 16 + h:17 + h], 0.0,
                                          ALU.subtract, ALU.min).then_inc(ssd_seg, 1)
                        if h:
                            ssd_weights(h - 1)
                        if h == 15:
                            ssd_weights(15)
                    elif stage == "ssd_c" and h % 2:
                        c = h // 2
                        dve.wait_ge(ssd_out, h + 1)
                        dve.wait_ge(conv_out, 16)
                        dve.wait_ge(z_out, 8)
                        dve.scalar_tensor_tensor(yT[:, 1, c, :], xbcT[:, c, :], dsk[:, c:c + 1],
                                                 OB[c % 2][:, 0:T], ALU.mult, ALU.add).then_inc(ssd_y, 1)
                        dve.wait_ge(ssd_y, 2 * c + 1)
                        dve.scalar_tensor_tensor(yT[:, 1, c, :], yT[:, 1, c, :], 0.5, zu[:, c, :], ALU.mult, ALU.mult)\
                            .then_inc(ssd_y, 1)
                    elif stage in ("ssd_norm", "ml_norm"):
                        k = 0 if stage == "ssd_norm" else 1
                        for g in range(4):
                            dve.wait_ge(nrm_rt, 4 * k + g + 1)
                            step(dve.reciprocal(tmpu[:, g % 2, :], tmpu[:, g % 2, :]))
                            for c in (2 * g, 2 * g + 1):
                                wcol = pc[:, 0, (88 if k == 0 else 96) + c:(89 if k == 0 else 97) + c]
                                y = yT[:, 1 + k, c, :]
                                if k == 0:
                                    dve.scalar_tensor_tensor(y, y, wcol, tmpu[:, g % 2, :], ALU.mult, ALU.mult)\
                                        .then_inc(nrm_y, 1)
                                else:
                                    step(dve.scalar_tensor_tensor(y, y, wcol, tmpu[:, g % 2, :], ALU.mult, ALU.mult))
                                    dve.scalar_tensor_tensor(y, moT[:, c, :], 1.0, y, ALU.add, ALU.mult)\
                                        .then_inc(nrm_y, 1)
                    elif stage == "ml_a":
                        dve.wait_ge(ml_scores, h + 1)
                        if h == 0:
                            dve.wait_ge(ssd_exp, 16)
                        dve.tensor_tensor_reduce(work[:, 0, 0:T], SC[1][:, 0:T], mneg[:, :], 1.0, -3e38,
                                                 ALU.add, ALU.max, mls[:, 0, 1:2]).then_inc(ml_neg, 1)
                        dve.tensor_tensor_reduce(work[:, 0, T:384], SC[1][:, 0:P], mneg[:, P:T], 1.0, -3e38,
                                                 ALU.add, ALU.max, mls[:, 0, 0:1]).then_inc(ml_neg, 1)
                        dve.wait_ge(ml_neg, ML_NEG * h + 2)
                        dve.tensor_scalar(mls[:, 1, :], mls[:, 0, :], 0.0, -1.0, ALU.max, ALU.mult).then_inc(ml_neg, 1)
                        dve.wait_ge(ml_neg, ML_NEG * h + 3)
                        dve.tensor_tensor(mls[:, 2, :], mls[:, 1, :], cum[:, :, 32 + h], ALU.subtract).then_inc(ml_neg, 1)
                    elif stage == "ml_b":
                        w = work[:, 2, :]
                        b0 = ML_W * h
                        if h:
                            dve.wait_ge(ml_turned, h)
                        dve.wait_ge(ml_exp, 3 * h + 3)
                        dve.tensor_tensor_reduce(w[:, 0:T], work[:, 1, 0:T], SC[0][:, 0:T], 256 ** -0.5, 0.0,
                                                 ALU.mult, ALU.add, mls[:, 4, 1:2]).then_inc(ml_w, 1)
                        dve.tensor_tensor_reduce(w[:, T:384], work[:, 1, T:384], SC[0][:, T:384], 256 ** -0.5, 0.0,
                                                 ALU.mult, ALU.add, mls[:, 4, 0:1]).then_inc(ml_w, 1)
                        dve.wait_ge(ml_w, b0 + 2)
                        step(dve.scalar_tensor_tensor(mls[:, 5, :], mls[:, 4, :], -1.0, mls[:, 4, :], ALU.mult, ALU.max))
                        step(dve.tensor_tensor(mls[:, 5, :], mls[:, 5, :], mls[:, 3, :], ALU.max))
                        step(dve.reciprocal(mls[:, 5, :], mls[:, 5, :]))
                        dve.tensor_scalar(w[:, 0:T], w[:, 0:T], mls[:, 5, 1:2], None, ALU.mult).then_inc(ml_w, 1)
                        dve.tensor_scalar(w[:, T:384], w[:, T:384], mls[:, 5, 0:1], None, ALU.mult).then_inc(ml_w, 1)
                    elif stage == "ml_c":
                        for i in range(2):
                            dve.wait_ge(ml_out, 2 * h + i + 1)
                            dve.tensor_copy(yT[:, 2, 2 * h + i, :], OB[i][:, 0:T]).then_inc(ml_y, 1)

            rv = 0

            def route(ins):
                nonlocal rv
                rv += 1
                ins.then_inc(r_v, 1)
                dve.wait_ge(r_v, rv)
                return rv

            for t in range(NT):
                dve.tensor_tensor_reduce(bigt, xs[:, t, :], xs[:, t, :], 1.0, 0.0, ALU.mult, ALU.add,
                                         ss[:, t:t + 1]).then_inc(x1_ready, 1)
                dve.wait_ge(x1_ready, t + 1)
            for t in range(NT):
                dve.wait_ge(r_a, t + 1)
                route(dve.reciprocal(ss[:, 4 + t:5 + t], ss[:, 2 + t:3 + t]))
            assert rv == RV_RSTD
            for t in range(NT):
                for half in range(2):
                    dve.wait_ge(r_p, 8 * t + 4 * half + 4)
                    n = route(dve.tensor_tensor(
                        h2T[:, 4 * half:4 * half + 4, P * t:P * t + P],
                        SC[half][:, :].rearrange("p (c t) -> p c t", c=4),
                        n2[:, 4 * half:4 * half + 4, None].to_broadcast([P, 4, P]), ALU.mult))
                assert n == RV_H2T[t] + 1
            dve.memset(bigt[:, 0:512], 0.0).then_inc(acc_zero, 1)
            dve.wait_ge(r_p, 18)
            route(dve.tensor_copy(lg[:, :, :], OB[0][:, 0:T].rearrange("p (t n) -> p t n", t=NT)[:, :, 0:NR]))

            def top8(src):
                for t in range(NT):
                    route(dve.max(top[:, t, :], src[:, t, :]))
                    route(dve.max_index(topi[:, t, :], top[:, t, :], src[:, t, :]))

            top8(lg[:, :, 0:NG])
            n = route(dve.tensor_tensor(pe8[:, :, :], lg[:, :, 0:NG], top[:, :, 0:1].to_broadcast([P, NT, NG]),
                                        ALU.subtract))
            assert n == RV_GSUB
            route(dve.tensor_copy(rt[:, 0, :], topi[:, :, 0]))
            route(dve.tensor_tensor(ohg[:, :, :], iota[:, None, 0:NG].to_broadcast([P, NT, NG]),
                                    rt[:, 0, :, None].to_broadcast([P, NT, NG]), ALU.is_equal))
            for t in range(NT):
                route(dve.tensor_tensor(egs[:, t, :, :], lg[:, t, NG:NR].rearrange("p (g e) -> p e g", g=NG),
                                        ohg[:, t, None, :].to_broadcast([P, EG, NG]), ALU.mult))
            route(dve.tensor_reduce(ein[:, :, :], egs[:, :, :, :], AX_X, ALU.add))
            top8(ein)
            n = route(dve.tensor_tensor(rt[:, 3, :], top[:, :, 1], top[:, :, 0], ALU.subtract))
            assert n == RV_VD
            route(dve.tensor_copy(eid[:, :, :], topi[:, :, 0:2]))
            route(dve.scalar_tensor_tensor(eid[:, :, :], rt[:, 0, :, None].to_broadcast([P, NT, 2]), float(EG),
                                           eid[:, :, :], ALU.mult, ALU.add))
            route(dve.tensor_tensor(ohe[:, :, :], iota[:, None, 0:NE].to_broadcast([P, NT * 2, NE]),
                                    eid[:, :, :].rearrange("p t k -> p (t k)")[:, :, None]
                                    .to_broadcast([P, NT * 2, NE]), ALU.is_equal))
            ohv = ohe[:, :, :].rearrange("p (t k) e -> p t k e", k=2)
            n = route(dve.tensor_tensor(ohm[:, :, :], ohv[:, :, 0, :], ohv[:, :, 1, :], ALU.add))
            assert n == RV_OHM
            dve.wait_ge(r_a, RA_LGT + 2)
            route(dve.tensor_reduce(rt[:, 1, :], pe8[:, :, :], AX_X, ALU.add))
            route(dve.tensor_scalar(rt[:, 5, :], rt[:, 4, :], 1.0, None, ALU.add))
            route(dve.tensor_tensor(rt[:, 6, :], rt[:, 5, :], rt[:, 1, :], ALU.mult))
            route(dve.reciprocal(wtok[:, :, 0], rt[:, 6, :]))
            route(dve.tensor_tensor(wtok[:, :, 1], wtok[:, :, 0], rt[:, 4, :], ALU.mult))
            dve.wait_ge(r_p, 19)
            for t in range(NT):
                route(dve.tensor_tensor(rke[:, 2 * t:2 * t + 2, :], ohe[:, 2 * t:2 * t + 2, :],
                                        OB[1][:, None, NE * t:NE * t + NE].to_broadcast([P, 2, NE]), ALU.mult))
            route(dve.tensor_reduce(rank[:, :], rke[:, :, :], AX_X, ALU.add))
            n = route(dve.scalar_tensor_tensor(pos[:, :], eid[:, :, :].rearrange("p t k -> p (t k)"), float(T),
                                               rank[:, :], ALU.mult, ALU.add))
            assert n == RV_POS
            route(dve.tensor_tensor(cnt8[:, :, :], OB[1][:, 2 * NE:3 * NE, None].to_broadcast([P, NE, 8]),
                                    thr[:, None, :].to_broadcast([P, NE, 8]), ALU.is_gt))
            route(dve.tensor_reduce(nbk[:, 0, :], cnt8[:, :, :], AX_X, ALU.add))
            route(dve.tensor_tensor(nbk[:, 0, :], nbk[:, 0, :], two[:, :], ALU.subtract))
            route(dve.tensor_scalar(nbk[:, 0, :], nbk[:, 0, :], 0.0, None, ALU.max))
            route(dve.tensor_tensor_scan(nbk[:, 1, :], ones[:, 0:NE], nbk[:, 0, :], 0.0, ALU.mult, ALU.add))
            route(dve.tensor_scalar(nbk[:, 2, :], nbk[:, 1, :], pidx[:, :], None, ALU.is_le))
            route(dve.tensor_reduce(itc[:, 1:2], nbk[:, 2, :], AX_X, ALU.add))
            route(dve.tensor_tensor(nbk[:, 2, :], nbk[:, 2, :], nbk[:, 0, :], ALU.mult))
            route(dve.tensor_reduce(itc[:, 2:3], nbk[:, 2, :], AX_X, ALU.add))
            route(dve.tensor_tensor(itc[:, 3:4], pidx[:, :], itc[:, 2:3], ALU.subtract))
            route(dve.tensor_scalar(itc[:, 4:5], itc[:, 1:2], 2.0, None, ALU.is_lt))
            route(dve.tensor_tensor(itc[:, 3:4], itc[:, 3:4], itc[:, 4:5], ALU.add))
            route(dve.tensor_scalar(itc[:, 5:6], itc[:, 1:2], float(T), None, ALU.mult))
            route(dve.scalar_tensor_tensor(itc[:, 0:1], itc[:, 3:4], float(SLOT), itc[:, 5:6], ALU.mult, ALU.add))
            n = route(dve.tensor_scalar(itc[:, 1:2], itc[:, 1:2], float(NE - 1), None, ALU.min))
            assert n == RV_ITC
            route(dve.tensor_scalar(itc[:, 6:7], nbk[:, 1, NE - 1:NE], 2.0, 0.5, ALU.add, ALU.mult))
            route(dve.tensor_scalar(base[:, :], iota[:, :], itc[:, 6:7], None, ALU.is_lt))
            route(dve.tensor_reduce(itc[:, 7:8], base[:, :], AX_X, ALU.add))
            route(dve.tensor_copy(npair[:, :], itc[:, 7:8]))
            dve.wait_ge(r_p, 20)
            route(dve.tensor_copy(posb, SC[0][:, :]))
            route(dve.tensor_copy(wb, SC[1][:, :]))
            dve.wait_ge(r_p, 21)
            route(dve.tensor_copy(base[:, :], TR[:, 0:P]))
            route(dve.memset(base[:, 0:1], 0.0))
            route(dve.memset(base[:, 1:2], float(T)))
            n = route(dve.tensor_copy(eint[:, :], TR[:, P:T]))
            assert n == RV_ITEMS

            def pick_pair(cols, first):
                k = first
                dve.tensor_copy(bnxt[:, :], cols).then_inc(pick_v, 1)
                dve.wait_ge(pick_v, k + 1)
                dve.tensor_tensor(tgt.rearrange("p (j s) -> p j s", j=2), iota[:, None, 0:SLOT].to_broadcast([P, 2, SLOT]),
                                  bnxt[:, :, None].to_broadcast([P, 2, SLOT]), ALU.add).then_inc(pick_v, 1)
                dve.wait_ge(pick_v, k + 2)
                for t in range(NT):
                    dve.tensor_scalar(pick[:, t, :], tgt, pos[:, 2 * t:2 * t + 1], None, ALU.is_equal)\
                        .then_inc(pick_v, 1)
                dve.wait_ge(pick_v, k + 4)
                dve.scalar_tensor_tensor(pick[:, 0, :], tgt, pos[:, 1:2], pick[:, 0, :], ALU.is_equal, ALU.add)\
                    .then_inc(pick_v, 1)
                dve.wait_ge(pick_v, k + 5)
                dve.scalar_tensor_tensor(pick[:, 1, :], tgt, pos[:, 3:4], pick[:, 1, :], ALU.is_equal, ALU.add)\
                    .then_inc(picked, 1)

            def keep_gathered(i):
                dve.tensor_tensor(xg, GAB[:, :].rearrange("p (c s) -> p c s", c=KC),
                                  n2[:, :, None].to_broadcast([P, KC, 64]), ALU.mult).then_inc(xg_ready, 1)

            pairs = dve.value_load(npair[0:1, 0:1], min_val=1, max_val=P // 2 - 1)
            pick_pair(base[:, 0:2], 0)
            dve.wait_ge(gathered, 1)
            keep_gathered(0)
            with dve.Fori(0, pairs) as i:
                dve.tensor_copy(bcur[:, :], base[:, bass.ds(2 * i, 2)]).then_inc(comb_v, 1)
                dve.wait_ge(comb_v, 4 * i + 1)
                dve.tensor_scalar(scol[:, :], bcur[:, :], pmod[:, :], None, ALU.add).then_inc(comb_v, 1)
                dve.wait_ge(comb_v, 4 * i + 2)
                dve.wait_ge(comb_done, 2 * i + 1)
                for j in range(2):
                    dve.scalar_tensor_tensor(combt, posb, scol[:, j:j + 1], wb, ALU.is_equal, ALU.mult)\
                        .then_inc(comb_v, 1)
                    dve.wait_ge(comb_v, 4 * i + (3 + j))
                    dve.tensor_tensor(comb[:, j, :], combt[:, 0:T], combt[:, T:2 * T], ALU.add).then_inc(combined, 1)
                    dve.wait_ge(combined, 2 * i + (j + 1))
                dve.wait_ge(gathered, i + 1)
                pick_pair(base[:, bass.ds(2 * i + 2, 2)], 5 * i + 5)
                for j in range(2):
                    tr = TRB[:, T * j:T * j + T].rearrange("p (i s) -> p i s", i=2)
                    dve.wait_ge(hid_tanh, 2 * i + (j + 1))
                    dve.scalar_tensor_tensor(gt1[:, j, :, :], tht[:, j, :, :], 1.0, tr[:, :, 0:64], ALU.add, ALU.mult)\
                        .then_inc(hid_v, 1)
                    dve.wait_ge(hid_v, 4 * i + (2 * j + 1))
                    dve.scalar_tensor_tensor(actT[:, j, :, :], gt1[:, j, :, :], 0.5, tr[:, :, 64:128],
                                             ALU.mult, ALU.mult).then_inc(hid_v, 1)
                dve.wait_ge(gathered, i + 2)
                keep_gathered(i)

            fv = 0

            def fin(ins):
                nonlocal fv
                fv += 1
                ins.then_inc(fin_v, 1)
                dve.wait_ge(fin_v, fv)
                return fv

            dve.wait_ge(comb_done, 2 * pairs + 1)
            dve.wait_ge(fw_in, 16)
            for t in range(NT):
                for n in range(4):
                    xo = xs[:, t, T * n:T * n + T]
                    fin(dve.tensor_tensor(xo, xo, ACCB[n][:, T * t:T * t + T], ALU.add))
                n = fin(dve.tensor_tensor_reduce(bigt, xs[:, t, :], xs[:, t, :], 1.0, 0.0, ALU.mult, ALU.add,
                                                 ss[:, t:t + 1]))
                assert n == FIN_SQ[t]
            for t in range(NT):
                dve.wait_ge(fin_a, t + 1)
                fin(dve.reciprocal(ss[:, 4 + t:5 + t], ss[:, 2 + t:3 + t]))
                n = fin(dve.scalar_tensor_tensor(xs[:, t, :], xs[:, t, :], ss[:, 4 + t:5 + t], fw, ALU.mult, ALU.mult))
                assert n == FIN_OUT[t]


_INS = ["x", "norm1_w", "w_in", "att_f_bias", "ssd_conv_w", "ssd_conv_b", "ssd_dt_bias", "ssd_a_log", "ssd_d",
        "ssd_norm_w", "ml_conv_w", "ml_conv_b", "ml_i_bias", "ml_f_bias", "ml_norm_w", "gate_bias", "w_branch",
        "w_out", "norm2_w", "w_group", "b_group", "w_expert_router", "b_expert_router", "w_gate", "w_up", "w_down",
        "final_norm_w"]


def kernel(**inputs):
    import numpy as np
    import concourse.bacc as bacc
    from concourse.bass_utils import run_bass_kernel_spmd

    nc = bacc.Bacc("TRN2", target_bir_lowering=False, num_devices=1)
    arrays, args = {}, []
    for name in _INS:
        a = np.ascontiguousarray(inputs[name])
        arrays[f"in_{name}"] = a
        args.append(nc.dram_tensor(f"in_{name}", a.shape, mybir.dt.from_np(a.dtype), kind="ExternalInput").ap())
    args.append(nc.dram_tensor("out_0", inputs["x"].shape, F32, kind="ExternalOutput").ap())
    build_trunk(nc, *args)
    r = run_bass_kernel_spmd(nc, [arrays], core_ids=[0])
    return r.results[0]["out_0"]
```

```python
from contextlib import ExitStack

import concourse.bass as bass
from concourse import mybir

F32 = mybir.dt.float32
I32 = mybir.dt.int32
U32 = mybir.dt.uint32
ALU = mybir.AluOpType
ACT = mybir.ActivationFunctionType
AX_X = mybir.AxisListType.X

P = 128
EPS = 1e-6
MASKED = -1e30


def plan(D, W):
    blocks, units = [], []
    col = 0
    at = {}
    for name, width in (("aq", D), ("ak", D), ("av", D), ("af", 16), ("z", D), ("xbc", 2 * D), ("dt", 16),
                        ("mq", D), ("mk", D), ("mv", D), ("mi", 4), ("mf", 4), ("mo", D), ("g", 3 * D)):
        at[name] = col
        col += width
    assert col == W
    for name in ("aq", "ak", "av", "xbc", "z", "mq", "mk", "mv", "mo", "g", "br", "out"):
        width = {"xbc": 2 * D, "g": 3 * D, "br": 3 * D}.get(name, D)
        for b in range(width // 512):
            if name == "br":
                blocks.append(("br", b // 2, 512 * (b % 2)))
            elif name == "out":
                blocks.append(("out", 0, 512 * b))
            else:
                blocks.append(("in", 0, at[name] + 512 * b))
            n = len(blocks) - 1
            if name == "out":
                if b:
                    units += [(name, n - 1 + h, t, h) for t in range(2) for h in range(2)]
            elif name in ("av", "mv"):
                units += [(name, n, t, b) for t in range(2)]
            else:
                units += [(name, n, c, 4 * b + c) for c in range(4)]
    return blocks, units, at


def stages(units):
    first = {}
    for u, unit in enumerate(units):
        first.setdefault(unit[0], u)
    follow = [[] for _ in units]
    follow[1].append(("gates", 0))
    follow[4].append(("sums", 0))
    u0 = first["xbc"]
    for s in range(19):
        follow[u0 + s] += [(k, s - lag) for lag, k in enumerate(("fox_a", "fox_p", "fox_b", "fox_c"))
                           if 0 <= s - lag < 16]
    u0 = first["mq"]
    for s in range(24):
        if s < 8:
            follow[u0 + s] += [("ssd_x", s)] + ([("ssd_cb", s // 2)] if s % 2 else [])
        if 0 <= s - 6 < 16:
            follow[u0 + s] += [("ssd_a", s - 6)]
        if 0 <= s - 8 < 16:
            follow[u0 + s] += [("ssd_c", s - 8)]
    follow[first["g"]] += [("ssd_norm", 0)]
    for h in range(4):
        u = first["g"] + 2 + 5 * h
        follow[u] += [("ml_a", h)]
        follow[u + 2] += [("ml_b", h)]
        follow[u + 3] += [("ml_c", h)]
    follow[first["g"] + 22] += [("ml_norm", 0)]
    return follow, first


def build_trunk(nc, x, norm1_w, w_in, att_f_bias, ssd_conv_w, ssd_conv_b, ssd_dt_bias, ssd_a_log, ssd_d,
                ssd_norm_w, ml_conv_w, ml_conv_b, ml_i_bias, ml_f_bias, ml_norm_w, gate_bias, w_branch, w_out,
                norm2_w, w_group, b_group, w_expert_router, b_expert_router, w_gate, w_up, w_down,
                final_norm_w, out):
    D = x.shape[2]
    T = x.shape[1]
    NT = T // P
    KC = D // P
    NE = w_gate.shape[1]
    NG = w_group.shape[2]
    EG = NE // NG
    FE = w_gate.shape[3]
    HC = FE // P
    NR = NG + NE
    SLOT = 32
    assert (D, T, NE, NG, FE) == (1024, 256, 64, 8, 512)
    BLOCKS, UNITS, COL = plan(D, w_in.shape[2])
    FOLLOW, FIRST = stages(UNITS)
    NB = len(BLOCKS)
    RING = 3
    BANKS = 3
    NU = len(UNITS)
    LAST = {unit[1]: u for u, unit in enumerate(UNITS)}
    CONSTS = 26
    PAR_IN = 16 * 21
    SMALL_GL = 4
    ML_NEG, ML_W = 4, 4

    ctx = ExitStack()
    with ctx:
        def sb(name, shape, dt=F32):
            return ctx.enter_context(nc.sbuf_tensor(name, shape, dt))

        def sem(name):
            return ctx.enter_context(nc.semaphore(name))

        xs = sb("xs", [P, NT, D])
        ring = sb("ring", [P, RING, KC, 512])
        r1 = sb("r1", [P, 12288])
        r2 = sb("r2", [P, 6144])
        zu = sb("zu", [P, KC, T])
        r3 = sb("r3", [P, 6144])
        cbm = sb("cbm", [P, 4, 384])
        ident = sb("ident", [P, P])
        tri = sb("tri", [P, P])
        stri = sb("stri", [P, P])
        ones = sb("ones", [P, P])
        mean = sb("mean", [P, P])
        mask01 = sb("mask01", [P, 384])
        mneg = sb("mneg", [P, 256])
        eps = sb("eps", [P, 1])
        pc = sb("pc", [P, 2, 112])
        prow = sb("prow", [112, 2, P])
        n2 = sb("n2", [P, KC])
        dsk = sb("dsk", [P, KC])
        wsm = sb("wsm", [P, KC, 40])
        bsm = sb("bsm", [P, 40])
        alog = sb("alog", [P, 16])
        sm = sb("sm", [P, NT, 40])
        smw = sb("smw", [P, 6, NT, 40])
        dtt = sb("dtt", [P, NT, 16])
        gl = sb("gl", [P, NT, 36])
        li = sb("li", [P, NT, 4])
        cum = sb("cum", [P, NT, 36])
        rn = sb("rn", [P, NT, 20])
        ss = sb("ss", [P, 8])
        work = sb("work", [P, 10, 384])
        acc = sb("acc", [P, 3, T])
        thb = sb("thb", [P, 3, T])
        mx = sb("mx", [P, 2, 2])
        nmx = sb("nmx", [P, 2, 2])
        rsum = sb("rsum", [P, 2, 2])
        rinv = sb("rinv", [P, 2, 2])
        mls = sb("mls", [P, 6, 2])
        tmpu = sb("tmpu", [P, 2, T])
        sqj = thb[:, :, :].rearrange("p a b -> p (a b)")[:, 0:512]
        bigt = work[:, :, :].rearrange("p a b -> p (a b)")[:, 0:D]

        qT = r1[:, 0:2048].rearrange("p (c t) -> p c t", c=KC)
        kT = r1[:, 2048:4096].rearrange("p (c t) -> p c t", c=KC)
        vN = r1[:, 4096:6144].rearrange("p (t n) -> p t n", t=NT)
        moT = r1[:, 6144:8192].rearrange("p (c t) -> p c t", c=KC)
        hT = r1[:, 8192:10240].rearrange("p (c t) -> p c t", c=KC)
        hN = r1[:, 10240:12288].rearrange("p (t n) -> p t n", t=NT)
        xbcT = r2[:, 0:4096].rearrange("p (c t) -> p c t", c=2 * KC)
        xdt = r2[:, 4096:6144].rearrange("p (t n) -> p t n", t=NT)
        gT = r2[:, :].rearrange("p (c t) -> p c t", c=3 * KC)
        yT = r3[:, :].rearrange("p (b c t) -> p b c t", b=3, c=KC)
        h2p = r3[:, 0:2048].rearrange("p (t c d) -> p t c d", t=NT, c=KC)
        x1T = r3[:, 2048:4096].rearrange("p (c t) -> p c t", c=KC)
        posb = r3[:, 4096:4608]
        wb = r3[:, 4608:5120]
        comb = r3[:, 5120:5632].rearrange("p (j t) -> p j t", j=2)
        combt = r3[:, 5632:6144]
        wg_s = [r1[:, 0:4096].rearrange("p (c n) -> p c n", c=KC), ring[:, 0, :, :]]
        wu_s = [r1[:, 4096:8192].rearrange("p (c n) -> p c n", c=KC), ring[:, 1, :, :]]
        wd_s = [r1[:, 8192:12288].rearrange("p (c n) -> p c n", c=HC),
                ring[:, 2, :, :].rearrange("p a b -> p (a b)").rearrange("p (c n) -> p c n", c=HC)]
        xg = r2[:, 0:512].rearrange("p (c s) -> p c s", c=KC)
        gus = r2[:, 512:1024].rearrange("p (j n) -> p j n", j=2)
        tht = r2[:, 1024:1280].rearrange("p (j i s) -> p j i s", j=2, i=2)
        gt1 = r2[:, 1280:1536].rearrange("p (j i s) -> p j i s", j=2, i=2)
        actT = r2[:, 1536:1792].rearrange("p (j i s) -> p j i s", j=2, i=2)
        ysb = r2[:, 1792:2304].rearrange("p (j n) -> p j n", j=2)
        pick = r2[:, 2304:2432].rearrange("p (t s) -> p t s", t=2)
        tgt = r2[:, 2432:2496]
        fw = r2[:, 2560:2560 + D]
        wrt = sb("wrt", [P, KC, NR])
        brow = sb("brow", [P, NR])
        lg = r2[:, 3584:3728].rearrange("p (t n) -> p t n", t=NT)
        top = sb("top", [P, NT, 8])
        tope = sb("tope", [P, NT, 8])
        tally = sb("tally", [P, NE])
        topi = sb("topi", [P, NT, 8], U32)
        rt = sb("rt", [P, 24, NT])
        ohg = sb("ohg", [P, NT, NG])
        egs = r2[:, 3728:3856].rearrange("p (t e g) -> p t e g", t=NT, e=EG)
        ein = sb("ein", [P, NT, EG])
        pe8 = sb("pe8", [P, NT, NG])
        eid = sb("eid", [P, NT, 2])
        ohe = r2[:, 3856:4112].rearrange("p (a e) -> p a e", e=NE)
        ohm = r2[:, 4368:4496].rearrange("p (a e) -> p a e", e=NE)
        rke = r2[:, 4112:4368].rearrange("p (a e) -> p a e", e=NE)
        rank = sb("rank", [P, NT * 2])
        pos = sb("pos", [P, NT * 2])
        wtok = sb("wtok", [P, NT, 2])
        iota = sb("iota", [P, P])
        thr = sb("thr", [P, 8])
        pmod = sb("pmod", [P, 1])
        pidx = sb("pidx", [P, 1])
        first_blk = r2[:, 5200:5712].rearrange("p (e b) -> p e b", b=8)
        gcst = r2[:, 5712:5776]
        place0 = sb("place0", [P, 1])
        halfc = sb("halfc", [P, 2])
        cnt8 = r2[:, 4496:5008].rearrange("p (e b) -> p e b", b=8)
        nbk = r2[:, 5008:5200].rearrange("p (a e) -> p a e", e=NE)
        itc = sb("itc", [P, 8])
        base = sb("base", [P, P])
        eint = sb("eint", [P, P], I32)
        npf = sb("npf", [P, 2])
        npair = sb("npair", [P, 2], I32)
        bcur = sb("bcur", [P, 2])
        bnxt = sb("bnxt", [P, 2])
        scol = sb("scol", [P, 2])

        acc4 = ctx.enter_context(nc.psum_tensor("acc4", [P, 4, 512], F32))
        bank = [acc4[:, i, :] for i in range(4)] + \
            [ctx.enter_context(nc.psum_tensor(f"bank{i}", [P, 512], F32)) for i in range(4, 8)]
        PJ = bank[0:3]
        SC = bank[3:5]
        TR = bank[5]
        OB = bank[6:8]
        ACCB = bank[0:4]
        GAB, GUB, TRB, DNB = bank[4:8]

        par_in = sem("par_in")
        x_in = sem("x_in")
        rt_in = sem("rt_in")
        w_in_sem = [sem(f"w_block{i}") for i in range(RING)]
        fw_in = sem("fw_in")
        x1_part = sem("x1_part")
        consts = sem("consts")
        dstep = sem("dstep")
        astep = sem("astep")
        x_sq = sem("x_sq")
        x_norm = sem("x_norm")
        h_turned = sem("h_turned")
        h_ready = sem("h_ready")
        par_turned = sem("par_turned")
        par_ready = sem("par_ready")
        small_done = sem("small_done")
        small_v = sem("small_v")
        small_a = sem("small_a")
        cum_done = sem("cum_done")
        cum_ready = sem("cum_ready")
        proj = sem("proj")
        kept = sem("kept")
        conv_pre = sem("conv_pre")
        conv_sum = sem("conv_sum")
        conv_tanh = sem("conv_tanh")
        conv_out = sem("conv_out")
        fox_scores = sem("fox_scores")
        fox_masked = sem("fox_masked")
        fox_negmax = sem("fox_negmax")
        fox_exp = sem("fox_exp")
        fox_probs = sem("fox_probs")
        fox_turned = sem("fox_turned")
        fox_pt = sem("fox_pt")
        fox_out = sem("fox_out")
        fox_y = sem("fox_y")
        z_tanh = sem("z_tanh")
        z_out = sem("z_out")
        ssd_turned = sem("ssd_turned")
        ssd_x = sem("ssd_x")
        ssd_cb = sem("ssd_cb")
        ssd_cbm = sem("ssd_cbm")
        ssd_bc = sem("ssd_bc")
        ssd_seg = sem("ssd_seg")
        ssd_exp = sem("ssd_exp")
        ssd_w = sem("ssd_w")
        ssd_out = sem("ssd_out")
        ssd_y = sem("ssd_y")
        nrm_sq = sem("nrm_sq")
        nrm_ms = sem("nrm_ms")
        nrm_rt = sem("nrm_rt")
        nrm_y = sem("nrm_y")
        ml_scores = sem("ml_scores")
        ml_neg = sem("ml_neg")
        ml_exp = sem("ml_exp")
        ml_w = sem("ml_w")
        ml_turned = sem("ml_turned")
        ml_pt = sem("ml_pt")
        ml_out = sem("ml_out")
        ml_y = sem("ml_y")
        g_ready = sem("g_ready")
        u_ready = sem("u_ready")
        r_v = sem("r_v")
        wrt_ready = sem("wrt_ready")
        x1_sq = sem("x1_sq")
        x1_sum = sem("x1_sum")
        x1_root = sem("x1_root")
        x1_rstd = sem("x1_rstd")
        h2_ready = sem("h2_ready")
        x1_turned = sem("x1_turned")
        x1_copied = sem("x1_copied")
        logits = sem("logits")
        chosen = sem("chosen")
        ranked = sem("ranked")
        placed = sem("placed")
        grp_sub = sem("grp_sub")
        grp_exp = sem("grp_exp")
        first_pick = sem("first_pick")
        item_cols = sem("item_cols")
        item_rows = sem("item_rows")
        items_ready = sem("items_ready")
        weighed = sem("weighed")
        place_rows = sem("place_rows")
        weight_rows = sem("weight_rows")
        rows_copied = sem("rows_copied")
        gu_in = [sem(f"gu_in{j}") for j in range(2)]
        dn_in = [sem(f"dn_in{j}") for j in range(2)]
        picked = sem("picked")
        combined = sem("combined")
        gathered = sem("gathered")
        xg_ready = sem("xg_ready")
        gu_done = sem("gu_done")
        gu_copied = sem("gu_copied")
        hid_turned = sem("hid_turned")
        hid_tanh = sem("hid_tanh")
        hid_v = sem("hid_v")
        down_done = sem("down_done")
        y_copied = sem("y_copied")
        comb_done = sem("comb_done")
        pick_v = sem("pick_v")
        comb_v = sem("comb_v")
        fin_sq = sem("fin_sq")
        fin_root = sem("fin_root")
        fin_rstd = sem("fin_rstd")
        fin_out = sem("fin_out")
        out_done = sem("out_done")

        lay = w_in[0]
        blk_src = {
            "in": lambda i, c: lay[:, c:c + 512],
            "br": lambda i, c: w_branch[0, i, :, c:c + 512],
            "out": lambda i, c: w_out[0, :, c:c + 512],
        }
        CONV = [u for u, unit in enumerate(UNITS) if unit[0] in ("xbc", "mq", "mk")]
        conv_no = {u: i for i, u in enumerate(CONV)}
        Z0 = FIRST["z"]
        G0 = FIRST["g"]
        BR0 = FIRST["br"]
        OUT0 = FIRST["out"]

        FREED, n = [], {}
        for kind, *_ in UNITS:
            s = {"xbc": conv_sum, "mq": conv_sum, "mk": conv_sum, "z": z_out, "br": u_ready, "out": x1_part}.get(kind, kept)
            n[s.name] = n.get(s.name, 0) + 1
            FREED.append((s, n[s.name]))

        block = ctx.enter_context(nc.Block())

        @block.sync
        def _(sp):
            for t in range(NT):
                sp.dma_start(xs[:, t, :], x[0, t * P:(t + 1) * P, :]).then_inc(x_in, 16)
            sp.wait_ge(par_in, PAR_IN)
            for n, (kind, i, c) in enumerate(BLOCKS):
                if n >= RING:
                    sp.wait_ge(proj, LAST[n - RING] + 1)
                sp.dma_start(ring[:, n % RING, :, :],
                             blk_src[kind](i, c).rearrange("(c p) n -> p c n", p=P)).then_inc(w_in_sem[n % RING], 16)
                if n == UNITS[BR0][1] + RING:
                    sp.wait_ge(proj, BR0 + 1)
                    sp.wait_ge(nrm_y, 16)
                    sp.dma_start(wg_s[0], w_gate[0, 0].rearrange("(p c) n -> p c n", p=P)).then_inc(gu_in[0], 16)
                    sp.dma_start(wu_s[0], w_up[0, 0].rearrange("(p c) n -> p c n", p=P)).then_inc(gu_in[0], 16)
                    sp.dma_start(wd_s[0], w_down[0, 0].rearrange("(c p) n -> p c n", p=P)).then_inc(dn_in[0], 16)
            sp.wait_ge(u_ready, 24)
            sp.dma_start(fw, final_norm_w.rearrange("(a n) -> a n", a=1).to_broadcast([P, D])).then_inc(fw_in, 16)
            assert UNITS[OUT0][1] % RING == 2
            sp.dma_start(wu_s[1], w_up[0, 1].rearrange("(p c) n -> p c n", p=P)).then_inc(gu_in[1], 16)
            sp.wait_ge(proj, NU)
            sp.dma_start(wg_s[1], w_gate[0, 1].rearrange("(p c) n -> p c n", p=P)).then_inc(gu_in[1], 16)
            sp.dma_start(wd_s[1], w_down[0, 1].rearrange("(c p) n -> p c n", p=P)).then_inc(dn_in[1], 16)
            sp.wait_ge(items_ready, 1)
            pairs = sp.value_load(npair[0:1, 0:1], min_val=1, max_val=P // 2 - 1)
            whole = sp.value_load(npair[0:1, 1:2], min_val=0, max_val=P // 2 - 2) + 1

            def load_item(i, j):
                e = sp.value_load(eint[0:1, bass.ds(2 * i + j, 1)], min_val=0, max_val=NE - 1)
                sp.wait_ge(gu_done, 2 * i + (j - 1))
                sp.dma_start(wg_s[j], w_gate[0, bass.ds(e, 1), :, :].rearrange(
                    "a (p c) n -> p (a c) n", p=P)).then_inc(gu_in[j], 16)
                sp.dma_start(wu_s[j], w_up[0, bass.ds(e, 1), :, :].rearrange(
                    "a (p c) n -> p (a c) n", p=P)).then_inc(gu_in[j], 16)
                sp.wait_ge(down_done, 2 * i + (j - 1))
                sp.dma_start(wd_s[j], w_down[0, bass.ds(e, 1), :, :].rearrange(
                    "a (c p) n -> p (a c) n", p=P)).then_inc(dn_in[j], 16)

            with sp.If(whole > 1):
                with sp.Fori(1, whole) as i:
                    for j in range(2):
                        load_item(i, j)
            with sp.If(pairs > whole):
                load_item(whole, 0)
            for t in range(NT):
                sp.wait_ge(fin_out, t + 1)
                sp.dma_start(out[0, t * P:(t + 1) * P, :], xs[:, t, :]).then_inc(out_done, 16)
            sp.wait_ge(out_done, 16 * NT)

        @block.gpsimd
        def _(pool):
            def aff(t, pattern, op, base_, mult, fill, inp=None):
                return pool.affine_select(out=t, in_=t if inp is None else inp, compare_op=op, fill=fill, base=base_,
                                          pattern=pattern, channel_multiplier=mult)
            pool.memset(ident[:, :], 0.0).then_inc(consts, 1)
            pool.memset(tri[:, :], 1.0).then_inc(consts, 1)
            pool.memset(stri[:, :], 1.0).then_inc(consts, 1)
            pool.memset(ones[:, :], 1.0).then_inc(consts, 1)
            pool.memset(mean[:, :], 1.0 / 256).then_inc(consts, 1)
            pool.memset(mask01[:, :], 1.0).then_inc(consts, 1)
            pool.memset(mneg[:, :], 0.0).then_inc(consts, 1)
            pool.memset(eps[:, :], EPS).then_inc(consts, 1)
            pool.memset(halfc[:, :], 3.0).then_inc(consts, 1)
            pool.iota(iota[:, :], [[1, P]], base=0, channel_multiplier=0,
                      allow_small_or_imprecise_dtypes=True).then_inc(consts, 1)
            pool.iota(thr[:, :], [[SLOT, 8]], base=0, channel_multiplier=0,
                      allow_small_or_imprecise_dtypes=True).then_inc(consts, 1)
            pool.iota(pidx[:, :], [[0, 1]], base=-2, channel_multiplier=1,
                      allow_small_or_imprecise_dtypes=True).then_inc(consts, 1)
            pool.iota(place0[:, :], [[0, 1]], base=-SLOT, channel_multiplier=SLOT,
                      allow_small_or_imprecise_dtypes=True).then_inc(consts, 1)
            for q in range(4):
                pool.wait_ge(consts, 13 + q)
                pool.iota(pmod[32 * q:32 * q + 32, :], [[0, 1]], base=0, channel_multiplier=1,
                          allow_small_or_imprecise_dtypes=True).then_inc(consts, 1)
            pool.wait_ge(consts, 17)
            aff(ident[:, :], [[-1, P]], ALU.not_equal, 0, 1, 1.0).then_inc(consts, 1)
            aff(tri[:, :], [[1, P]], ALU.is_ge, 0, -1, 0.0).then_inc(consts, 1)
            aff(stri[:, :], [[1, P]], ALU.is_gt, 0, -1, 0.0).then_inc(consts, 1)
            aff(mask01[:, 0:P], [[1, P]], ALU.is_ge, 0, -1, 0.0).then_inc(consts, 1)
            aff(mask01[:, 256:384], [[1, P]], ALU.is_ge, 0, -1, 0.0).then_inc(consts, 1)
            aff(mneg[:, P:256], [[-1, P]], ALU.is_ge, 0, 1, MASKED).then_inc(consts, 1)
            pool.memset(halfc[:, 1:2], 0.0).then_inc(consts, 1)
            aff(place0[:, :], [[0, 1]], ALU.is_gt, -1, 1, float(T)).then_inc(consts, 1)
            pool.wait_ge(consts, 25)
            aff(place0[:, :], [[0, 1]], ALU.not_equal, 0, 1, 0.0).then_inc(consts, 1)
        @block.tensor
        def _(pe):
            pe.wait_ge(consts, CONSTS)
            pe.wait_ge(par_in, PAR_IN)
            for i, n in enumerate((104, 112)):
                mm = pe.transpose(SC[0][:, 112 * i:112 * i + n], prow[0:n, i, :], ident[0:n, 0:n])
            mm.then_inc(par_turned, 1)
            for t in range(NT):
                pe.wait_ge(x_norm, t + 1)
                for c in range(KC):
                    b = OB[c // 4]
                    if t and c % 4 == 0:
                        pe.wait_ge(h_ready, 8 * (t - 1) + 4 * (c // 4) + 4)
                    pe.transpose(b[:, P * (c % 4):P * (c % 4) + P], hN[:, t, P * c:P * c + P],
                                 ident[:, :]).then_inc(h_turned, 1)
            pe.wait_ge(h_ready, 16)

            def x1_turn(t, half):
                pe.wait_ge(x1_part, 2 * t + half + 1)
                if t:
                    pe.wait_ge(x1_copied, half + 1)
                for c in range(4):
                    mm = pe.transpose(SC[half][:, P * c:P * c + P],
                                      xs[:, t, 512 * half + P * c:512 * half + P * c + P], ident[:, :])
                mm.then_inc(x1_turned, 1)

            def x1_logits(t, half):
                pe.wait_ge(wrt_ready, 1)
                pe.wait_ge(x1_copied, 2 * t + half + 1)
                for c in range(4 * half, 4 * half + 4):
                    mm = pe.matmul((TR, OB[0])[t][:, 0:NR], x1T[:, c, P * t:P * t + P], wrt[:, c, :],
                                   start=(c == 0), stop=(c == KC - 1))
                mm.then_inc(logits, 1)

            def rank(t):
                pe.wait_ge(chosen, t + 1)
                if t == 0:
                    pe.matmul(OB[1][:, 0:NE], stri[:, :], ohm[:, 0, :], start=True, stop=True)
                    pe.matmul(OB[1][:, NE:2 * NE], ones[:, :], ohm[:, 0, :], start=True, stop=True)\
                        .then_inc(ranked, 1)
                else:
                    pe.matmul(OB[1][:, 2 * NE:3 * NE], stri[:, :], ohm[:, 1, :], start=True, stop=True)
                    pe.matmul(OB[1][:, 3 * NE:4 * NE], ones[:, :], ohm[:, 1, :], start=True, stop=True)\
                        .then_inc(ranked, 1)

            router_in = {(OUT0 + 1, 2): [(x1_turn, 0, 0)], (OUT0 + 2, 2): [(x1_turn, 0, 1)],
                         (OUT0 + 2, 4): [(x1_logits, 0, 0), (x1_logits, 0, 1)],
                         (OUT0 + 3, 2): [(rank, 0)], (OUT0 + 3, 4): [(x1_turn, 1, 0)],
                         (OUT0 + 3, 7): [(x1_logits, 1, 0)]}
            for u, (kind, n, part, chunk) in enumerate(UNITS):
                if kind == "br" and chunk % KC == 0:
                    b = chunk // KC
                    pe.wait_ge(*((fox_y, 8), (nrm_y, 8), (nrm_y, 16))[b])
                if kind == "out" and u == OUT0:
                    pe.wait_ge(u_ready, 24)
                pe.wait_ge(w_in_sem[n % RING], 16 * (n // RING + 1))
                if u >= BANKS:
                    pe.wait_ge(*FREED[u - BANKS])
                pj = PJ[u % BANKS]
                w = ring[:, n % RING, :, :]
                for c in range(KC):
                    f, l = c == 0, c == KC - 1
                    if kind in ("av", "mv", "out"):
                        src = zu if kind == "out" else hT
                        mm = pe.matmul(pj[:, :], src[:, c, P * part:P * part + P], w[:, c, :], start=f, stop=l)
                    else:
                        rhs = yT[:, chunk // KC, c, :] if kind == "br" else hT[:, c, :]
                        mm = pe.matmul(pj[:, 0:T], w[:, c, P * part:P * part + P], rhs, start=f, stop=l)
                    if c < KC - 1:
                        for job, *of in router_in.get((u, c), ()):
                            job(*of)
                mm.then_inc(proj, 1)
                for job, *of in router_in.get((u, KC - 1), ()):
                    job(*of)
                for stage, h in FOLLOW[u]:
                    if stage == "gates":
                        for t in range(NT):
                            for c in range(KC):
                                mm = pe.matmul(TR[:, 40 * t:40 * t + 40], hT[:, c, P * t:P * t + P], wsm[:, c, :],
                                               start=(c == 0), stop=(c == KC - 1))
                            mm.then_inc(small_done, 1)
                    elif stage == "sums":
                        pe.wait_ge(small_v, SMALL_GL)
                        pe.matmul(TR[:, 128:164], tri[:, :], gl[:, 0, :], start=True, stop=True)
                        pe.matmul(TR[:, 192:228], ones[:, :], gl[:, 0, :], start=True, stop=False)
                        pe.matmul(TR[:, 192:228], tri[:, :], gl[:, 1, :], start=False, stop=True).then_inc(cum_done, 1)
                    elif stage == "fox_a":
                        s = SC[h % 2]
                        if h == 0:
                            pe.wait_ge(*FREED[FIRST["xbc"] - 1])
                            pe.wait_ge(cum_ready, 4)
                        if h >= 2:
                            pe.wait_ge(fox_masked, 2 * (h - 1))
                        q = slice(64 * (h % 2), 64 * (h % 2) + 64)
                        for lo, qs, nk in ((0, slice(P, T), T), (T, slice(0, P), P)):
                            pe.matmul(s[:, lo:lo + nk], qT[q, h // 2, qs], kT[q, h // 2, 0:nk], start=True, stop=False)
                            for t in range(nk // P):
                                mm = pe.matmul(s[:, lo + P * t:lo + P * t + P],
                                               rn[:, t, h:h + 1].to_broadcast([P, P]), ident[:, :],
                                               start=False, stop=(t == nk // P - 1))
                        mm.then_inc(fox_scores, 1)
                    elif stage == "fox_b":
                        pe.wait_ge(fox_probs, 2 * h + 2)
                        if h:
                            pe.wait_ge(fox_pt, h)
                        p = work[:, 2 + h % 2, :]
                        pe.transpose(TR[:, 0:P], p[:, T:384], ident[:, :])
                        pe.transpose(TR[:, P:T], p[:, 0:P], ident[:, :])
                        pe.transpose(TR[:, T:384], p[:, P:T], ident[:, :]).then_inc(fox_turned, 1)
                    elif stage == "fox_c":
                        pe.wait_ge(fox_pt, h + 1)
                        if h >= 4 and h % 2 == 0:
                            pe.wait_ge(fox_y, h // 2 - 1)
                        o = OB[(h // 2) % 2][64 * (h % 2):64 * (h % 2) + 64, :]
                        pt = work[:, 4 + h % 2, :]
                        pe.matmul(o[:, 0:T], vN[:, 0, 64 * h:64 * h + 64], pt[:, 0:T], start=True, stop=False)
                        pe.matmul(o[:, P:T], vN[:, 1, 64 * h:64 * h + 64], pt[:, T:384],
                                  start=False, stop=True).then_inc(fox_out, 1)
                    elif stage == "ssd_x":
                        if h == 0:
                            pe.wait_ge(fox_pt, 16)
                            pe.wait_ge(fox_y, 8)
                            pe.wait_ge(conv_out, 16)
                        elif h >= 2:
                            pe.wait_ge(ssd_x, h - 1)
                        for t in range(NT):
                            mm = pe.transpose((TR, OB[0])[h % 2][:, P * t:P * t + P],
                                              xbcT[:, h, P * t:P * t + P], ident[:, :])
                        mm.then_inc(ssd_turned, 1)
                    elif stage == "ssd_cb":
                        if h:
                            pe.wait_ge(ssd_cbm, h)
                        pe.matmul(OB[1][:, 0:T], xbcT[:, 8 + h, 0:P], xbcT[:, 12 + h, 0:T], start=True, stop=True)
                        pe.matmul(OB[1][:, T:384], xbcT[:, 8 + h, P:T], xbcT[:, 12 + h, P:T],
                                  start=True, stop=True).then_inc(ssd_cb, 1)
                    elif stage == "ssd_a":
                        s = SC[h % 2]
                        if h >= 2:
                            pe.wait_ge(ssd_seg, 2 * (h - 1))
                        else:
                            pe.wait_ge(fox_masked, 32)
                        for t in range(NT):
                            mm = pe.matmul(s[:, P * t:P * t + P], cum[:, t, 16 + h:17 + h].to_broadcast([P, P]),
                                           ident[:, :], start=True, stop=True)
                        mm.then_inc(ssd_bc, 1)
                    elif stage == "ssd_c":
                        pe.wait_ge(ssd_w, h + 1)
                        pe.wait_ge(ssd_x, h // 2 + 1)
                        if h == 0:
                            pe.wait_ge(ssd_x, 8)
                        elif h == 2:
                            pe.wait_ge(ssd_cbm, 4)
                        elif h % 2 == 0:
                            pe.wait_ge(ssd_y, 2 * (h // 2 - 1))
                        o = OB[(h // 2) % 2][64 * (h % 2):64 * (h % 2) + 64, :]
                        w2 = work[:, 4 + h % 2, :]
                        pe.matmul(o[:, 0:T], xdt[:, 0, 64 * h:64 * h + 64], w2[:, 0:T], start=True, stop=False)
                        pe.matmul(o[:, P:T], xdt[:, 1, 64 * h:64 * h + 64], w2[:, T:384],
                                  start=False, stop=True).then_inc(ssd_out, 1)
                    elif stage in ("ssd_norm", "ml_norm"):
                        k = 0 if stage == "ssd_norm" else 1
                        for g in range(4):
                            pe.wait_ge(nrm_sq, 4 * k + g + 1)
                            if g >= 2 or k:
                                pe.wait_ge(nrm_rt, 4 * k + g - 1)
                            if g < 2:
                                pe.wait_ge(*((ssd_y, 16), (ml_y, 8))[k])
                            o = OB[g % 2]
                            for i in range(2):
                                mm = pe.matmul(o[:, 0:T], mean[:, :], work[:, 6 + 2 * (g % 2) + i, 0:T],
                                               start=(i == 0), stop=(i == 1))
                            mm.then_inc(nrm_ms, 1)
                    elif stage == "ml_a":
                        if h == 0:
                            pe.wait_ge(*FREED[G0 - 1])
                            pe.wait_ge(conv_out, len(CONV))
                            pe.wait_ge(ssd_seg, 32)
                        else:
                            pe.wait_ge(ml_w, ML_W * h)
                        for lo, qs, nk in ((0, slice(P, T), T), (T, slice(0, P), P)):
                            for i in range(2):
                                pe.matmul(SC[0][:, lo:lo + nk], qT[:, 2 * h + i, qs], kT[:, 2 * h + i, 0:nk],
                                          start=(i == 0), stop=(i == 1))
                        for t in range(NT):
                            mm = pe.matmul(SC[1][:, P * t:P * t + P], rn[:, t, 16 + h:17 + h].to_broadcast([P, P]),
                                           ident[:, :], start=True, stop=True)
                        mm.then_inc(ml_scores, 1)
                    elif stage == "ml_b":
                        pe.wait_ge(ml_w, ML_W * (h + 1))
                        if h:
                            pe.wait_ge(ml_pt, h)
                        p = work[:, 2, :]
                        pe.transpose(TR[:, 0:P], p[:, T:384], ident[:, :])
                        pe.transpose(TR[:, P:T], p[:, 0:P], ident[:, :])
                        pe.transpose(TR[:, T:384], p[:, P:T], ident[:, :]).then_inc(ml_turned, 1)
                    elif stage == "ml_c":
                        pe.wait_ge(ml_pt, h + 1)
                        if h == 0:
                            pe.wait_ge(nrm_rt, 4)
                        else:
                            pe.wait_ge(ml_y, 2 * h)
                        pt = work[:, 4, :]
                        for i in range(2):
                            v = slice(256 * h + P * i, 256 * h + P * i + P)
                            pe.matmul(OB[i][:, 0:T], vN[:, 0, v], pt[:, 0:T], start=True, stop=False)
                            pe.matmul(OB[i][:, P:T], vN[:, 1, v], pt[:, T:384],
                                      start=False, stop=True).then_inc(ml_out, 1)

            x1_turn(1, 1)
            x1_logits(1, 1)

            def gather_first(t):
                pe.wait_ge(first_pick, t + 1)
                pe.wait_ge(h2_ready, t + 1)
                for c in range(KC):
                    mm = pe.matmul(GAB[:, 64 * c:64 * c + 64], h2p[:, t, c, :], pick[:, t, :],
                                   start=(t == 0 and c == 0), stop=(t == 1), skip_group_check=True)
                return mm

            def gather(i):
                pe.wait_ge(picked, i)
                for c in range(KC):
                    for t in range(NT):
                        mm = pe.matmul(GAB[:, 64 * c:64 * c + 64], h2p[:, t, c, :], pick[:, t, :],
                                       start=(t == 0), stop=(t == NT - 1))
                mm.then_inc(gathered, 1)

            def start_sums(banks):
                pe.wait_ge(x1_part, 4)
                for n in banks:
                    mm = pe.matmul(ACCB[n], ident[:, :], xs[:, :, T * n:T * n + T], start=True, stop=True)
                return mm

            def gate_up(i, j, chunks=range(KC)):
                for c in chunks:
                    if c == 0:
                        pe.wait_ge(gu_in[j], 32 * i + 32)
                        if j == 0:
                            pe.wait_ge(xg_ready, i + 1)
                    for g in range(4):
                        w = (wg_s[j] if g < 2 else wu_s[j])[:, c, T * (g % 2):T * (g % 2) + T]
                        mm = pe.matmul(GUB[32 * g:32 * g + 32, T * j:T * j + T], xg[:, c, 32 * j:32 * j + 32], w,
                                       start=(c == 0), stop=(c == KC - 1))
                if KC - 1 in chunks:
                    mm.then_inc(gu_done, 1)

            def hidden_turn(i, j):
                pe.wait_ge(gu_copied, 2 * i + (j + 1))
                for k in range(2):
                    mm = pe.transpose(TRB[:, T * j + P * k:T * j + P * k + P], gus[:, j, P * k:P * k + P],
                                      ident[:, :])
                mm.then_inc(hid_turned, 1)

            def down(i, j):
                pe.wait_ge(hid_v, 4 * i + (2 * j + 2))
                pe.wait_ge(dn_in[j], 16 * i + 16)
                dn = DNB[:, T * j:T * j + T]
                for c in range(HC):
                    a = actT[:, j, c % 2, 32 * (c // 2):32 * (c // 2) + 32]
                    for g in range(4):
                        mm = pe.matmul(dn[32 * g:32 * g + 32, :], a, wd_s[j][:, c, T * g:T * g + T],
                                       start=(c == 0), stop=(c == HC - 1))
                mm.then_inc(down_done, 1)

            def combine(i, j):
                pe.wait_ge(y_copied, 2 * i + (j + 1))
                pe.wait_ge(combined, 2 * i + (j + 1))
                for t in range(NT):
                    for g in range(4):
                        r = slice(32 * g, 32 * g + 32)
                        mm = pe.matmul(ACCB[g][:, T * t:T * t + T], comb[r, j, P * t:P * t + P], ysb[r, j, :],
                                       start=False, stop=True, skip_group_check=True)
                mm.then_inc(comb_done, 1)

            gather_first(0)
            rank(1)
            start_sums((0,))
            gather_first(1).then_inc(gathered, 1)
            gate_up(0, 0, range(0, 4))
            pe.wait_ge(item_cols, 1)
            for i in range(2):
                mm = pe.matmul(OB[1][:, 256 + P * i:256 + P * i + P], itc[:, i:i + 1].to_broadcast([P, P]),
                               ident[:, :], start=True, stop=True)
            mm.then_inc(item_rows, 1)
            gate_up(0, 0, range(4, KC))
            hidden_turn(0, 0)
            pe.wait_ge(items_ready, 1)
            down(0, 0)
            gate_up(0, 1)
            for dst, src, done in ((SC[0], pos[:, :].rearrange("p (t k) -> p t k", t=NT), place_rows),
                                   (GAB, wtok, weight_rows)):
                if done is weight_rows:
                    pe.wait_ge(weighed, 1)
                for k in range(2):
                    for t in range(NT):
                        mm = pe.matmul(dst[:, T * k + P * t:T * k + P * t + P],
                                       src[:, t, k:k + 1].to_broadcast([P, P]), ident[:, :], start=True, stop=True)
                mm.then_inc(done, 1)
            start_sums((1, 2))
            pe.wait_ge(rows_copied, 1)
            start_sums((3,)).then_inc(comb_done, 1)
            pe.wait_ge(rows_copied, 2)
            gather(1)
            combine(0, 0)
            hidden_turn(0, 1)
            down(0, 1)
            combine(0, 1)

            def item(i, j):
                gate_up(i, j)
                if j == 0:
                    gather(i + 1)
                hidden_turn(i, j)
                down(i, j)
                combine(i, j)

            pairs = pe.value_load(npair[0:1, 0:1], min_val=1, max_val=P // 2 - 1)
            whole = pe.value_load(npair[0:1, 1:2], min_val=0, max_val=P // 2 - 2) + 1
            with pe.If(whole > 1):
                with pe.Fori(1, whole) as i:
                    item(i, 0)
                    item(i, 1)
            with pe.If(pairs > whole):
                gate_up(whole, 0)
                hidden_turn(whole, 0)
                down(whole, 0)
                combine(whole, 0)

        @block.scalar
        def _(act):
            rows = ((0, 0, norm1_w[0], KC), (0, 8, ssd_conv_w[0].rearrange("k n -> (k n)"), 64),
                    (0, 72, ssd_conv_b[0], 16), (0, 88, ssd_norm_w[0], 8), (0, 96, ml_norm_w[0], 8),
                    (1, 0, ml_conv_w[0].rearrange("k n -> (k n)"), 64), (1, 64, ml_conv_b[0], 16),
                    (1, 80, gate_bias[0], 24))
            for i, r, src, n in rows:
                act.dma_start(prow[r:r + n, i, :], src.rearrange("(r p) -> r p", p=P)).then_inc(par_in, 16)
            act.dma_start(prow[104:112, 1, :], norm2_w[0].rearrange("(r p) -> r p", p=P)).then_inc(par_in, 16)
            act.dma_start(n2[:, :], norm2_w[0].rearrange("(p c) -> p c", p=P)).then_inc(par_in, 16)
            col = 0
            for name, n, bias in (("af", 16, att_f_bias), ("dt", 16, ssd_dt_bias), ("mi", 4, ml_i_bias),
                                  ("mf", 4, ml_f_bias)):
                act.dma_start(wsm[:, :, col:col + n],
                              lay[:, COL[name]:COL[name] + n].rearrange("(c p) n -> p c n", p=P)).then_inc(par_in, 16)
                act.dma_start(bsm[:, col:col + n], bias[0:1, :].to_broadcast([P, n])).then_inc(par_in, 16)
                col += n
            act.dma_start(alog[:, :], ssd_a_log[0:1, :].to_broadcast([P, 16])).then_inc(par_in, 16)
            for i in range(2):
                with nc.allow_non_contiguous_dma("eight values"):
                    act.dma_start(dsk[64 * i:64 * i + 64, :],
                                  ssd_d[0:1, :].rearrange("a (c two) -> a c two", two=2)[:, :, i]
                                  .to_broadcast([64, KC])).then_inc(par_in, 16)
            act.wait_ge(consts, CONSTS)
            for t in range(NT):
                act.wait_ge(x_sq, t + 1)
                act.activation(ss[:, 2 + t:3 + t], ss[:, t:t + 1], ACT.Sqrt, bias=eps[:, :], scale=1.0 / D)\
                    .then_inc(astep, 1)
            with nc.allow_non_contiguous_dma("router weights"):
                act.dma_start(wrt[:, :, 0:NG], w_group[0].rearrange("(c p) n -> p c n", p=P)).then_inc(rt_in, 16)
                act.dma_start(wrt[:, :, NG:NR], w_expert_router[0].rearrange("(c p) n -> p c n", p=P))\
                    .then_inc(rt_in, 16)
            act.dma_start(brow[:, 0:NG], b_group[0:1, :].to_broadcast([P, NG])).then_inc(rt_in, 16)
            act.dma_start(brow[:, NG:NR], b_expert_router[0:1, :].to_broadcast([P, NE])).then_inc(rt_in, 16)
            act.wait_ge(par_ready, 3)

            def tanh_of(u):
                i = conv_no[u]
                act.wait_ge(conv_sum, i + 1)
                if i >= 3:
                    act.wait_ge(conv_out, i - 2)
                act.activation(thb[:, i % 3, :], acc[:, i % 3, :], ACT.Tanh).then_inc(conv_tanh, 1)

            for u, (kind, n, part, chunk) in enumerate(UNITS):
                pj = PJ[u % BANKS]
                if kind in ("aq", "ak", "av", "mv", "mo", "z", "g", "xbc", "mq", "mk"):
                    act.wait_ge(proj, u + 1)
                if kind == "aq":
                    act.activation(qT[:, chunk, :], pj[:, 0:T], ACT.Copy, scale=64 ** -0.5).then_inc(kept, 1)
                elif kind == "ak":
                    act.activation(kT[:, chunk, :], pj[:, 0:T], ACT.Copy).then_inc(kept, 1)
                elif kind in ("av", "mv"):
                    act.activation(vN[:, part, 512 * chunk:512 * chunk + 512], pj[:, :], ACT.Copy).then_inc(kept, 1)
                elif kind == "mo":
                    act.activation(moT[:, chunk, :], pj[:, 0:T], ACT.Tanh, scale=0.5).then_inc(kept, 1)
                elif kind == "z":
                    i = u - Z0
                    if i >= 2:
                        act.wait_ge(z_out, i - 1)
                    act.activation(work[:, 8 + i % 2, 0:T], pj[:, 0:T], ACT.Tanh, scale=0.5).then_inc(z_tanh, 1)
                elif kind == "g":
                    if u == G0:
                        act.wait_ge(ssd_y, 16)
                    act.activation(gT[:, chunk, :], pj[:, 0:T], ACT.Tanh, bias=pc[:, 1, 80 + chunk:81 + chunk],
                                   scale=0.5).then_inc(kept, 1)
                elif u in conv_no:
                    i = conv_no[u]
                    w0, b0, wi, ch = (8, 72, 0, chunk) if kind == "xbc" else (0, 64, 1, chunk + (8 if kind == "mk" else 0))
                    if i >= 3:
                        act.wait_ge(conv_out, i - 2)
                    act.activation(acc[:, i % 3, :], pj[:, 0:T], ACT.Identity, bias=pc[:, wi, b0 + ch:b0 + ch + 1],
                                   scale=pc[:, wi, w0 + 48 + ch:w0 + 49 + ch]).then_inc(conv_pre, 1)
                if u and u - 1 in conv_no:
                    tanh_of(u - 1)
                for stage, h in FOLLOW[u]:
                    if stage == "gates":
                        act.wait_ge(small_v, 2)
                        act.activation(smw[:, 1, :, :], smw[:, 0, :, :], ACT.Exp, scale=-1.0).then_inc(small_a, 1)
                        act.activation(alog[:, :], alog[:, :], ACT.Exp).then_inc(small_a, 1)
                        act.wait_ge(small_v, 3)
                        act.activation(smw[:, 3, :, :], smw[:, 2, :, :], ACT.Ln).then_inc(small_a, 1)
                    elif stage == "fox_a":
                        act.wait_ge(fox_negmax, h + 1)
                        if h >= 2:
                            act.wait_ge(fox_turned, h - 1)
                        b = h % 2
                        act.activation(work[:, 2 + b, 0:T], work[:, b, 0:T], ACT.Exp, bias=nmx[:, b, 1:2],
                                       accum_out=rsum[:, b, 1:2]).then_inc(fox_exp, 1)
                        act.activation(work[:, 2 + b, T:384], work[:, b, T:384], ACT.Exp, bias=nmx[:, b, 0:1],
                                       accum_out=rsum[:, b, 0:1]).then_inc(fox_exp, 1)
                    elif stage == "fox_b":
                        act.wait_ge(fox_turned, h + 1)
                        if h >= 2:
                            act.wait_ge(fox_out, h - 1)
                        act.activation(work[:, 4 + h % 2, :], TR[:, 0:384], ACT.Copy).then_inc(fox_pt, 1)
                    elif stage == "ssd_a":
                        act.wait_ge(ssd_seg, 2 * h + 2)
                        if h >= 2:
                            act.wait_ge(ssd_w, h - 1)
                        act.activation(work[:, 2 + h % 2, :], work[:, h % 2, :], ACT.Exp).then_inc(ssd_exp, 1)
                    elif stage in ("ssd_norm", "ml_norm"):
                        k = 0 if stage == "ssd_norm" else 1
                        if k == 0:
                            act.wait_ge(ssd_y, 16)
                            act.wait_ge(z_out, 8)
                        else:
                            act.wait_ge(ml_y, 8)
                        for g in range(5):
                            if g < 4:
                                if g >= 2:
                                    act.wait_ge(nrm_ms, 4 * k + g - 1)
                                act.activation(work[:, 6 + 2 * (g % 2):8 + 2 * (g % 2), 0:T],
                                               yT[:, 1 + k, 2 * g:2 * g + 2, :], ACT.Square).then_inc(nrm_sq, 1)
                            if g:
                                act.wait_ge(nrm_ms, 4 * k + g)
                                q = g - 1
                                if q >= 2 or k:
                                    act.wait_ge(nrm_y, 8 * k + 2 * (q - 1) if q >= 2 else 8)
                                act.activation(tmpu[:, q % 2, :], OB[q % 2][:, 0:T], ACT.Sqrt, bias=eps[:, :])\
                                    .then_inc(nrm_rt, 1)
                    elif stage == "ml_a":
                        act.wait_ge(ml_neg, ML_NEG * (h + 1))
                        act.activation(work[:, 1, 0:T], work[:, 0, 0:T], ACT.Exp, bias=mls[:, 1, 1:2]).then_inc(ml_exp, 1)
                        act.activation(work[:, 1, T:384], work[:, 0, T:384], ACT.Exp, bias=mls[:, 1, 0:1])\
                            .then_inc(ml_exp, 1)
                        act.activation(mls[:, 3, :], mls[:, 2, :], ACT.Exp).then_inc(ml_exp, 1)
                    elif stage == "ml_b":
                        act.wait_ge(ml_turned, h + 1)
                        if h:
                            act.wait_ge(ml_out, 2 * h)
                        act.activation(work[:, 4, :], TR[:, 0:384], ACT.Copy).then_inc(ml_pt, 1)

            for t in range(NT):
                for half in range(2):
                    act.wait_ge(x1_part, 2 * t + half + 1)
                    if t or half:
                        act.wait_ge(x1_sq, 2 * t + half)
                    act.activation(sqj, xs[:, t, 512 * half:512 * half + 512], ACT.Square,
                                   accum_out=rt[:, 8 + half, t:t + 1]).then_inc(x1_sq, 1)
                act.wait_ge(x1_sum, t + 1)
                act.activation(ss[:, 2 + t:3 + t], ss[:, t:t + 1], ACT.Sqrt, bias=eps[:, :], scale=1.0 / D)\
                    .then_inc(x1_root, 1)
                act.wait_ge(x1_rstd, t + 1)
                act.activation(h2p[:, t, :, :], xs[:, t, :].rearrange("q (p c) -> q c p", c=KC), ACT.Copy,
                               scale=ss[:, 4 + t:5 + t]).then_inc(h2_ready, 1)
            act.wait_ge(grp_sub, 1)
            act.activation(pe8[:, :, :], pe8[:, :, :], ACT.Exp).then_inc(grp_exp, 1)
            act.activation(rt[:, 4, :], rt[:, 3, :], ACT.Exp).then_inc(grp_exp, 1)

            def item(i, j):
                act.wait_ge(gu_done, 2 * i + (j + 1))
                act.activation(gus[:, j, :], GUB[:, T * j:T * j + T], ACT.Copy).then_inc(gu_copied, 1)
                act.wait_ge(hid_turned, 2 * i + (j + 1))
                act.activation(tht[:, j, :, :], TRB[:, T * j:T * j + T].rearrange("p (i s) -> p i s", i=2)[:, :, 0:64],
                               ACT.Tanh, scale=0.5).then_inc(hid_tanh, 1)
                act.wait_ge(down_done, 2 * i + (j + 1))
                act.activation(ysb[:, j, :], DNB[:, T * j:T * j + T], ACT.Copy).then_inc(y_copied, 1)

            item(0, 0)
            act.wait_ge(place_rows, 1)
            act.activation(posb, SC[0][:, :], ACT.Copy).then_inc(rows_copied, 1)
            act.wait_ge(weight_rows, 1)
            act.activation(wb, GAB[:, :], ACT.Copy).then_inc(rows_copied, 1)
            item(0, 1)
            act.wait_ge(items_ready, 1)
            pairs = act.value_load(npair[0:1, 0:1], min_val=1, max_val=P // 2 - 1)
            whole = act.value_load(npair[0:1, 1:2], min_val=0, max_val=P // 2 - 2) + 1
            with act.If(whole > 1):
                with act.Fori(1, whole) as i:
                    item(i, 0)
                    item(i, 1)
            with act.If(pairs > whole):
                item(whole, 0)

            act.wait_ge(comb_done, pairs + whole + 1)
            for t in range(NT):
                act.activation(bigt.rearrange("p (b n) -> p b n", b=4), acc4[:, :, T * t:T * t + T], ACT.Square,
                               accum_out=ss[:, t:t + 1]).then_inc(fin_sq, 1)
                act.wait_ge(fin_sq, t + 1)
            act.activation(ss[:, 2:4], ss[:, 0:2], ACT.Sqrt, bias=eps[:, :], scale=1.0 / D).then_inc(fin_root, 1)

        @block.vector
        def _(dve):
            steps = 0

            def step(ins):
                nonlocal steps
                steps += 1
                ins.then_inc(dstep, 1)
                dve.wait_ge(dstep, steps)

            def recip_rms(t):
                step(dve.reciprocal(ss[:, 4 + t:5 + t], ss[:, 2 + t:3 + t]))

            for t in range(NT):
                dve.wait_ge(x_in, 32)
                dve.tensor_tensor_reduce(bigt, xs[:, t, :], xs[:, t, :], 1.0, 0.0, ALU.mult, ALU.add,
                                         ss[:, t:t + 1]).then_inc(x_sq, 1)
                dve.wait_ge(x_sq, t + 1)
            dve.wait_ge(par_turned, 1)
            dve.tensor_copy(pc[:, 0, 0:104], SC[0][:, 0:104]).then_inc(par_ready, 1)
            dve.tensor_scalar(pc[:, 1, 0:104], SC[0][:, 112:216], 0.5, None, ALU.mult).then_inc(par_ready, 1)
            dve.wait_ge(par_ready, 2)
            dve.tensor_scalar(pc[:, 0, 8:88], pc[:, 0, 8:88], 0.5, None, ALU.mult).then_inc(par_ready, 1)
            dve.wait_ge(par_ready, 3)
            step(dve.tensor_copy(pc[:, 1, 104:112], SC[0][:, 216:224]))
            step(dve.tensor_scalar(pc[:, 0, 96:104], pc[:, 0, 96:104], 0.5, None, ALU.mult))
            for t in range(NT):
                dve.wait_ge(astep, t + 1)
                recip_rms(t)
                dve.tensor_scalar(hN[:, t, :], xs[:, t, :], ss[:, 4 + t:5 + t], None, ALU.mult).then_inc(x_norm, 1)
            for t in range(NT):
                for c in range(KC):
                    dve.wait_ge(h_turned, 8 * t + 4 * (c // 4) + 4)
                    dve.tensor_scalar(hT[:, c, P * t:P * t + P], OB[c // 4][:, P * (c % 4):P * (c % 4) + P],
                                      pc[:, 0, c:c + 1], None, ALU.mult).then_inc(h_ready, 1)
            def silu_of(u):
                i = conv_no[u]
                kind, n, part, chunk = UNITS[u]
                dve.wait_ge(conv_tanh, i + 1)
                dst = {"xbc": xbcT, "mq": qT, "mk": kT}[kind]
                dve.scalar_tensor_tensor(dst[:, chunk, :], thb[:, i % 3, :], 1.0, acc[:, i % 3, :], ALU.add, ALU.mult)\
                    .then_inc(conv_out, 1)

            def ssd_weights(h):
                b = h % 2
                dve.wait_ge(ssd_exp, h + 1)
                dve.wait_ge(ssd_cbm, h // 4 + 1)
                if h >= 2:
                    dve.wait_ge(ssd_out, h - 1)
                dve.tensor_tensor(work[:, 4 + b, :], work[:, 2 + b, :], cbm[:, h // 4, :], ALU.mult).then_inc(ssd_w, 1)

            rv = 0

            def route(ins):
                nonlocal rv
                rv += 1
                ins.then_inc(r_v, 1)
                dve.wait_ge(r_v, rv)

            def x1_copy(t, half):
                dve.wait_ge(x1_turned, 2 * t + half + 1)
                dve.tensor_copy(x1T[:, 4 * half:4 * half + 4, P * t:P * t + P],
                                SC[half][:, :].rearrange("p (c t) -> p c t", c=4)).then_inc(x1_copied, 1)

            def x1_norm(t):
                dve.wait_ge(x1_sq, 2 * t + 2)
                dve.tensor_tensor(ss[:, t:t + 1], rt[:, 8, t:t + 1], rt[:, 9, t:t + 1], ALU.add).then_inc(x1_sum, 1)
                dve.wait_ge(x1_root, t + 1)
                dve.reciprocal(ss[:, 4 + t:5 + t], ss[:, 2 + t:3 + t]).then_inc(x1_rstd, 1)
                dve.wait_ge(x1_rstd, t + 1)

            def choose(t):
                dve.wait_ge(logits, 2 * t + 2)
                route(dve.scalar_tensor_tensor(lg[:, t, :], (TR, OB[0])[t][:, 0:NR], ss[:, 4 + t:5 + t], brow[:, :],
                                               ALU.mult, ALU.add))
                route(dve.max(top[:, t, :], lg[:, t, 0:NG]))
                route(dve.max_index(topi[:, t, :], top[:, t, :], lg[:, t, 0:NG]))
                route(dve.tensor_copy(rt[:, 0, t:t + 1], topi[:, t, 0:1]))
                route(dve.tensor_tensor(ohg[:, t, :], iota[:, 0:NG], rt[:, 0, t:t + 1].to_broadcast([P, NG]),
                                        ALU.is_equal))
                route(dve.tensor_tensor(egs[:, t, :, :], lg[:, t, NG:NR].rearrange("p (g e) -> p e g", g=NG),
                                        ohg[:, t, None, :].to_broadcast([P, EG, NG]), ALU.mult))
                route(dve.tensor_reduce(ein[:, t, :], egs[:, t, :, :], AX_X, ALU.add))
                route(dve.max(tope[:, t, :], ein[:, t, :]))
                route(dve.max_index(topi[:, t, :], tope[:, t, :], ein[:, t, :]))
                route(dve.tensor_copy(eid[:, t, :], topi[:, t, 0:2]))
                route(dve.scalar_tensor_tensor(eid[:, t, :], rt[:, 0, t:t + 1].to_broadcast([P, 2]), float(EG),
                                               eid[:, t, :], ALU.mult, ALU.add))
                route(dve.tensor_tensor(ohe[:, 2 * t:2 * t + 2, :], iota[:, None, 0:NE].to_broadcast([P, 2, NE]),
                                        eid[:, t, :, None].to_broadcast([P, 2, NE]), ALU.is_equal))
                dve.tensor_tensor(ohm[:, t, :], ohe[:, 2 * t, :], ohe[:, 2 * t + 1, :], ALU.add).then_inc(chosen, 1)

            def place(t):
                dve.wait_ge(ranked, t + 1)
                before = OB[1][:, 2 * NE * t:2 * NE * t + NE]
                if t == 0:
                    route(dve.tensor_copy(tally[:, :], OB[1][:, NE:2 * NE]))
                else:
                    route(dve.tensor_tensor(rke[:, 0, :], tally[:, :], before, ALU.add))
                    before = rke[:, 0, :]
                route(dve.tensor_tensor(rke[:, 2 * t:2 * t + 2, :], ohe[:, 2 * t:2 * t + 2, :],
                                        before[:, None, :].to_broadcast([P, 2, NE]), ALU.mult))
                route(dve.tensor_reduce(rank[:, 2 * t:2 * t + 2], rke[:, 2 * t:2 * t + 2, :], AX_X, ALU.add))
                dve.scalar_tensor_tensor(pos[:, 2 * t:2 * t + 2], eid[:, t, :], float(T), rank[:, 2 * t:2 * t + 2],
                                         ALU.mult, ALU.add).then_inc(placed, 1)
                dve.wait_ge(placed, t + 1)
                route(dve.tensor_scalar(pick[:, t, :], tgt, pos[:, 2 * t:2 * t + 1], None, ALU.is_equal))
                dve.scalar_tensor_tensor(pick[:, t, :], tgt, pos[:, 2 * t + 1:2 * t + 2], pick[:, t, :], ALU.is_equal,
                                         ALU.add).then_inc(first_pick, 1)

            router_after = {OUT0: [(x1_copy, 0, 0)],
                            OUT0 + 1: [(x1_norm, 0), (x1_copy, 0, 1), (choose, 0)],
                            OUT0 + 2: [(x1_copy, 1, 0), (place, 0)],
                            OUT0 + 3: [(x1_copy, 1, 1), (x1_norm, 1), (choose, 1), (place, 1)]}

            for u, (kind, n, part, chunk) in enumerate(UNITS):
                pj = PJ[u % BANKS]
                if u == OUT0:
                    route(dve.tensor_copy(first_blk, thr[:, None, :].to_broadcast([P, NE, 8])))
                    route(dve.memset(first_blk[:, 0:2, 0:1], 1e9))
                    route(dve.memset(gcst, float(T)))
                    route(dve.memset(gcst[:, 1:2], float(T - SLOT)))
                    for j in range(2):
                        route(dve.tensor_scalar(tgt[:, SLOT * j:SLOT * j + SLOT], iota[:, 0:SLOT], float(T * j), None,
                                                ALU.add))
                    dve.wait_ge(rt_in, 64)
                    dve.tensor_tensor(wrt[:, :, :], wrt[:, :, :], pc[:, 1, 104:112, None].to_broadcast([P, KC, NR]),
                                      ALU.mult).then_inc(wrt_ready, 1)
                if u in conv_no:
                    i = conv_no[u]
                    wi, w0, ch = (0, 8, chunk) if kind == "xbc" else (1, 0, chunk + (8 if kind == "mk" else 0))
                    dve.wait_ge(conv_pre, i + 1)
                    a = acc[:, i % 3, :]
                    for back in (1, 2, 3):
                        k = w0 + 16 * (3 - back) + ch
                        ins = dve.scalar_tensor_tensor(a[:, back:T], pj[:, 0:T - back], pc[:, wi, k:k + 1], a[:, back:T],
                                                       ALU.mult, ALU.add)
                        if back < 3:
                            step(ins)
                    ins.then_inc(conv_sum, 1)
                elif kind == "z":
                    i = u - Z0
                    dve.wait_ge(z_tanh, i + 1)
                    dve.scalar_tensor_tensor(zu[:, chunk, :], work[:, 8 + i % 2, 0:T], 1.0, pj[:, 0:T], ALU.add, ALU.mult)\
                        .then_inc(z_out, 1)
                elif kind == "br":
                    b, oc = divmod(chunk, KC)
                    dve.wait_ge(proj, u + 1)
                    if u == BR0:
                        dve.wait_ge(nrm_y, 8)
                    gate = gT[:, chunk, :]
                    if b == 0:
                        dve.scalar_tensor_tensor(zu[:, oc, :], gate, 1.0, pj[:, 0:T], ALU.add, ALU.mult)\
                            .then_inc(u_ready, 1)
                    else:
                        dve.wait_ge(u_ready, u - BR0 - 1)
                        step(dve.scalar_tensor_tensor(tmpu[:, u % 2, :], gate, 1.0, pj[:, 0:T], ALU.add, ALU.mult))
                        dve.tensor_tensor(zu[:, oc, :], zu[:, oc, :], tmpu[:, u % 2, :], ALU.add).then_inc(u_ready, 1)
                elif kind == "out":
                    dve.wait_ge(proj, u + 1)
                    xo = xs[:, part, 512 * chunk:512 * chunk + 512]
                    dve.scalar_tensor_tensor(xo, pj[:, :], 0.5, xo, ALU.mult, ALU.add).then_inc(x1_part, 1)
                    dve.wait_ge(x1_part, u - OUT0 + 1)
                for job, *of in router_after.get(u, ()):
                    job(*of)
                if u and u - 1 in conv_no:
                    silu_of(u - 1)
                for stage, h in FOLLOW[u]:
                    if stage == "gates":
                        dve.wait_ge(small_done, 2)
                        dve.tensor_tensor(sm[:, :, :], TR[:, 0:80].rearrange("p (t n) -> p t n", t=NT),
                                          bsm[:, None, :].to_broadcast([P, NT, 40]), ALU.add).then_inc(small_v, 1)
                        dve.wait_ge(small_v, 1)
                        dve.scalar_tensor_tensor(smw[:, 0, :, :], sm[:, :, :], -1.0, sm[:, :, :], ALU.mult, ALU.max)\
                            .then_inc(small_v, 1)
                        dve.wait_ge(small_a, 1)
                        dve.tensor_scalar(smw[:, 2, :, :], smw[:, 1, :, :], 1.0, None, ALU.add).then_inc(small_v, 1)
                        dve.wait_ge(small_v, 3)
                        step(dve.scalar_tensor_tensor(smw[:, 4, :, :], smw[:, 2, :, :], -1.0, smw[:, 1, :, :], ALU.add, ALU.subtract))
                        dve.wait_ge(small_a, 3)
                        step(dve.tensor_tensor(smw[:, 5, :, :], smw[:, 3, :, :], smw[:, 4, :, :], ALU.subtract))
                        softplus = smw[:, 5, :, :]
                        step(dve.scalar_tensor_tensor(dtt[:, :, :], sm[:, :, 16:32], 0.0, softplus[:, :, 16:32], ALU.max, ALU.add))
                        step(dve.scalar_tensor_tensor(gl[:, :, 0:16], sm[:, :, 0:16], 0.0, softplus[:, :, 0:16],
                                                      ALU.min, ALU.subtract))
                        step(dve.scalar_tensor_tensor(gl[:, :, 32:36], sm[:, :, 36:40], 0.0, softplus[:, :, 36:40],
                                                      ALU.min, ALU.subtract))
                        dve.scalar_tensor_tensor(gl[:, :, 16:32], dtt[:, :, :], -1.0, alog[:, None, :].to_broadcast([P, NT, 16]),
                                                 ALU.mult, ALU.mult).then_inc(small_v, 1)
                    elif stage == "sums":
                        dve.wait_ge(cum_done, 1)
                        for t in range(NT):
                            dve.tensor_copy(cum[:, t, :], TR[:, 128 + 64 * t:164 + 64 * t]).then_inc(cum_ready, 1)
                        dve.wait_ge(cum_ready, 2)
                        dve.tensor_scalar(rn[:, :, 0:16], cum[:, :, 0:16], -1.0, None, ALU.mult).then_inc(cum_ready, 1)
                        dve.tensor_tensor(rn[:, :, 16:20], sm[:, :, 32:36], cum[:, :, 32:36], ALU.subtract).then_inc(cum_ready, 1)
                    elif stage == "fox_a":
                        b = h % 2
                        dve.wait_ge(fox_scores, h + 1)
                        if h >= 2:
                            dve.wait_ge(fox_exp, 2 * (h - 1))
                        dve.tensor_tensor_reduce(work[:, b, 0:T], SC[b][:, 0:T], mneg[:, :], 1.0, -3e38,
                                                 ALU.add, ALU.max, mx[:, b, 1:2]).then_inc(fox_masked, 1)
                        dve.tensor_tensor_reduce(work[:, b, T:384], SC[b][:, T:384], mneg[:, P:T], 1.0, -3e38,
                                                 ALU.add, ALU.max, mx[:, b, 0:1]).then_inc(fox_masked, 1)
                        dve.wait_ge(fox_masked, 2 * h + 2)
                        dve.tensor_scalar(nmx[:, b, :], mx[:, b, :], -1.0, None, ALU.mult).then_inc(fox_negmax, 1)
                    elif stage == "fox_p":
                        b = h % 2
                        dve.wait_ge(fox_exp, 2 * h + 2)
                        step(dve.reciprocal(rinv[:, b, :], rsum[:, b, :]))
                        p = work[:, 2 + b, :]
                        dve.tensor_scalar(p[:, 0:T], p[:, 0:T], rinv[:, b, 1:2], None, ALU.mult).then_inc(fox_probs, 1)
                        dve.tensor_scalar(p[:, T:384], p[:, T:384], rinv[:, b, 0:1], None, ALU.mult)\
                            .then_inc(fox_probs, 1)
                    elif stage == "fox_c" and h % 2:
                        dve.wait_ge(fox_out, h + 1)
                        dve.tensor_copy(yT[:, 0, h // 2, :], OB[(h // 2) % 2][:, 0:T]).then_inc(fox_y, 1)
                    elif stage == "ssd_x":
                        dve.wait_ge(ssd_turned, h + 1)
                        dve.tensor_tensor(
                            xdt[:, :, P * h:P * h + P].rearrange("p t (a d) -> p t a d", a=2),
                            (TR, OB[0])[h % 2][:, 0:T].rearrange("p (t a d) -> p t a d", t=NT, a=2),
                            dtt[:, :, 2 * h:2 * h + 2, None].to_broadcast([P, NT, 2, 64]), ALU.mult).then_inc(ssd_x, 1)
                    elif stage == "ssd_cb":
                        dve.wait_ge(ssd_cb, h + 1)
                        dve.tensor_tensor(cbm[:, h, :], OB[1][:, 0:384], mask01[:, :], ALU.mult).then_inc(ssd_cbm, 1)
                    elif stage == "ssd_a":
                        b = h % 2
                        dve.wait_ge(ssd_bc, h + 1)
                        if h >= 2:
                            dve.wait_ge(ssd_exp, h - 1)
                        dve.tensor_scalar(work[:, b, 0:T], SC[b][:, 0:T], cum[:, 0, 16 + h:17 + h], 0.0,
                                          ALU.subtract, ALU.min).then_inc(ssd_seg, 1)
                        dve.tensor_scalar(work[:, b, T:384], SC[b][:, P:T], cum[:, 1, 16 + h:17 + h], 0.0,
                                          ALU.subtract, ALU.min).then_inc(ssd_seg, 1)
                        if h:
                            ssd_weights(h - 1)
                        if h == 15:
                            ssd_weights(15)
                    elif stage == "ssd_c" and h % 2:
                        c = h // 2
                        dve.wait_ge(ssd_out, h + 1)
                        dve.wait_ge(conv_out, 16)
                        dve.wait_ge(z_out, 8)
                        dve.scalar_tensor_tensor(yT[:, 1, c, :], xbcT[:, c, :], dsk[:, c:c + 1],
                                                 OB[c % 2][:, 0:T], ALU.mult, ALU.add).then_inc(ssd_y, 1)
                        dve.wait_ge(ssd_y, 2 * c + 1)
                        dve.scalar_tensor_tensor(yT[:, 1, c, :], yT[:, 1, c, :], 0.5, zu[:, c, :], ALU.mult, ALU.mult)\
                            .then_inc(ssd_y, 1)
                    elif stage in ("ssd_norm", "ml_norm"):
                        k = 0 if stage == "ssd_norm" else 1
                        for g in range(4):
                            dve.wait_ge(nrm_rt, 4 * k + g + 1)
                            step(dve.reciprocal(tmpu[:, g % 2, :], tmpu[:, g % 2, :]))
                            for c in (2 * g, 2 * g + 1):
                                wcol = pc[:, 0, (88 if k == 0 else 96) + c:(89 if k == 0 else 97) + c]
                                y = yT[:, 1 + k, c, :]
                                if k == 0:
                                    dve.scalar_tensor_tensor(y, y, wcol, tmpu[:, g % 2, :], ALU.mult, ALU.mult)\
                                        .then_inc(nrm_y, 1)
                                else:
                                    step(dve.scalar_tensor_tensor(y, y, wcol, tmpu[:, g % 2, :], ALU.mult, ALU.mult))
                                    dve.scalar_tensor_tensor(y, moT[:, c, :], 1.0, y, ALU.add, ALU.mult)\
                                        .then_inc(nrm_y, 1)
                    elif stage == "ml_a":
                        dve.wait_ge(ml_scores, h + 1)
                        if h == 0:
                            dve.wait_ge(ssd_exp, 16)
                        dve.tensor_tensor_reduce(work[:, 0, 0:T], SC[1][:, 0:T], mneg[:, :], 1.0, -3e38,
                                                 ALU.add, ALU.max, mls[:, 0, 1:2]).then_inc(ml_neg, 1)
                        dve.tensor_tensor_reduce(work[:, 0, T:384], SC[1][:, 0:P], mneg[:, P:T], 1.0, -3e38,
                                                 ALU.add, ALU.max, mls[:, 0, 0:1]).then_inc(ml_neg, 1)
                        dve.wait_ge(ml_neg, ML_NEG * h + 2)
                        dve.tensor_scalar(mls[:, 1, :], mls[:, 0, :], 0.0, -1.0, ALU.max, ALU.mult).then_inc(ml_neg, 1)
                        dve.wait_ge(ml_neg, ML_NEG * h + 3)
                        dve.tensor_tensor(mls[:, 2, :], mls[:, 1, :], cum[:, :, 32 + h], ALU.subtract).then_inc(ml_neg, 1)
                    elif stage == "ml_b":
                        w = work[:, 2, :]
                        b0 = ML_W * h
                        if h:
                            dve.wait_ge(ml_turned, h)
                        dve.wait_ge(ml_exp, 3 * h + 3)
                        dve.tensor_tensor_reduce(w[:, 0:T], work[:, 1, 0:T], SC[0][:, 0:T], 256 ** -0.5, 0.0,
                                                 ALU.mult, ALU.add, mls[:, 4, 1:2]).then_inc(ml_w, 1)
                        dve.tensor_tensor_reduce(w[:, T:384], work[:, 1, T:384], SC[0][:, T:384], 256 ** -0.5, 0.0,
                                                 ALU.mult, ALU.add, mls[:, 4, 0:1]).then_inc(ml_w, 1)
                        dve.wait_ge(ml_w, b0 + 2)
                        step(dve.scalar_tensor_tensor(mls[:, 5, :], mls[:, 4, :], -1.0, mls[:, 4, :], ALU.mult, ALU.max))
                        step(dve.tensor_tensor(mls[:, 5, :], mls[:, 5, :], mls[:, 3, :], ALU.max))
                        step(dve.reciprocal(mls[:, 5, :], mls[:, 5, :]))
                        dve.tensor_scalar(w[:, 0:T], w[:, 0:T], mls[:, 5, 1:2], None, ALU.mult).then_inc(ml_w, 1)
                        dve.tensor_scalar(w[:, T:384], w[:, T:384], mls[:, 5, 0:1], None, ALU.mult).then_inc(ml_w, 1)
                    elif stage == "ml_c":
                        for i in range(2):
                            dve.wait_ge(ml_out, 2 * h + i + 1)
                            dve.tensor_copy(yT[:, 2, 2 * h + i, :], OB[i][:, 0:T]).then_inc(ml_y, 1)

            route(dve.tensor_tensor(tally[:, :], tally[:, :], OB[1][:, 3 * NE:4 * NE], ALU.add))
            route(dve.tensor_tensor(cnt8[:, :, :], tally[:, :, None].to_broadcast([P, NE, 8]), first_blk, ALU.is_gt))
            route(dve.tensor_reduce(nbk[:, 0, :], cnt8[:, :, :], AX_X, ALU.add))
            route(dve.tensor_tensor_scan(nbk[:, 1, :], ones[:, 0:NE], nbk[:, 0, :], 0.0, ALU.mult, ALU.add))
            route(dve.tensor_scalar(nbk[:, 2, :], nbk[:, 1, :], pidx[:, :], None, ALU.is_le))
            route(dve.tensor_reduce(itc[:, 1:2], nbk[:, 2, :], AX_X, ALU.add))
            route(dve.scalar_tensor_tensor(nbk[:, 0, :], nbk[:, 0, :], -float(SLOT), gcst, ALU.mult, ALU.add))
            route(dve.tensor_tensor_reduce(nbk[:, 0, :], nbk[:, 2, :], nbk[:, 0, :], 1.0, 0.0, ALU.mult, ALU.add,
                                           itc[:, 2:3]))
            dve.tensor_tensor(itc[:, 0:1], itc[:, 2:3], place0[:, :], ALU.add).then_inc(item_cols, 1)
            dve.wait_ge(gathered, 1)
            dve.tensor_tensor(xg, GAB[:, :].rearrange("p (c s) -> p c s", c=KC),
                              n2[:, :, None].to_broadcast([P, KC, 64]), ALU.mult).then_inc(xg_ready, 1)
            route(dve.tensor_scalar(npf[:, :], halfc[:, :], nbk[:, 1, NE - 1:NE], 0.5, ALU.add, ALU.mult))
            route(dve.tensor_scalar(base[:, :], iota[:, :], npf[:, 0:1], None, ALU.is_le))
            route(dve.tensor_reduce(npf[:, 0:1], base[:, :], AX_X, ALU.add))
            route(dve.tensor_scalar(base[:, :], iota[:, :], npf[:, 1:2], None, ALU.is_le))
            route(dve.tensor_reduce(npf[:, 1:2], base[:, :], AX_X, ALU.add))
            route(dve.tensor_scalar(npair[:, :], npf[:, :], -1.0, None, ALU.add))
            dve.wait_ge(item_rows, 1)
            route(dve.tensor_copy(base[:, :], OB[1][:, 256:384]))
            dve.tensor_copy(eint[:, :], OB[1][:, 384:512]).then_inc(items_ready, 1)
            route(dve.tensor_tensor(pe8[:, :, :], lg[:, :, 0:NG], top[:, :, 0:1].to_broadcast([P, NT, NG]),
                                    ALU.subtract))
            dve.tensor_tensor(rt[:, 3, :], tope[:, :, 1], tope[:, :, 0], ALU.subtract).then_inc(grp_sub, 1)
            dve.wait_ge(grp_exp, 2)
            route(dve.tensor_reduce(rt[:, 1, :], pe8[:, :, :], AX_X, ALU.add))
            route(dve.tensor_scalar(rt[:, 5, :], rt[:, 4, :], 1.0, None, ALU.add))
            route(dve.tensor_tensor(rt[:, 6, :], rt[:, 5, :], rt[:, 1, :], ALU.mult))
            route(dve.reciprocal(wtok[:, :, 0], rt[:, 6, :]))
            dve.wait_ge(r_v, rv)
            dve.tensor_tensor(wtok[:, :, 1], wtok[:, :, 0], rt[:, 4, :], ALU.mult).then_inc(weighed, 1)

            def pick_pair(cols, first):
                k = first
                dve.tensor_copy(bnxt[:, :], cols).then_inc(pick_v, 1)
                dve.wait_ge(pick_v, k + 1)
                dve.tensor_tensor(tgt.rearrange("p (j s) -> p j s", j=2), iota[:, None, 0:SLOT].to_broadcast([P, 2, SLOT]),
                                  bnxt[:, :, None].to_broadcast([P, 2, SLOT]), ALU.add).then_inc(pick_v, 1)
                dve.wait_ge(pick_v, k + 2)
                for t in range(NT):
                    dve.tensor_scalar(pick[:, t, :], tgt, pos[:, 2 * t:2 * t + 1], None, ALU.is_equal)\
                        .then_inc(pick_v, 1)
                dve.wait_ge(pick_v, k + 4)
                dve.scalar_tensor_tensor(pick[:, 0, :], tgt, pos[:, 1:2], pick[:, 0, :], ALU.is_equal, ALU.add)\
                    .then_inc(pick_v, 1)
                dve.wait_ge(pick_v, k + 5)
                dve.scalar_tensor_tensor(pick[:, 1, :], tgt, pos[:, 3:4], pick[:, 1, :], ALU.is_equal, ALU.add)\
                    .then_inc(picked, 1)

            def pair_weights(i, cols):
                dve.tensor_copy(bcur[:, :], cols)\
                    .then_inc(comb_v, 1)
                dve.wait_ge(comb_v, 4 * i + 1)
                dve.tensor_scalar(scol[:, :], bcur[:, :], pmod[:, :], None, ALU.add).then_inc(comb_v, 1)
                dve.wait_ge(comb_v, 4 * i + 2)
                dve.wait_ge(comb_done, 2 * i + 1)
                for j in range(2):
                    dve.scalar_tensor_tensor(combt, posb, scol[:, j:j + 1], wb, ALU.is_equal, ALU.mult)\
                        .then_inc(comb_v, 1)
                    dve.wait_ge(comb_v, 4 * i + (3 + j))
                    dve.tensor_tensor(comb[:, j, :], combt[:, 0:T], combt[:, T:2 * T], ALU.add).then_inc(combined, 1)
                    dve.wait_ge(combined, 2 * i + (j + 1))

            def hidden(i, j):
                tr = TRB[:, T * j:T * j + T].rearrange("p (i s) -> p i s", i=2)
                dve.wait_ge(hid_tanh, 2 * i + (j + 1))
                dve.scalar_tensor_tensor(gt1[:, j, :, :], tht[:, j, :, :], 1.0, tr[:, :, 0:64], ALU.add, ALU.mult)\
                    .then_inc(hid_v, 1)
                dve.wait_ge(hid_v, 4 * i + (2 * j + 1))
                dve.scalar_tensor_tensor(actT[:, j, :, :], gt1[:, j, :, :], 0.5, tr[:, :, 64:128],
                                         ALU.mult, ALU.mult).then_inc(hid_v, 1)

            def keep_gathered(i):
                dve.wait_ge(gathered, i + 2)
                dve.wait_ge(gu_done, 2 * i + 2)
                dve.tensor_tensor(xg, GAB[:, :].rearrange("p (c s) -> p c s", c=KC),
                                  n2[:, :, None].to_broadcast([P, KC, 64]), ALU.mult).then_inc(xg_ready, 1)

            hidden(0, 0)
            pick_pair(base[:, 2:4], 0)
            dve.wait_ge(rows_copied, 2)
            pair_weights(0, base[:, 0:2])
            hidden(0, 1)
            keep_gathered(0)
            pairs = dve.value_load(npair[0:1, 0:1], min_val=1, max_val=P // 2 - 1)
            whole = dve.value_load(npair[0:1, 1:2], min_val=0, max_val=P // 2 - 2) + 1
            with dve.If(whole > 1):
                with dve.Fori(1, whole) as i:
                    dve.wait_ge(gathered, i + 1)
                    pick_pair(base[:, bass.ds(2 * i + 2, 2)], 5 * i)
                    pair_weights(i, base[:, bass.ds(2 * i, 2)])
                    hidden(i, 0)
                    hidden(i, 1)
                    keep_gathered(i)
            with dve.If(pairs > whole):
                pair_weights(whole, base[:, bass.ds(2 * whole, 2)])
                hidden(whole, 0)

            dve.wait_ge(fw_in, 16)
            dve.wait_ge(fin_root, 1)
            dve.reciprocal(ss[:, 4:6], ss[:, 2:4]).then_inc(fin_rstd, 1)
            dve.wait_ge(fin_rstd, 1)
            for t in range(NT):
                dve.scalar_tensor_tensor(xs[:, t, :].rearrange("p (b n) -> p b n", b=4), acc4[:, :, T * t:T * t + T],
                                         ss[:, 4 + t:5 + t], fw.rearrange("p (b n) -> p b n", b=4),
                                         ALU.mult, ALU.mult).then_inc(fin_out, 1)


_INS = ["x", "norm1_w", "w_in", "att_f_bias", "ssd_conv_w", "ssd_conv_b", "ssd_dt_bias", "ssd_a_log", "ssd_d",
        "ssd_norm_w", "ml_conv_w", "ml_conv_b", "ml_i_bias", "ml_f_bias", "ml_norm_w", "gate_bias", "w_branch",
        "w_out", "norm2_w", "w_group", "b_group", "w_expert_router", "b_expert_router", "w_gate", "w_up", "w_down",
        "final_norm_w"]


def kernel(**inputs):
    import numpy as np
    import concourse.bacc as bacc
    from concourse.bass_utils import run_bass_kernel_spmd

    nc = bacc.Bacc("TRN2", target_bir_lowering=False, num_devices=1)
    arrays, args = {}, []
    for name in _INS:
        a = np.ascontiguousarray(inputs[name])
        arrays[f"in_{name}"] = a
        args.append(nc.dram_tensor(f"in_{name}", a.shape, mybir.dt.from_np(a.dtype), kind="ExternalInput").ap())
    args.append(nc.dram_tensor("out_0", inputs["x"].shape, F32, kind="ExternalOutput").ap())
    build_trunk(nc, *args)
    r = run_bass_kernel_spmd(nc, [arrays], core_ids=[0])
    return r.results[0]["out_0"]
```

```python
from contextlib import ExitStack

import concourse.bass as bass
from concourse import mybir

F32 = mybir.dt.float32
F32R = mybir.dt.float32r
I32 = mybir.dt.int32
U32 = mybir.dt.uint32
ALU = mybir.AluOpType
ACT = mybir.ActivationFunctionType
AX_X = mybir.AxisListType.X

P = 128
EPS = 1e-6
MASKED = -1e30


def plan(D, W):
    blocks, units = [], []
    col = 0
    at = {}
    for name, width in (("aq", D), ("ak", D), ("av", D), ("af", 16), ("z", D), ("xbc", 2 * D), ("dt", 16),
                        ("mq", D), ("mk", D), ("mv", D), ("mi", 4), ("mf", 4), ("mo", D), ("g", 3 * D)):
        at[name] = col
        col += width
    assert col == W

    def blocks_of(name):
        return [(name, b) for b in range({"xbc": 2 * D, "g": 3 * D, "br": 3 * D}.get(name, D) // 256)]

    qkv, xbc = blocks_of("aq") + blocks_of("ak") + blocks_of("av"), blocks_of("xbc")
    order = [b for pair in zip(qkv, xbc) for b in pair] + qkv[len(xbc):] + blocks_of("z") + blocks_of("mo")
    conv, mv = blocks_of("mq") + blocks_of("mk"), blocks_of("mv")
    for i in range(4):
        order += conv[2 * i:2 * i + 2] + mv[i:i + 1]
    order += blocks_of("g") + blocks_of("br") + blocks_of("out")
    for name, b in order:
        if name == "br":
            blocks.append(("br", b // 4, 256 * (b % 4)))
        elif name == "out":
            blocks.append(("out", 0, 256 * b))
        else:
            blocks.append(("in", 0, at[name] + 256 * b))
        n = len(blocks) - 1
        if name == "out" and b >= 2:
            if b == 3:
                units += [(name, n - 3 + h, t, h) for t in range(2) for h in (2, 3)]
        elif name in ("av", "mv", "out"):
            units += [(name, n, t, b) for t in range(2)]
        else:
            units += [(name, n, c, 2 * b + c) for c in range(2)]
    return blocks, units, at


def stages(units):
    first = {}
    for u, unit in enumerate(units):
        first.setdefault(unit[0], u)
    follow = [[] for _ in units]
    follow[4].append(("sums", 0))
    u0 = first["z"]
    for s in range(19):
        follow[u0 + s] += [(k, s - lag) for lag, k in enumerate(("fox_a", "fox_p", "fox_b", "fox_c"))
                           if 0 <= s - lag < 16]
    u0 = first["mq"] + 3
    for s in range(20):
        if s < 4:
            follow[u0 + s] += [("ssd_x", 2 * s), ("ssd_x", 2 * s + 1), ("ssd_cb", s)]
        if 0 <= s - 1 < 16:
            follow[u0 + s] += [("ssd_a", s - 1)]
        if 0 <= s - 2 < 16:
            follow[u0 + s] += [("ssd_w", s - 2)]
        if 0 <= s - 4 < 16:
            follow[u0 + s] += [("ssd_c", s - 4)]

    def norm(k, u0):
        for pair in range(2):
            for lag, step in enumerate(("norm_sq", "norm_ms", "norm_rt")):
                follow[u0 + 2 * pair + lag] += [(step, 4 * k + 2 * pair + i) for i in range(2)]
            for i in range(2):
                follow[u0 + 3 * pair + 2 + i] += [("norm_y", 4 * k + 2 * pair + i)]

    norm(0, first["g"])
    for h in range(4):
        u = first["g"] + 1 + 5 * h
        for lag, step in ((0, "ml_a"), (1, "ml_w"), (3, "ml_b"), (4, "ml_c")):
            follow[u + lag] += [(step, h)]
    norm(1, first["g"] + 22)
    for b, s in enumerate((18, 20, 30)):
        follow[first["g"] + s] += [("y_split", b)]
    return follow, first


def build_trunk(nc, x, norm1_w, w_in, att_f_bias, ssd_conv_w, ssd_conv_b, ssd_dt_bias, ssd_a_log, ssd_d,
                ssd_norm_w, ml_conv_w, ml_conv_b, ml_i_bias, ml_f_bias, ml_norm_w, gate_bias, w_branch, w_out,
                norm2_w, w_group, b_group, w_expert_router, b_expert_router, w_gate, w_up, w_down,
                final_norm_w, out):
    D = x.shape[2]
    T = x.shape[1]
    NT = T // P
    KC = D // P
    NE = w_gate.shape[1]
    NG = w_group.shape[2]
    EG = NE // NG
    FE = w_gate.shape[3]
    HC = FE // P
    NR = NG + NE
    SLOT = 32
    assert (D, T, NE, NG, FE) == (1024, 256, 64, 8, 512)
    BLOCKS, UNITS, COL = plan(D, w_in.shape[2])
    FOLLOW, FIRST = stages(UNITS)
    NB = len(BLOCKS)
    RING = 3
    BANKS = 3
    NU = len(UNITS)
    LAST = {unit[1]: u for u, unit in enumerate(UNITS)}
    CONSTS = 26
    PAR_IN, GATE_IN = 16 * 10, 16 * 11
    SMALL_GL = 4
    ML_NEG, ML_W = 4, 4

    ctx = ExitStack()
    with ctx:
        def sb(name, shape, dt=F32):
            return ctx.enter_context(nc.sbuf_tensor(name, shape, dt))

        def sb_two(name, shape):
            with nc.sbuf_tensor(name + "_parts", shape, F32R) as parts:
                pass
            return sb(name, shape), parts

        def sem(name):
            return ctx.enter_context(nc.semaphore(name))

        xs = sb("xs", [P, NT, D])
        ring, ring_parts = sb_two("ring", [P, RING, 2, KC, 256])
        r1, r1_parts = sb_two("r1", [P, 12288])
        r2, r2_parts = sb_two("r2", [P, 6144])
        zu, zu_parts = sb_two("zu", [P, KC, T])
        r3, r3_parts = sb_two("r3", [P, 6144])
        cbm = sb("cbm", [P, 4, 384])
        ident = sb("ident", [P, P])
        identr = sb("identr", [P, P], F32R)
        cols_hi = sb("cols_hi", [P, NT, 36], F32R)
        cols_lo = sb("cols_lo", [P, NT, 36], F32R)
        tri = sb("tri", [P, P])
        stri = sb("stri", [P, P])
        ones = sb("ones", [P, P])
        mean = sb("mean", [P, P])
        mask01 = sb("mask01", [P, 384])
        mneg = sb("mneg", [P, 256])
        eps = sb("eps", [P, 1])
        pc = sb("pc", [P, 2, 112])
        prow = sb("prow", [112, 2, P])
        n2 = sb("n2", [P, KC])
        dsk = sb("dsk", [P, KC])
        wsm = sb("wsm", [P, KC, 40])
        bsm = sb("bsm", [P, 40])
        alog = sb("alog", [P, 16])
        sm = sb("sm", [P, NT, 40])
        smw = sb("smw", [P, 6, NT, 40])
        dtt = sb("dtt", [P, NT, 16])
        gl = sb("gl", [P, NT, 36])
        li = sb("li", [P, NT, 4])
        cum = sb("cum", [P, NT, 36])
        rn = sb("rn", [P, NT, 20])
        ss = sb("ss", [P, 8])
        work = sb("work", [P, 10, 384])
        acc = sb("acc", [P, 3, T])
        thb = sb("thb", [P, 3, T])
        mx = sb("mx", [P, 2, 2])
        nmx = sb("nmx", [P, 2, 2])
        rsum = sb("rsum", [P, 2, 2])
        rinv = sb("rinv", [P, 2, 2])
        mls = sb("mls", [P, 6, 2])
        tmpu = sb("tmpu", [P, 2, T])
        sqj = thb[:, :, :].rearrange("p a b -> p (a b)")[:, 0:512]
        root = [acc[:, 0, :], acc[:, 1, :], acc[:, 2, :], thb[:, 0, :]]
        bigt = work[:, :, :].rearrange("p a b -> p (a b)")[:, 0:D]

        qT = r1[:, 0:2048].rearrange("p (c t) -> p c t", c=KC)
        kT = r1[:, 2048:4096].rearrange("p (c t) -> p c t", c=KC)
        vN = r1[:, 4096:6144].rearrange("p (t n) -> p t n", t=NT)
        moT = r1[:, 6144:8192].rearrange("p (c t) -> p c t", c=KC)
        hraw = r3[:, 4096:6144].rearrange("p (c t) -> p c t", c=KC)
        hH = r1_parts[:, 8192:10240].rearrange("p (c t) -> p c t", c=KC)
        hL = r1_parts[:, 10240:12288].rearrange("p (c t) -> p c t", c=KC)
        yH = r1_parts[:, 0:6144].rearrange("p (b c t) -> p b c t", b=3, c=KC)
        zuH = r2_parts[:, 0:2048].rearrange("p (c t) -> p c t", c=KC)
        hN = r1[:, 10240:12288].rearrange("p (t n) -> p t n", t=NT)
        xbcT = r2[:, 0:4096].rearrange("p (c t) -> p c t", c=2 * KC)
        xdt = r2[:, 4096:6144].rearrange("p (t n) -> p t n", t=NT)
        gT = r2[:, :].rearrange("p (c t) -> p c t", c=3 * KC)
        yL = r3_parts[:, :].rearrange("p (b c t) -> p b c t", b=3, c=KC)
        yT = r3[:, :].rearrange("p (b c t) -> p b c t", b=3, c=KC)
        h2p = r3[:, 0:2048].rearrange("p (t c d) -> p t c d", t=NT, c=KC)
        x1T = r3[:, 2048:4096].rearrange("p (c t) -> p c t", c=KC)
        posb = r3[:, 4096:4608]
        wb = r3[:, 4608:5120]
        comb = r3[:, 5120:5632].rearrange("p (j t) -> p j t", j=2)
        combt = r3[:, 5632:6144]
        slot1 = ring[:, :, :, :, :].rearrange("p r h c n -> p (r h c n)")
        wg_s = [r1[:, 8192:12288].rearrange("p (c n) -> p c n", c=KC), slot1[:, 0:4096].rearrange("p (c n) -> p c n", c=KC)]
        wu_s = [r1[:, 0:4096].rearrange("p (c n) -> p c n", c=KC), slot1[:, 8192:12288].rearrange("p (c n) -> p c n", c=KC)]
        wd_s = [r1[:, 4096:8192].rearrange("p (c n) -> p c n", c=HC), slot1[:, 4096:8192].rearrange("p (c n) -> p c n", c=HC)]
        xg = r2[:, 0:512].rearrange("p (c s) -> p c s", c=KC)
        gus = r2[:, 512:1024].rearrange("p (j n) -> p j n", j=2)
        tht = r2[:, 1024:1280].rearrange("p (j i s) -> p j i s", j=2, i=2)
        gt1 = r2[:, 1280:1536].rearrange("p (j i s) -> p j i s", j=2, i=2)
        actT = r2[:, 1536:1792].rearrange("p (j i s) -> p j i s", j=2, i=2)
        ysb = r2[:, 1792:2304].rearrange("p (j n) -> p j n", j=2)
        pick = r2[:, 2304:2432].rearrange("p (t s) -> p t s", t=2)
        tgt = r2[:, 2432:2496]
        fw = r2[:, 2560:2560 + D]
        wrt = sb("wrt", [P, KC, NR])
        brow = sb("brow", [P, NR])
        lg = r2[:, 3584:3728].rearrange("p (t n) -> p t n", t=NT)
        top = sb("top", [P, NT, 8])
        tope = sb("tope", [P, NT, 8])
        tally = sb("tally", [P, NE])
        topi = sb("topi", [P, NT, 8], U32)
        rt = sb("rt", [P, 24, NT])
        ohg = sb("ohg", [P, NT, NG])
        egs = r2[:, 3728:3856].rearrange("p (t e g) -> p t e g", t=NT, e=EG)
        ein = sb("ein", [P, NT, EG])
        pe8 = sb("pe8", [P, NT, NG])
        eid = sb("eid", [P, NT, 2])
        ohe = r2[:, 3856:4112].rearrange("p (a e) -> p a e", e=NE)
        ohm = r2[:, 4368:4496].rearrange("p (a e) -> p a e", e=NE)
        rke = r2[:, 4112:4368].rearrange("p (a e) -> p a e", e=NE)
        rank = sb("rank", [P, NT * 2])
        pos = sb("pos", [P, NT * 2])
        wtok = sb("wtok", [P, NT, 2])
        iota = sb("iota", [P, P])
        thr = sb("thr", [P, 8])
        pmod = sb("pmod", [P, 1])
        pidx = sb("pidx", [P, 1])
        first_blk = r2[:, 5200:5712].rearrange("p (e b) -> p e b", b=8)
        gcst = r2[:, 5712:5776]
        place0 = sb("place0", [P, 1])
        halfc = sb("halfc", [P, 2])
        cnt8 = r2[:, 4496:5008].rearrange("p (e b) -> p e b", b=8)
        nbk = r2[:, 5008:5200].rearrange("p (a e) -> p a e", e=NE)
        itc = sb("itc", [P, 8])
        base = sb("base", [P, P])
        eint = sb("eint", [P, P], I32)
        npf = sb("npf", [P, 2])
        npair = sb("npair", [P, 2], I32)
        bcur = sb("bcur", [P, 2])
        bnxt = sb("bnxt", [P, 2])
        scol = sb("scol", [P, 2])

        acc4 = ctx.enter_context(nc.psum_tensor("acc4", [P, 4, 512], F32))
        bank = [acc4[:, i, :] for i in range(4)] + \
            [ctx.enter_context(nc.psum_tensor(f"bank{i}", [P, 512], F32)) for i in range(4, 8)]
        PJ = bank[0:3]
        SC = bank[3:5]
        TR = bank[5]
        OB = bank[6:8]
        HT_BANK = ((OB[0], OB[1]), (SC[1], TR))
        ACCB = bank[0:4]
        GAB, GUB, TRB, DNB = bank[4:8]

        par_in = sem("par_in")
        gate_in = sem("gate_in")
        x_in = sem("x_in")
        rt_in = sem("rt_in")
        w_in_sem = [sem(f"w_block{i}") for i in range(RING)]
        fw_in = sem("fw_in")
        x1_part = sem("x1_part")
        blk_hi = sem("blk_hi")
        blk_lo = sem("blk_lo")
        h_hi = sem("h_hi")
        h_lo = sem("h_lo")
        y_hi = sem("y_hi")
        y_lo = sem("y_lo")
        u_hi = sem("u_hi")
        u_lo = sem("u_lo")
        consts = sem("consts")
        dstep = sem("dstep")
        astep = sem("astep")
        x_sq = sem("x_sq")
        x_norm = sem("x_norm")
        h_turned = sem("h_turned")
        h_ready = sem("h_ready")
        par_turned = sem("par_turned")
        par_ready = sem("par_ready")
        small_done = sem("small_done")
        small_v = sem("small_v")
        small_a = sem("small_a")
        cum_done = sem("cum_done")
        cum_ready = sem("cum_ready")
        cols_ready = sem("cols_ready")
        proj = sem("proj")
        kept = sem("kept")
        conv_pre = sem("conv_pre")
        conv_sum = sem("conv_sum")
        conv_tanh = sem("conv_tanh")
        conv_out = sem("conv_out")
        fox_scores = sem("fox_scores")
        fox_masked = sem("fox_masked")
        fox_negmax = sem("fox_negmax")
        fox_exp = sem("fox_exp")
        fox_probs = sem("fox_probs")
        fox_turned = sem("fox_turned")
        fox_pt = sem("fox_pt")
        fox_out = sem("fox_out")
        fox_y = sem("fox_y")
        z_tanh = sem("z_tanh")
        z_out = sem("z_out")
        ssd_turned = sem("ssd_turned")
        ssd_x = sem("ssd_x")
        ssd_cb = sem("ssd_cb")
        ssd_cbm = sem("ssd_cbm")
        ssd_bc = sem("ssd_bc")
        ssd_seg = sem("ssd_seg")
        ssd_exp = sem("ssd_exp")
        ssd_w = sem("ssd_w")
        ssd_out = sem("ssd_out")
        ssd_y = sem("ssd_y")
        nrm_sq = sem("nrm_sq")
        nrm_ms = sem("nrm_ms")
        nrm_rt = sem("nrm_rt")
        nrm_y = sem("nrm_y")
        ml_scores = sem("ml_scores")
        ml_neg = sem("ml_neg")
        ml_exp = sem("ml_exp")
        ml_w = sem("ml_w")
        ml_turned = sem("ml_turned")
        ml_pt = sem("ml_pt")
        ml_out = sem("ml_out")
        ml_y = sem("ml_y")
        g_ready = sem("g_ready")
        u_ready = sem("u_ready")
        r_v = sem("r_v")
        wrt_ready = sem("wrt_ready")
        x1_sq = sem("x1_sq")
        x1_sum = sem("x1_sum")
        x1_root = sem("x1_root")
        x1_rstd = sem("x1_rstd")
        h2_ready = sem("h2_ready")
        x1_turned = sem("x1_turned")
        x1_copied = sem("x1_copied")
        logits = sem("logits")
        chosen = sem("chosen")
        ranked = sem("ranked")
        placed = sem("placed")
        grp_sub = sem("grp_sub")
        grp_exp = sem("grp_exp")
        first_pick = sem("first_pick")
        item_cols = sem("item_cols")
        item_rows = sem("item_rows")
        items_ready = sem("items_ready")
        weighed = sem("weighed")
        place_rows = sem("place_rows")
        weight_rows = sem("weight_rows")
        rows_copied = sem("rows_copied")
        gu_in = [sem(f"gu_in{j}") for j in range(2)]
        g0_in = sem("g0_in")
        dn_in = [sem(f"dn_in{j}") for j in range(2)]
        picked = sem("picked")
        combined = sem("combined")
        gathered = sem("gathered")
        xg_ready = sem("xg_ready")
        gu_done = sem("gu_done")
        gu_copied = sem("gu_copied")
        hid_turned = sem("hid_turned")
        hid_tanh = sem("hid_tanh")
        hid_v = sem("hid_v")
        down_done = sem("down_done")
        y_copied = sem("y_copied")
        comb_done = sem("comb_done")
        pick_v = sem("pick_v")
        comb_v = sem("comb_v")
        fin_sq = sem("fin_sq")
        fin_root = sem("fin_root")
        fin_rstd = sem("fin_rstd")
        fin_out = sem("fin_out")
        out_done = sem("out_done")

        lay = w_in[0]
        blk_src = {
            "in": lambda i, c: lay[:, c:c + 256],
            "br": lambda i, c: w_branch[0, i, :, c:c + 256],
            "out": lambda i, c: w_out[0, :, c:c + 256],
        }
        CONV = [u for u, unit in enumerate(UNITS) if unit[0] in ("xbc", "mq", "mk")]
        conv_no = {u: i for i, u in enumerate(CONV)}
        Z0 = FIRST["z"]
        G0 = FIRST["g"]
        BR0 = FIRST["br"]
        OPENS = {}
        for u, unit in enumerate(UNITS):
            if unit[1] + 1 not in OPENS.values():
                OPENS[u] = unit[1] + 1
        OUT0 = FIRST["out"]
        HALF_NO = {(0, 0): 1, (1, 0): 2, (0, 1): 3, (1, 1): 4}
        HALF_UNITS = {(0, 0): 3, (1, 0): 4, (0, 1): 6, (1, 1): 8}

        FREED, n = [], {}
        for kind, *_ in UNITS:
            s = {"xbc": conv_sum, "mq": conv_sum, "mk": conv_sum, "z": z_out, "br": u_ready, "out": x1_part}.get(kind, kept)
            n[s.name] = n.get(s.name, 0) + 1
            FREED.append((s, n[s.name]))

        block = ctx.enter_context(nc.Block())

        @block.sync
        def _(sp):
            for t in range(NT):
                sp.dma_start(xs[:, t, :], x[0, t * P:(t + 1) * P, :]).then_inc(x_in, 16)
            for n, (kind, i, c) in enumerate(BLOCKS):
                if n >= RING:
                    sp.wait_ge(proj, LAST[n - RING] + 1)
                sp.dma_start(ring[:, n % RING, 0, :, :],
                             blk_src[kind](i, c).rearrange("(c p) n -> p c n", p=P)).then_inc(w_in_sem[n % RING], 16)
                if n == 0:
                    col = 0
                    for name, n, bias in (("af", 16, att_f_bias), ("dt", 16, ssd_dt_bias), ("mi", 4, ml_i_bias),
                                          ("mf", 4, ml_f_bias)):
                        sp.dma_start(wsm[:, :, col:col + n],
                                      lay[:, COL[name]:COL[name] + n].rearrange("(c p) n -> p c n", p=P)).then_inc(gate_in, 16)
                        sp.dma_start(bsm[:, col:col + n], bias[0:1, :].to_broadcast([P, n])).then_inc(gate_in, 16)
                        col += n
                    sp.dma_start(alog[:, :], ssd_a_log[0:1, :].to_broadcast([P, 16])).then_inc(gate_in, 16)
                    for i in range(2):
                        with nc.allow_non_contiguous_dma("eight values"):
                            sp.dma_start(dsk[64 * i:64 * i + 64, :],
                                          ssd_d[0:1, :].rearrange("a (c two) -> a c two", two=2)[:, :, i]
                                          .to_broadcast([64, KC])).then_inc(gate_in, 16)
                quarter, odd = divmod(n - UNITS[BR0][1] - RING, 2)
                if 0 <= quarter < 4 and not odd:
                    sp.wait_ge(proj, BR0)
                    c = slice(2 * quarter, 2 * quarter + 2)
                    sp.dma_start(wg_s[0][:, c, :], w_gate[0, 0].rearrange("(p c) n -> p c n", p=P)[:, c, :])\
                        .then_inc(gu_in[0] if quarter == 3 else g0_in, 16)
            sp.wait_ge(proj, OUT0)
            sp.wait_ge(nrm_y, 16)
            sp.dma_start(wu_s[0], w_up[0, 0].rearrange("(p c) n -> p c n", p=P)).then_inc(gu_in[0], 16)
            sp.dma_start(wd_s[0], w_down[0, 0].rearrange("(c p) n -> p c n", p=P)).then_inc(dn_in[0], 16)
            assert UNITS[OUT0 + 2][1] % RING == 2
            sp.wait_ge(proj, OUT0 + 4)
            sp.dma_start(wu_s[1], w_up[0, 1].rearrange("(p c) n -> p c n", p=P)).then_inc(gu_in[1], 16)
            sp.wait_ge(u_ready, 24)
            sp.dma_start(fw, final_norm_w.rearrange("(a n) -> a n", a=1).to_broadcast([P, D])).then_inc(fw_in, 16)
            sp.wait_ge(proj, NU)
            sp.dma_start(wg_s[1], w_gate[0, 1].rearrange("(p c) n -> p c n", p=P)).then_inc(gu_in[1], 16)
            sp.dma_start(wd_s[1], w_down[0, 1].rearrange("(c p) n -> p c n", p=P)).then_inc(dn_in[1], 16)
            sp.wait_ge(items_ready, 1)
            pairs = sp.value_load(npair[0:1, 0:1], min_val=1, max_val=P // 2 - 1)
            whole = sp.value_load(npair[0:1, 1:2], min_val=0, max_val=P // 2 - 2) + 1

            def load_item(i, j):
                e = sp.value_load(eint[0:1, bass.ds(2 * i + j, 1)], min_val=0, max_val=NE - 1)
                sp.wait_ge(gu_done, 2 * i + (j - 1))
                sp.dma_start(wg_s[j], w_gate[0, bass.ds(e, 1), :, :].rearrange(
                    "a (p c) n -> p (a c) n", p=P)).then_inc(gu_in[j], 16)
                sp.dma_start(wu_s[j], w_up[0, bass.ds(e, 1), :, :].rearrange(
                    "a (p c) n -> p (a c) n", p=P)).then_inc(gu_in[j], 16)
                sp.wait_ge(down_done, 2 * i + (j - 1))
                sp.dma_start(wd_s[j], w_down[0, bass.ds(e, 1), :, :].rearrange(
                    "a (c p) n -> p (a c) n", p=P)).then_inc(dn_in[j], 16)

            with sp.If(whole > 1):
                with sp.Fori(1, whole) as i:
                    for j in range(2):
                        load_item(i, j)
            with sp.If(pairs > whole):
                load_item(whole, 0)
            for t in range(NT):
                sp.wait_ge(fin_out, t + 1)
                sp.dma_start(out[0, t * P:(t + 1) * P, :], xs[:, t, :]).then_inc(out_done, 16)
            sp.wait_ge(out_done, 16 * NT)

        @block.gpsimd
        def _(pool):
            def aff(t, pattern, op, base_, mult, fill, inp=None):
                return pool.affine_select(out=t, in_=t if inp is None else inp, compare_op=op, fill=fill, base=base_,
                                          pattern=pattern, channel_multiplier=mult)
            pool.memset(ident[:, :], 0.0).then_inc(consts, 1)
            pool.memset(tri[:, :], 1.0).then_inc(consts, 1)
            pool.memset(stri[:, :], 1.0).then_inc(consts, 1)
            pool.memset(ones[:, :], 1.0).then_inc(consts, 1)
            pool.memset(mean[:, :], 1.0 / 256).then_inc(consts, 1)
            pool.memset(mask01[:, :], 1.0).then_inc(consts, 1)
            pool.memset(mneg[:, :], 0.0).then_inc(consts, 1)
            pool.memset(eps[:, :], EPS).then_inc(consts, 1)
            pool.memset(halfc[:, :], 3.0).then_inc(consts, 1)
            pool.iota(iota[:, :], [[1, P]], base=0, channel_multiplier=0,
                      allow_small_or_imprecise_dtypes=True).then_inc(consts, 1)
            pool.iota(thr[:, :], [[SLOT, 8]], base=0, channel_multiplier=0,
                      allow_small_or_imprecise_dtypes=True).then_inc(consts, 1)
            pool.iota(pidx[:, :], [[0, 1]], base=-2, channel_multiplier=1,
                      allow_small_or_imprecise_dtypes=True).then_inc(consts, 1)
            pool.iota(place0[:, :], [[0, 1]], base=-SLOT, channel_multiplier=SLOT,
                      allow_small_or_imprecise_dtypes=True).then_inc(consts, 1)
            for q in range(4):
                pool.wait_ge(consts, 13 + q)
                pool.iota(pmod[32 * q:32 * q + 32, :], [[0, 1]], base=0, channel_multiplier=1,
                          allow_small_or_imprecise_dtypes=True).then_inc(consts, 1)
            pool.wait_ge(consts, 17)
            aff(ident[:, :], [[-1, P]], ALU.not_equal, 0, 1, 1.0).then_inc(consts, 1)
            aff(tri[:, :], [[1, P]], ALU.is_ge, 0, -1, 0.0).then_inc(consts, 1)
            aff(stri[:, :], [[1, P]], ALU.is_gt, 0, -1, 0.0).then_inc(consts, 1)
            aff(mask01[:, 0:P], [[1, P]], ALU.is_ge, 0, -1, 0.0).then_inc(consts, 1)
            aff(mask01[:, 256:384], [[1, P]], ALU.is_ge, 0, -1, 0.0).then_inc(consts, 1)
            aff(mneg[:, P:256], [[-1, P]], ALU.is_ge, 0, 1, MASKED).then_inc(consts, 1)
            pool.memset(halfc[:, 1:2], 0.0).then_inc(consts, 1)
            aff(place0[:, :], [[0, 1]], ALU.is_gt, -1, 1, float(T)).then_inc(consts, 1)
            pool.wait_ge(consts, 25)
            aff(place0[:, :], [[0, 1]], ALU.not_equal, 0, 1, 0.0).then_inc(consts, 1)
        @block.tensor
        def _(pe):
            pe.wait_ge(consts, CONSTS)
            pe.wait_ge(par_in, PAR_IN)
            for i, n in enumerate((104, 112)):
                mm = pe.transpose(SC[0][:, 112 * i:112 * i + n], prow[0:n, i, :], ident[0:n, 0:n])
            mm.then_inc(par_turned, 1)
            for t in range(NT):
                pe.wait_ge(x_norm, t + 1)
                for c in range(KC):
                    mm = pe.transpose(HT_BANK[t][c // 4][:, P * (c % 4):P * (c % 4) + P], hN[:, t, P * c:P * c + P],
                                      ident[:, :])
                    if c % 4 == 3:
                        mm.then_inc(h_turned, 1)
            pe.wait_ge(gate_in, GATE_IN)
            pe.wait_ge(h_ready, 4)
            for t in range(NT):
                for c in range(KC):
                    mm = pe.matmul(SC[0][:, 256 + 40 * t:256 + 40 * t + 40], hraw[:, c, P * t:P * t + P], wsm[:, c, :],
                                   start=(c == 0), stop=(c == KC - 1))
                mm.then_inc(small_done, 1)

            def x1_turn(t, half):
                pe.wait_ge(x1_part, HALF_UNITS[t, half])
                if t:
                    pe.wait_ge(x1_copied, HALF_NO[0, half])
                for c in range(4):
                    mm = pe.transpose(SC[half][:, P * c:P * c + P],
                                      xs[:, t, 512 * half + P * c:512 * half + P * c + P], ident[:, :])
                mm.then_inc(x1_turned, 1)

            def x1_logits(t, half):
                pe.wait_ge(wrt_ready, 1)
                pe.wait_ge(x1_copied, HALF_NO[t, half])
                for c in range(4 * half, 4 * half + 4):
                    mm = pe.matmul((TR, OB[0])[t][:, 0:NR], x1T[:, c, P * t:P * t + P], wrt[:, c, :],
                                   start=(c == 0), stop=(c == KC - 1))
                mm.then_inc(logits, 1)

            def rank(t):
                pe.wait_ge(chosen, t + 1)
                if t == 0:
                    pe.matmul(OB[1][:, 0:NE], stri[:, :], ohm[:, 0, :], start=True, stop=True)
                    pe.matmul(OB[1][:, NE:2 * NE], ones[:, :], ohm[:, 0, :], start=True, stop=True)\
                        .then_inc(ranked, 1)
                else:
                    pe.matmul(OB[1][:, 2 * NE:3 * NE], stri[:, :], ohm[:, 1, :], start=True, stop=True)
                    pe.matmul(OB[1][:, 3 * NE:4 * NE], ones[:, :], ohm[:, 1, :], start=True, stop=True)\
                        .then_inc(ranked, 1)

            router_in = {(OUT0 + 3, 2): [(x1_turn, 0, 0)], (OUT0 + 4, 5): [(x1_turn, 1, 0)],
                         (OUT0 + 5, 2): [(x1_logits, 0, 0)], (OUT0 + 5, 5): [(x1_logits, 1, 0)],
                         (OUT0 + 6, 2): [(x1_turn, 0, 1)], (OUT0 + 6, 6): [(x1_logits, 0, 1)]}

            def row_of(to, t, col, start, stop):
                for part, of in enumerate((cols_hi, cols_lo)):
                    mm = pe.matmul(to, of[:, t, col:col + 1].to_broadcast([P, P]), identr[:, :],
                                   start=start and part == 0, stop=stop and part == 1)
                return mm

            def product(to, a, b, start, stop):
                (ah, al), (bh, bl) = a, b
                pe.matmul(to, ah, bh, start=start, stop=False)
                pe.matmul(to, ah, bl, start=False, stop=False)
                return pe.matmul(to, al, bh, start=False, stop=stop)

            for u, (kind, n, part, chunk) in enumerate(UNITS):
                if kind == "br" and chunk % KC == 0:
                    pe.wait_ge(y_lo, chunk // KC + 1)
                if u == 0:
                    pe.wait_ge(h_lo, NT)
                if u >= BANKS:
                    pe.wait_ge(*FREED[u - BANKS])
                pj = PJ[u % BANKS]
                w = ring_parts[:, n % RING, :, :, :]
                for c in range(KC):
                    f, l = c == 0, c == KC - 1
                    if c % 4 == 0:
                        pe.wait_ge(blk_lo, 2 * n + c // 4 + 1)
                    if u == OUT0:
                        pe.wait_ge(u_lo, c + 1)
                    if kind in ("av", "mv", "out"):
                        x = [v[:, c, P * part:P * part + P] for v in ((zuH, zu_parts) if kind == "out" else (hH, hL))]
                        mm = product(pj[:, 0:T], x, (w[:, 1, c, :], w[:, 0, c, :]), f, l)
                    else:
                        wc = [w[:, i, c, P * part:P * part + P] for i in (1, 0)]
                        if kind == "br":
                            x = [v[:, chunk // KC, c, :] for v in (yH, yL)]
                        else:
                            x = [v[:, c, :] for v in (hH, hL)]
                        mm = product(pj[:, 0:T], wc, x, f, l)
                    if c < KC - 1:
                        for job, *of in router_in.get((u, c), ()):
                            job(*of)
                mm.then_inc(proj, 1)
                for job, *of in router_in.get((u, KC - 1), ()):
                    job(*of)
                for stage, h in FOLLOW[u]:
                    if stage == "sums":
                        pe.wait_ge(small_v, SMALL_GL)
                        pe.matmul(TR[:, 128:164], tri[:, :], gl[:, 0, :], start=True, stop=True)
                        pe.matmul(TR[:, 192:228], ones[:, :], gl[:, 0, :], start=True, stop=False)
                        pe.matmul(TR[:, 192:228], tri[:, :], gl[:, 1, :], start=False, stop=True).then_inc(cum_done, 1)
                    elif stage == "fox_a":
                        s = SC[h % 2]
                        if h == 0:
                            pe.wait_ge(*FREED[FIRST["z"] - 1])
                            pe.wait_ge(cols_ready, 5)
                        if h >= 2:
                            pe.wait_ge(fox_masked, 2 * (h - 1))
                        q = slice(64 * (h % 2), 64 * (h % 2) + 64)
                        for lo, qs, nk in ((0, slice(P, T), T), (T, slice(0, P), P)):
                            pe.matmul(s[:, lo:lo + nk], qT[q, h // 2, qs], kT[q, h // 2, 0:nk], start=True, stop=False)
                            for t in range(nk // P):
                                mm = row_of(s[:, lo + P * t:lo + P * t + P], t, h, False, t == nk // P - 1)
                        mm.then_inc(fox_scores, 1)
                    elif stage == "fox_b":
                        pe.wait_ge(fox_probs, 2 * h + 2)
                        if h:
                            pe.wait_ge(fox_pt, h)
                        p = work[:, 2 + h % 2, :]
                        pe.transpose(TR[:, 0:P], p[:, T:384], ident[:, :])
                        pe.transpose(TR[:, P:T], p[:, 0:P], ident[:, :])
                        pe.transpose(TR[:, T:384], p[:, P:T], ident[:, :]).then_inc(fox_turned, 1)
                    elif stage == "fox_c":
                        pe.wait_ge(fox_pt, h + 1)
                        if h >= 4 and h % 2 == 0:
                            pe.wait_ge(fox_y, h // 2 - 1)
                        o = OB[(h // 2) % 2][64 * (h % 2):64 * (h % 2) + 64, :]
                        pt = work[:, 4 + h % 2, :]
                        pe.matmul(o[:, 0:T], vN[:, 0, 64 * h:64 * h + 64], pt[:, 0:T], start=True, stop=False)
                        pe.matmul(o[:, P:T], vN[:, 1, 64 * h:64 * h + 64], pt[:, T:384],
                                  start=False, stop=True).then_inc(fox_out, 1)
                    elif stage == "ssd_x":
                        if h == 0:
                            pe.wait_ge(fox_pt, 16)
                            pe.wait_ge(fox_y, 8)
                            pe.wait_ge(conv_out, 16)
                        elif h >= 2:
                            pe.wait_ge(ssd_x, h - 1)
                        for t in range(NT):
                            mm = pe.transpose((TR, OB[0])[h % 2][:, P * t:P * t + P],
                                              xbcT[:, h, P * t:P * t + P], ident[:, :])
                        mm.then_inc(ssd_turned, 1)
                    elif stage == "ssd_cb":
                        if h:
                            pe.wait_ge(ssd_cbm, h)
                        pe.matmul(OB[1][:, 0:T], xbcT[:, 8 + h, 0:P], xbcT[:, 12 + h, 0:T], start=True, stop=True)
                        pe.matmul(OB[1][:, T:384], xbcT[:, 8 + h, P:T], xbcT[:, 12 + h, P:T],
                                  start=True, stop=True).then_inc(ssd_cb, 1)
                    elif stage == "ssd_a":
                        s = SC[h % 2]
                        if h >= 2:
                            pe.wait_ge(ssd_seg, 2 * (h - 1))
                        else:
                            pe.wait_ge(fox_masked, 32)
                        for t in range(NT):
                            mm = row_of(s[:, P * t:P * t + P], t, 20 + h, True, True)
                        mm.then_inc(ssd_bc, 1)
                    elif stage == "ssd_c":
                        pe.wait_ge(ssd_w, h + 1)
                        pe.wait_ge(ssd_x, h // 2 + 1)
                        if h == 0:
                            pe.wait_ge(ssd_x, 8)
                        elif h == 2:
                            pe.wait_ge(ssd_cbm, 4)
                        elif h % 2 == 0:
                            pe.wait_ge(ssd_y, 2 * (h // 2 - 1))
                        o = OB[(h // 2) % 2][64 * (h % 2):64 * (h % 2) + 64, :]
                        w2 = work[:, 4 + h % 4, :]
                        pe.matmul(o[:, 0:T], xdt[:, 0, 64 * h:64 * h + 64], w2[:, 0:T], start=True, stop=False)
                        pe.matmul(o[:, P:T], xdt[:, 1, 64 * h:64 * h + 64], w2[:, T:384],
                                  start=False, stop=True).then_inc(ssd_out, 1)
                    elif stage == "norm_ms":
                        pe.wait_ge(nrm_sq, h + 1)
                        if h >= 2:
                            pe.wait_ge(nrm_rt, h - 1)
                        if h % 4 == 0:
                            pe.wait_ge(*((ssd_y, 16), (ml_y, 8))[h // 4])
                        for i in range(2):
                            mm = pe.matmul(OB[h % 2][:, 0:T], mean[:, :], work[:, 6 + 2 * (h % 2) + i, 0:T],
                                           start=(i == 0), stop=(i == 1))
                        mm.then_inc(nrm_ms, 1)
                    elif stage == "ml_a":
                        if h == 0:
                            pe.wait_ge(*FREED[max(u for u, unit in enumerate(UNITS) if unit[0] == "mv")])
                            pe.wait_ge(conv_out, len(CONV))
                            pe.wait_ge(ssd_seg, 32)
                        else:
                            pe.wait_ge(ml_w, ML_W * h)
                        for lo, qs, nk in ((0, slice(P, T), T), (T, slice(0, P), P)):
                            for i in range(2):
                                pe.matmul(SC[0][:, lo:lo + nk], qT[:, 2 * h + i, qs], kT[:, 2 * h + i, 0:nk],
                                          start=(i == 0), stop=(i == 1))
                        for t in range(NT):
                            mm = row_of(SC[1][:, P * t:P * t + P], t, 16 + h, True, True)
                        mm.then_inc(ml_scores, 1)
                    elif stage == "ml_b":
                        pe.wait_ge(ml_w, ML_W * (h + 1))
                        if h:
                            pe.wait_ge(ml_pt, h)
                        p = work[:, 2, :]
                        pe.transpose(TR[:, 0:P], p[:, T:384], ident[:, :])
                        pe.transpose(TR[:, P:T], p[:, 0:P], ident[:, :])
                        pe.transpose(TR[:, T:384], p[:, P:T], ident[:, :]).then_inc(ml_turned, 1)
                    elif stage == "ml_c":
                        pe.wait_ge(ml_pt, h + 1)
                        if h == 0:
                            pe.wait_ge(nrm_rt, 4)
                        else:
                            pe.wait_ge(ml_y, 2 * h)
                        pt = work[:, 4, :]
                        for i in range(2):
                            v = slice(256 * h + P * i, 256 * h + P * i + P)
                            pe.matmul(OB[i][:, 0:T], vN[:, 0, v], pt[:, 0:T], start=True, stop=False)
                            pe.matmul(OB[i][:, P:T], vN[:, 1, v], pt[:, T:384],
                                      start=False, stop=True).then_inc(ml_out, 1)

            x1_turn(1, 1)
            rank(0)
            x1_logits(1, 1)

            def gather_first(t):
                pe.wait_ge(first_pick, t + 1)
                pe.wait_ge(h2_ready, t + 1)
                for c in range(KC):
                    mm = pe.matmul(GAB[:, 64 * c:64 * c + 64], h2p[:, t, c, :], pick[:, t, :],
                                   start=(t == 0 and c == 0), stop=(t == 1), skip_group_check=True)
                return mm

            def gather(i):
                pe.wait_ge(picked, i)
                for c in range(KC):
                    for t in range(NT):
                        mm = pe.matmul(GAB[:, 64 * c:64 * c + 64], h2p[:, t, c, :], pick[:, t, :],
                                       start=(t == 0), stop=(t == NT - 1))
                mm.then_inc(gathered, 1)

            def start_sums(banks):
                pe.wait_ge(x1_part, 8)
                for n in banks:
                    mm = pe.matmul(ACCB[n], ident[:, :], xs[:, :, T * n:T * n + T], start=True, stop=True)
                return mm

            def gate_up(i, j, chunks=range(KC)):
                for c in chunks:
                    if c == 0:
                        pe.wait_ge(gu_in[j], 32 * i + 32)
                        if j == 0:
                            pe.wait_ge(xg_ready, i + 1)
                    for g in range(4):
                        w = (wg_s[j] if g < 2 else wu_s[j])[:, c, T * (g % 2):T * (g % 2) + T]
                        mm = pe.matmul(GUB[32 * g:32 * g + 32, T * j:T * j + T], xg[:, c, 32 * j:32 * j + 32], w,
                                       start=(c == 0), stop=(c == KC - 1))
                if KC - 1 in chunks:
                    mm.then_inc(gu_done, 1)

            def hidden_turn(i, j):
                pe.wait_ge(gu_copied, 2 * i + (j + 1))
                for k in range(2):
                    mm = pe.transpose(TRB[:, T * j + P * k:T * j + P * k + P], gus[:, j, P * k:P * k + P],
                                      ident[:, :])
                mm.then_inc(hid_turned, 1)

            def down(i, j):
                pe.wait_ge(hid_v, 4 * i + (2 * j + 2))
                pe.wait_ge(dn_in[j], 16 * i + 16)
                dn = DNB[:, T * j:T * j + T]
                for c in range(HC):
                    a = actT[:, j, c % 2, 32 * (c // 2):32 * (c // 2) + 32]
                    for g in range(4):
                        mm = pe.matmul(dn[32 * g:32 * g + 32, :], a, wd_s[j][:, c, T * g:T * g + T],
                                       start=(c == 0), stop=(c == HC - 1))
                mm.then_inc(down_done, 1)

            def combine(i, j):
                pe.wait_ge(y_copied, 2 * i + (j + 1))
                pe.wait_ge(combined, 2 * i + (j + 1))
                for t in range(NT):
                    for g in range(4):
                        r = slice(32 * g, 32 * g + 32)
                        mm = pe.matmul(ACCB[g][:, T * t:T * t + T], comb[r, j, P * t:P * t + P], ysb[r, j, :],
                                       start=False, stop=True, skip_group_check=True)
                mm.then_inc(comb_done, 1)

            gather_first(0)
            rank(1)
            start_sums((0,))
            gather_first(1).then_inc(gathered, 1)
            pe.wait_ge(g0_in, 48)
            gate_up(0, 0, range(0, 4))
            pe.wait_ge(item_cols, 1)
            for i in range(2):
                mm = pe.matmul(OB[1][:, 256 + P * i:256 + P * i + P], itc[:, i:i + 1].to_broadcast([P, P]),
                               ident[:, :], start=True, stop=True)
            mm.then_inc(item_rows, 1)
            gate_up(0, 0, range(4, KC))
            hidden_turn(0, 0)
            pe.wait_ge(items_ready, 1)
            down(0, 0)
            gate_up(0, 1)
            for dst, src, done in ((SC[0], pos[:, :].rearrange("p (t k) -> p t k", t=NT), place_rows),
                                   (GAB, wtok, weight_rows)):
                if done is weight_rows:
                    pe.wait_ge(weighed, 1)
                for k in range(2):
                    for t in range(NT):
                        mm = pe.matmul(dst[:, T * k + P * t:T * k + P * t + P],
                                       src[:, t, k:k + 1].to_broadcast([P, P]), ident[:, :], start=True, stop=True)
                mm.then_inc(done, 1)
            start_sums((1, 2))
            pe.wait_ge(rows_copied, 1)
            start_sums((3,)).then_inc(comb_done, 1)
            pe.wait_ge(rows_copied, 2)
            gather(1)
            combine(0, 0)
            hidden_turn(0, 1)
            down(0, 1)
            combine(0, 1)

            def item(i, j):
                gate_up(i, j)
                if j == 0:
                    gather(i + 1)
                hidden_turn(i, j)
                down(i, j)
                combine(i, j)

            pairs = pe.value_load(npair[0:1, 0:1], min_val=1, max_val=P // 2 - 1)
            whole = pe.value_load(npair[0:1, 1:2], min_val=0, max_val=P // 2 - 2) + 1
            with pe.If(whole > 1):
                with pe.Fori(1, whole) as i:
                    item(i, 0)
                    item(i, 1)
            with pe.If(pairs > whole):
                gate_up(whole, 0)
                hidden_turn(whole, 0)
                down(whole, 0)
                combine(whole, 0)

        @block.scalar
        def _(act):
            rows = ((0, 0, norm1_w[0], KC), (0, 8, ssd_conv_w[0].rearrange("k n -> (k n)"), 64),
                    (0, 72, ssd_conv_b[0], 16), (0, 88, ssd_norm_w[0], 8), (0, 96, ml_norm_w[0], 8),
                    (1, 0, ml_conv_w[0].rearrange("k n -> (k n)"), 64), (1, 64, ml_conv_b[0], 16),
                    (1, 80, gate_bias[0], 24))
            for i, r, src, n in rows:
                act.dma_start(prow[r:r + n, i, :], src.rearrange("(r p) -> r p", p=P)).then_inc(par_in, 16)
            act.dma_start(prow[104:112, 1, :], norm2_w[0].rearrange("(r p) -> r p", p=P)).then_inc(par_in, 16)
            act.dma_start(n2[:, :], norm2_w[0].rearrange("(p c) -> p c", p=P)).then_inc(par_in, 16)
            act.wait_ge(consts, CONSTS)
            for t in range(NT):
                act.wait_ge(x_sq, t + 1)
                act.activation(ss[:, 2 + t:3 + t], ss[:, t:t + 1], ACT.Sqrt, bias=eps[:, :], scale=1.0 / D)\
                    .then_inc(astep, 1)

            def block_high(n):
                act.wait_ge(w_in_sem[n % RING], 16 * (n // RING + 1))
                for c in (slice(0, KC // 2), slice(KC // 2, KC)):
                    act.activation(ring_parts[:, n % RING, 1, c, :], ring[:, n % RING, 0, c, :], ACT.Copy)\
                        .then_inc(blk_hi, 1)

            for t in range(NT):
                act.wait_ge(h_ready, 2 * t + 2)
                act.activation(hH[:, :, P * t:P * t + P], hraw[:, :, P * t:P * t + P], ACT.Copy)\
                    .then_inc(h_hi, 1)
            block_high(0)
            act.wait_ge(small_v, 2)
            act.wait_ge(gate_in, GATE_IN)
            act.activation(smw[:, 1, :, :], smw[:, 0, :, :], ACT.Exp, scale=-1.0).then_inc(small_a, 1)
            act.activation(alog[:, :], alog[:, :], ACT.Exp).then_inc(small_a, 1)
            act.wait_ge(small_v, 3)
            act.activation(smw[:, 3, :, :], smw[:, 2, :, :], ACT.Ln).then_inc(small_a, 1)
            with nc.allow_non_contiguous_dma("router weights"):
                act.dma_start(wrt[:, :, 0:NG], w_group[0].rearrange("(c p) n -> p c n", p=P)).then_inc(rt_in, 16)
                act.dma_start(wrt[:, :, NG:NR], w_expert_router[0].rearrange("(c p) n -> p c n", p=P))\
                    .then_inc(rt_in, 16)
            act.dma_start(brow[:, 0:NG], b_group[0:1, :].to_broadcast([P, NG])).then_inc(rt_in, 16)
            act.dma_start(brow[:, NG:NR], b_expert_router[0:1, :].to_broadcast([P, NE])).then_inc(rt_in, 16)
            act.wait_ge(par_ready, 3)

            def tanh_of(u):
                i = conv_no[u]
                act.wait_ge(conv_sum, i + 1)
                if i >= 3:
                    act.wait_ge(conv_out, i - 2)
                act.activation(thb[:, i % 3, :], acc[:, i % 3, :], ACT.Tanh).then_inc(conv_tanh, 1)

            for u, (kind, n, part, chunk) in enumerate(UNITS):
                pj = PJ[u % BANKS]
                if u in OPENS and OPENS[u] < NB:
                    block_high(OPENS[u])
                if kind in ("aq", "ak", "av", "mv", "mo", "z", "g", "xbc", "mq", "mk"):
                    act.wait_ge(proj, u + 1)
                if kind == "aq":
                    act.activation(qT[:, chunk, :], pj[:, 0:T], ACT.Copy, scale=64 ** -0.5).then_inc(kept, 1)
                elif kind == "ak":
                    act.activation(kT[:, chunk, :], pj[:, 0:T], ACT.Copy).then_inc(kept, 1)
                elif kind in ("av", "mv"):
                    act.activation(vN[:, part, T * chunk:T * chunk + T], pj[:, 0:T], ACT.Copy).then_inc(kept, 1)
                elif kind == "mo":
                    act.activation(moT[:, chunk, :], pj[:, 0:T], ACT.Tanh, scale=0.5).then_inc(kept, 1)
                elif kind == "z":
                    i = u - Z0
                    if i >= 2:
                        act.wait_ge(z_out, i - 1)
                    act.activation(work[:, 8 + i % 2, 0:T], pj[:, 0:T], ACT.Tanh, scale=0.5).then_inc(z_tanh, 1)
                elif kind == "g":
                    if u == G0:
                        act.wait_ge(ssd_y, 16)
                    act.activation(gT[:, chunk, :], pj[:, 0:T], ACT.Tanh, bias=pc[:, 1, 80 + chunk:81 + chunk],
                                   scale=0.5).then_inc(kept, 1)
                elif u in conv_no:
                    i = conv_no[u]
                    w0, b0, wi, ch = (8, 72, 0, chunk) if kind == "xbc" else (0, 64, 1, chunk + (8 if kind == "mk" else 0))
                    if i >= 3:
                        act.wait_ge(conv_out, i - 2)
                    act.activation(acc[:, i % 3, :], pj[:, 0:T], ACT.Identity, bias=pc[:, wi, b0 + ch:b0 + ch + 1],
                                   scale=pc[:, wi, w0 + 48 + ch:w0 + 49 + ch]).then_inc(conv_pre, 1)
                if u and u - 1 in conv_no:
                    tanh_of(u - 1)
                if kind == "br" and chunk >= 2 * KC:
                    oc = chunk - 2 * KC
                    act.wait_ge(u_ready, 2 * KC + oc + 1)
                    act.activation(zuH[:, oc, :], zu[:, oc, :], ACT.Copy).then_inc(u_hi, 1)
                for stage, h in FOLLOW[u]:
                    if stage == "y_split":
                        if h < 2:
                            act.wait_ge(ml_scores, 4)
                            act.wait_ge(*((fox_y, 8), (nrm_y, 8))[h])
                        else:
                            act.wait_ge(ml_out, 8)
                            act.wait_ge(nrm_y, 16)
                        act.activation(yH[:, h, :, :], yT[:, h, :, :], ACT.Copy).then_inc(y_hi, 1)
                    elif stage == "fox_a":
                        act.wait_ge(fox_negmax, h + 1)
                        if h >= 2:
                            act.wait_ge(fox_turned, h - 1)
                        b = h % 2
                        act.activation(work[:, 2 + b, 0:T], work[:, b, 0:T], ACT.Exp, bias=nmx[:, b, 1:2],
                                       accum_out=rsum[:, b, 1:2]).then_inc(fox_exp, 1)
                        act.activation(work[:, 2 + b, T:384], work[:, b, T:384], ACT.Exp, bias=nmx[:, b, 0:1],
                                       accum_out=rsum[:, b, 0:1]).then_inc(fox_exp, 1)
                    elif stage == "fox_b":
                        act.wait_ge(fox_turned, h + 1)
                        if h >= 2:
                            act.wait_ge(fox_out, h - 1)
                        act.activation(work[:, 4 + h % 2, :], TR[:, 0:384], ACT.Copy).then_inc(fox_pt, 1)
                    elif stage == "ssd_a":
                        act.wait_ge(ssd_seg, 2 * h + 2)
                        if h >= 2:
                            act.wait_ge(ssd_w, h - 1)
                        act.activation(work[:, 2 + h % 2, :], work[:, h % 2, :], ACT.Exp).then_inc(ssd_exp, 1)
                    elif stage == "norm_sq":
                        k, g = divmod(h, 4)
                        act.wait_ge(*((ssd_y, 16), (ml_y, 8))[k])
                        if h >= 2:
                            act.wait_ge(nrm_ms, h - 1)
                        act.activation(work[:, 6 + 2 * (g % 2):8 + 2 * (g % 2), 0:T],
                                       yT[:, 1 + k, 2 * g:2 * g + 2, :], ACT.Square).then_inc(nrm_sq, 1)
                    elif stage == "norm_rt":
                        act.wait_ge(nrm_ms, h + 1)
                        if h == 0:
                            act.wait_ge(conv_out, len(CONV))
                        elif h >= 4:
                            act.wait_ge(nrm_y, 2 * (h - 3))
                        act.activation(root[h % 4], OB[h % 2][:, 0:T], ACT.Sqrt, bias=eps[:, :])\
                            .then_inc(nrm_rt, 1)
                    elif stage == "ml_a":
                        act.wait_ge(ml_neg, ML_NEG * (h + 1))
                        act.activation(work[:, 1, 0:T], work[:, 0, 0:T], ACT.Exp, bias=mls[:, 1, 1:2]).then_inc(ml_exp, 1)
                        act.activation(work[:, 1, T:384], work[:, 0, T:384], ACT.Exp, bias=mls[:, 1, 0:1])\
                            .then_inc(ml_exp, 1)
                        act.activation(mls[:, 3, :], mls[:, 2, :], ACT.Exp).then_inc(ml_exp, 1)
                    elif stage == "ml_b":
                        act.wait_ge(ml_turned, h + 1)
                        if h:
                            act.wait_ge(ml_out, 2 * h)
                        act.activation(work[:, 4, :], TR[:, 0:384], ACT.Copy).then_inc(ml_pt, 1)

            for (t, half), no in HALF_NO.items():
                act.wait_ge(x1_part, HALF_UNITS[t, half])
                if no > 1:
                    act.wait_ge(x1_sq, no - 1)
                act.activation(sqj, xs[:, t, 512 * half:512 * half + 512], ACT.Square,
                               accum_out=rt[:, 8 + half, t:t + 1]).then_inc(x1_sq, 1)
                if half:
                    act.wait_ge(x1_sum, t + 1)
                    act.activation(ss[:, 2 + t:3 + t], ss[:, t:t + 1], ACT.Sqrt, bias=eps[:, :], scale=1.0 / D)\
                        .then_inc(x1_root, 1)
                    act.wait_ge(x1_rstd, t + 1)
                    act.activation(h2p[:, t, :, :], xs[:, t, :].rearrange("q (p c) -> q c p", c=KC), ACT.Copy,
                                   scale=ss[:, 4 + t:5 + t]).then_inc(h2_ready, 1)
            act.wait_ge(grp_sub, 1)
            act.activation(pe8[:, :, :], pe8[:, :, :], ACT.Exp).then_inc(grp_exp, 1)
            act.activation(rt[:, 4, :], rt[:, 3, :], ACT.Exp).then_inc(grp_exp, 1)

            def item(i, j):
                act.wait_ge(gu_done, 2 * i + (j + 1))
                act.activation(gus[:, j, :], GUB[:, T * j:T * j + T], ACT.Copy).then_inc(gu_copied, 1)
                act.wait_ge(hid_turned, 2 * i + (j + 1))
                act.activation(tht[:, j, :, :], TRB[:, T * j:T * j + T].rearrange("p (i s) -> p i s", i=2)[:, :, 0:64],
                               ACT.Tanh, scale=0.5).then_inc(hid_tanh, 1)
                act.wait_ge(down_done, 2 * i + (j + 1))
                act.activation(ysb[:, j, :], DNB[:, T * j:T * j + T], ACT.Copy).then_inc(y_copied, 1)

            item(0, 0)
            act.wait_ge(place_rows, 1)
            act.activation(posb, SC[0][:, :], ACT.Copy).then_inc(rows_copied, 1)
            act.wait_ge(weight_rows, 1)
            act.activation(wb, GAB[:, :], ACT.Copy).then_inc(rows_copied, 1)
            item(0, 1)
            act.wait_ge(items_ready, 1)
            pairs = act.value_load(npair[0:1, 0:1], min_val=1, max_val=P // 2 - 1)
            whole = act.value_load(npair[0:1, 1:2], min_val=0, max_val=P // 2 - 2) + 1
            with act.If(whole > 1):
                with act.Fori(1, whole) as i:
                    item(i, 0)
                    item(i, 1)
            with act.If(pairs > whole):
                item(whole, 0)

            act.activation(ss[:, 6:7], eps[:, :], ACT.Sqrt)
            act.wait_ge(comb_done, pairs + whole + 1)
            for t in range(NT):
                act.activation(bigt.rearrange("p (b n) -> p b n", b=4), acc4[:, :, T * t:T * t + T], ACT.Square,
                               accum_out=ss[:, t:t + 1]).then_inc(fin_sq, 1)
                act.wait_ge(fin_sq, t + 1)
            act.activation(ss[:, 2:4], ss[:, 0:2], ACT.Sqrt, bias=eps[:, :], scale=1.0 / D).then_inc(fin_root, 1)

        @block.vector
        def _(dve):
            steps = 0

            def step(ins):
                nonlocal steps
                steps += 1
                ins.then_inc(dstep, 1)
                dve.wait_ge(dstep, steps)

            def recip_rms(t):
                step(dve.reciprocal(ss[:, 4 + t:5 + t], ss[:, 2 + t:3 + t]))

            for t in range(NT):
                dve.wait_ge(x_in, 32)
                dve.tensor_tensor_reduce(bigt, xs[:, t, :], xs[:, t, :], 1.0, 0.0, ALU.mult, ALU.add,
                                         ss[:, t:t + 1]).then_inc(x_sq, 1)
                dve.wait_ge(x_sq, t + 1)
            for t in range(NT):
                dve.wait_ge(astep, t + 1)
                recip_rms(t)
                dve.tensor_scalar(hN[:, t, :], xs[:, t, :], ss[:, 4 + t:5 + t], None, ALU.mult).then_inc(x_norm, 1)
            dve.wait_ge(par_turned, 1)
            dve.tensor_copy(pc[:, 0, 0:104], SC[0][:, 0:104]).then_inc(par_ready, 1)
            dve.tensor_scalar(pc[:, 1, 0:104], SC[0][:, 112:216], 0.5, None, ALU.mult).then_inc(par_ready, 1)
            dve.wait_ge(par_ready, 2)
            dve.tensor_scalar(pc[:, 0, 8:88], pc[:, 0, 8:88], 0.5, None, ALU.mult).then_inc(par_ready, 1)
            dve.wait_ge(par_ready, 3)
            step(dve.tensor_copy(pc[:, 1, 104:112], SC[0][:, 216:224]))
            step(dve.tensor_scalar(pc[:, 0, 96:104], pc[:, 0, 96:104], 0.5, None, ALU.mult))
            def block_low(n):
                for i, c in enumerate((slice(0, KC // 2), slice(KC // 2, KC))):
                    dve.wait_ge(blk_hi, 2 * n + i + 1)
                    dve.tensor_tensor(ring_parts[:, n % RING, 0, c, :], ring[:, n % RING, 0, c, :],
                                      ring_parts[:, n % RING, 1, c, :].bitcast(F32), ALU.subtract).then_inc(blk_lo, 1)

            for t in range(NT):
                for half in range(2):
                    dve.wait_ge(h_turned, 2 * t + half + 1)
                    dve.tensor_tensor(hraw[:, 4 * half:4 * half + 4, P * t:P * t + P],
                                      HT_BANK[t][half].rearrange("p (c t) -> p c t", c=4),
                                      pc[:, 0, 4 * half:4 * half + 4, None].to_broadcast([P, 4, P]),
                                      ALU.mult).then_inc(h_ready, 1)
            for t in range(NT):
                dve.wait_ge(h_hi, t + 1)
                dve.tensor_tensor(hL[:, :, P * t:P * t + P], hraw[:, :, P * t:P * t + P],
                                  hH[:, :, P * t:P * t + P].bitcast(F32), ALU.subtract).then_inc(h_lo, 1)
            block_low(0)
            dve.wait_ge(small_done, 2)
            dve.wait_ge(gate_in, GATE_IN)
            dve.tensor_tensor(sm[:, :, :], SC[0][:, 256:336].rearrange("p (t n) -> p t n", t=NT),
                              bsm[:, None, :].to_broadcast([P, NT, 40]), ALU.add).then_inc(small_v, 1)
            dve.wait_ge(small_v, 1)
            dve.scalar_tensor_tensor(smw[:, 0, :, :], sm[:, :, :], -1.0, sm[:, :, :], ALU.mult, ALU.max)\
                .then_inc(small_v, 1)
            dve.wait_ge(small_a, 1)
            dve.tensor_scalar(smw[:, 2, :, :], smw[:, 1, :, :], 1.0, None, ALU.add).then_inc(small_v, 1)
            dve.wait_ge(small_v, 3)
            step(dve.scalar_tensor_tensor(smw[:, 4, :, :], smw[:, 2, :, :], -1.0, smw[:, 1, :, :], ALU.add, ALU.subtract))
            dve.wait_ge(small_a, 3)
            step(dve.tensor_tensor(smw[:, 5, :, :], smw[:, 3, :, :], smw[:, 4, :, :], ALU.subtract))
            softplus = smw[:, 5, :, :]
            step(dve.scalar_tensor_tensor(dtt[:, :, :], sm[:, :, 16:32], 0.0, softplus[:, :, 16:32], ALU.max, ALU.add))
            step(dve.scalar_tensor_tensor(gl[:, :, 0:16], sm[:, :, 0:16], 0.0, softplus[:, :, 0:16],
                                          ALU.min, ALU.subtract))
            step(dve.scalar_tensor_tensor(gl[:, :, 32:36], sm[:, :, 36:40], 0.0, softplus[:, :, 36:40],
                                          ALU.min, ALU.subtract))
            dve.scalar_tensor_tensor(gl[:, :, 16:32], dtt[:, :, :], -1.0, alog[:, None, :].to_broadcast([P, NT, 16]),
                                     ALU.mult, ALU.mult).then_inc(small_v, 1)

            def silu_of(u):
                i = conv_no[u]
                kind, n, part, chunk = UNITS[u]
                dve.wait_ge(conv_tanh, i + 1)
                dst = {"xbc": xbcT, "mq": qT, "mk": kT}[kind]
                dve.scalar_tensor_tensor(dst[:, chunk, :], thb[:, i % 3, :], 1.0, acc[:, i % 3, :], ALU.add, ALU.mult)\
                    .then_inc(conv_out, 1)

            def ssd_weights(h):
                b = h % 2
                dve.wait_ge(ssd_exp, h + 1)
                dve.wait_ge(ssd_cbm, h // 4 + 1)
                if h >= 4:
                    dve.wait_ge(ssd_out, h - 3)
                dve.tensor_tensor(work[:, 4 + h % 4, :], work[:, 2 + b, :], cbm[:, h // 4, :], ALU.mult).then_inc(ssd_w, 1)

            rv = 0

            def route(ins):
                nonlocal rv
                rv += 1
                ins.then_inc(r_v, 1)
                dve.wait_ge(r_v, rv)

            def x1_copy(t, half):
                dve.wait_ge(x1_turned, HALF_NO[t, half])
                dve.tensor_copy(x1T[:, 4 * half:4 * half + 4, P * t:P * t + P],
                                SC[half][:, :].rearrange("p (c t) -> p c t", c=4)).then_inc(x1_copied, 1)

            def x1_norm(t):
                dve.wait_ge(x1_sq, HALF_NO[t, 1])
                dve.tensor_tensor(ss[:, t:t + 1], rt[:, 8, t:t + 1], rt[:, 9, t:t + 1], ALU.add).then_inc(x1_sum, 1)
                dve.wait_ge(x1_root, t + 1)
                dve.reciprocal(ss[:, 4 + t:5 + t], ss[:, 2 + t:3 + t]).then_inc(x1_rstd, 1)
                dve.wait_ge(x1_rstd, t + 1)

            def choose(t):
                dve.wait_ge(logits, HALF_NO[t, 1])
                route(dve.scalar_tensor_tensor(lg[:, t, :], (TR, OB[0])[t][:, 0:NR], ss[:, 4 + t:5 + t], brow[:, :],
                                               ALU.mult, ALU.add))
                route(dve.max(top[:, t, :], lg[:, t, 0:NG]))
                route(dve.max_index(topi[:, t, :], top[:, t, :], lg[:, t, 0:NG]))
                route(dve.tensor_copy(rt[:, 0, t:t + 1], topi[:, t, 0:1]))
                route(dve.tensor_tensor(ohg[:, t, :], iota[:, 0:NG], rt[:, 0, t:t + 1].to_broadcast([P, NG]),
                                        ALU.is_equal))
                route(dve.tensor_tensor(egs[:, t, :, :], lg[:, t, NG:NR].rearrange("p (g e) -> p e g", g=NG),
                                        ohg[:, t, None, :].to_broadcast([P, EG, NG]), ALU.mult))
                route(dve.tensor_reduce(ein[:, t, :], egs[:, t, :, :], AX_X, ALU.add))
                route(dve.max(tope[:, t, :], ein[:, t, :]))
                route(dve.max_index(topi[:, t, :], tope[:, t, :], ein[:, t, :]))
                route(dve.tensor_copy(eid[:, t, :], topi[:, t, 0:2]))
                route(dve.scalar_tensor_tensor(eid[:, t, :], rt[:, 0, t:t + 1].to_broadcast([P, 2]), float(EG),
                                               eid[:, t, :], ALU.mult, ALU.add))
                route(dve.tensor_tensor(ohe[:, 2 * t:2 * t + 2, :], iota[:, None, 0:NE].to_broadcast([P, 2, NE]),
                                        eid[:, t, :, None].to_broadcast([P, 2, NE]), ALU.is_equal))
                dve.tensor_tensor(ohm[:, t, :], ohe[:, 2 * t, :], ohe[:, 2 * t + 1, :], ALU.add).then_inc(chosen, 1)

            def place(t):
                dve.wait_ge(ranked, t + 1)
                before = OB[1][:, 2 * NE * t:2 * NE * t + NE]
                if t == 0:
                    route(dve.tensor_copy(tally[:, :], OB[1][:, NE:2 * NE]))
                else:
                    route(dve.tensor_tensor(rke[:, 0, :], tally[:, :], before, ALU.add))
                    before = rke[:, 0, :]
                route(dve.tensor_tensor(rke[:, 2 * t:2 * t + 2, :], ohe[:, 2 * t:2 * t + 2, :],
                                        before[:, None, :].to_broadcast([P, 2, NE]), ALU.mult))
                route(dve.tensor_reduce(rank[:, 2 * t:2 * t + 2], rke[:, 2 * t:2 * t + 2, :], AX_X, ALU.add))
                dve.scalar_tensor_tensor(pos[:, 2 * t:2 * t + 2], eid[:, t, :], float(T), rank[:, 2 * t:2 * t + 2],
                                         ALU.mult, ALU.add).then_inc(placed, 1)
                dve.wait_ge(placed, t + 1)
                route(dve.tensor_scalar(pick[:, t, :], tgt, pos[:, 2 * t:2 * t + 1], None, ALU.is_equal))
                dve.scalar_tensor_tensor(pick[:, t, :], tgt, pos[:, 2 * t + 1:2 * t + 2], pick[:, t, :], ALU.is_equal,
                                         ALU.add).then_inc(first_pick, 1)

            router_after = {OUT0 + 3: [(x1_copy, 0, 0)],
                            OUT0 + 4: [(x1_copy, 1, 0)],
                            OUT0 + 5: [(x1_norm, 0), (x1_copy, 0, 1), (choose, 0)],
                            OUT0 + 7: [(x1_copy, 1, 1), (place, 0), (x1_norm, 1), (choose, 1), (place, 1)]}

            def u_low(oc):
                dve.wait_ge(u_hi, oc + 1)
                dve.tensor_tensor(zu_parts[:, oc, :], zu[:, oc, :], zuH[:, oc, :].bitcast(F32), ALU.subtract).then_inc(u_lo, 1)

            for u, (kind, n, part, chunk) in enumerate(UNITS):
                pj = PJ[u % BANKS]
                if u == OUT0:
                    u_low(KC - 1)
                if u in OPENS and OPENS[u] < NB:
                    block_low(OPENS[u])
                if u == OUT0:
                    route(dve.tensor_copy(first_blk, thr[:, None, :].to_broadcast([P, NE, 8])))
                    route(dve.memset(first_blk[:, 0:2, 0:1], 1e9))
                    route(dve.memset(gcst, float(T)))
                    route(dve.memset(gcst[:, 1:2], float(T - SLOT)))
                    for j in range(2):
                        route(dve.tensor_scalar(tgt[:, SLOT * j:SLOT * j + SLOT], iota[:, 0:SLOT], float(T * j), None,
                                                ALU.add))
                    dve.wait_ge(rt_in, 64)
                    dve.tensor_tensor(wrt[:, :, :], wrt[:, :, :], pc[:, 1, 104:112, None].to_broadcast([P, KC, NR]),
                                      ALU.mult).then_inc(wrt_ready, 1)
                if u in conv_no:
                    i = conv_no[u]
                    wi, w0, ch = (0, 8, chunk) if kind == "xbc" else (1, 0, chunk + (8 if kind == "mk" else 0))
                    dve.wait_ge(conv_pre, i + 1)
                    a = acc[:, i % 3, :]
                    for back in (1, 2, 3):
                        k = w0 + 16 * (3 - back) + ch
                        ins = dve.scalar_tensor_tensor(a[:, back:T], pj[:, 0:T - back], pc[:, wi, k:k + 1], a[:, back:T],
                                                       ALU.mult, ALU.add)
                        if back < 3:
                            step(ins)
                    ins.then_inc(conv_sum, 1)
                elif kind == "z":
                    i = u - Z0
                    dve.wait_ge(z_tanh, i + 1)
                    dve.scalar_tensor_tensor(zu[:, chunk, :], work[:, 8 + i % 2, 0:T], 1.0, pj[:, 0:T], ALU.add, ALU.mult)\
                        .then_inc(z_out, 1)
                elif kind == "br":
                    b, oc = divmod(chunk, KC)
                    dve.wait_ge(proj, u + 1)
                    if u == BR0:
                        dve.wait_ge(nrm_y, 8)
                    gate = gT[:, chunk, :]
                    if b == 0:
                        dve.scalar_tensor_tensor(zu[:, oc, :], gate, 1.0, pj[:, 0:T], ALU.add, ALU.mult)\
                            .then_inc(u_ready, 1)
                    else:
                        dve.wait_ge(u_ready, u - BR0 - 1)
                        step(dve.scalar_tensor_tensor(tmpu[:, u % 2, :], gate, 1.0, pj[:, 0:T], ALU.add, ALU.mult))
                        dve.tensor_tensor(zu[:, oc, :], zu[:, oc, :], tmpu[:, u % 2, :], ALU.add).then_inc(u_ready, 1)
                        if b == 2 and oc:
                            u_low(oc - 1)
                elif kind == "out":
                    dve.wait_ge(proj, u + 1)
                    xo = xs[:, part, T * chunk:T * chunk + T]
                    dve.scalar_tensor_tensor(xo, pj[:, 0:T], 0.5, xo, ALU.mult, ALU.add).then_inc(x1_part, 1)
                    dve.wait_ge(x1_part, u - OUT0 + 1)
                for job, *of in router_after.get(u, ()):
                    job(*of)
                if u and u - 1 in conv_no:
                    silu_of(u - 1)
                for stage, h in FOLLOW[u]:
                    if stage == "y_split":
                        dve.wait_ge(y_hi, h + 1)
                        dve.tensor_tensor(yL[:, h, :, :], yT[:, h, :, :], yH[:, h, :, :].bitcast(F32), ALU.subtract)\
                            .then_inc(y_lo, 1)
                    elif stage == "sums":
                        dve.wait_ge(cum_done, 1)
                        for t in range(NT):
                            dve.tensor_copy(cum[:, t, :], TR[:, 128 + 64 * t:164 + 64 * t]).then_inc(cum_ready, 1)
                        dve.wait_ge(cum_ready, 2)
                        dve.tensor_scalar(rn[:, :, 0:16], cum[:, :, 0:16], -1.0, None, ALU.mult).then_inc(cum_ready, 1)
                        dve.tensor_tensor(rn[:, :, 16:20], sm[:, :, 32:36], cum[:, :, 32:36], ALU.subtract).then_inc(cum_ready, 1)
                        dve.wait_ge(cum_ready, 4)
                        dve.tensor_copy(cols_hi[:, :, 0:20], rn[:, :, :]).then_inc(cols_ready, 1)
                        dve.tensor_copy(cols_hi[:, :, 20:36], cum[:, :, 16:32]).then_inc(cols_ready, 1)
                        dve.tensor_copy(identr[:, :], ident[:, :]).then_inc(cols_ready, 1)
                        dve.wait_ge(cols_ready, 2)
                        dve.tensor_tensor(cols_lo[:, :, 0:20], rn[:, :, :], cols_hi[:, :, 0:20].bitcast(F32),
                                          ALU.subtract).then_inc(cols_ready, 1)
                        dve.tensor_tensor(cols_lo[:, :, 20:36], cum[:, :, 16:32], cols_hi[:, :, 20:36].bitcast(F32),
                                          ALU.subtract).then_inc(cols_ready, 1)
                    elif stage == "fox_a":
                        b = h % 2
                        dve.wait_ge(fox_scores, h + 1)
                        if h >= 2:
                            dve.wait_ge(fox_exp, 2 * (h - 1))
                        dve.tensor_tensor_reduce(work[:, b, 0:T], SC[b][:, 0:T], mneg[:, :], 1.0, -3e38,
                                                 ALU.add, ALU.max, mx[:, b, 1:2]).then_inc(fox_masked, 1)
                        dve.tensor_tensor_reduce(work[:, b, T:384], SC[b][:, T:384], mneg[:, P:T], 1.0, -3e38,
                                                 ALU.add, ALU.max, mx[:, b, 0:1]).then_inc(fox_masked, 1)
                        dve.wait_ge(fox_masked, 2 * h + 2)
                        dve.tensor_scalar(nmx[:, b, :], mx[:, b, :], -1.0, None, ALU.mult).then_inc(fox_negmax, 1)
                    elif stage == "fox_p":
                        b = h % 2
                        dve.wait_ge(fox_exp, 2 * h + 2)
                        step(dve.reciprocal(rinv[:, b, :], rsum[:, b, :]))
                        p = work[:, 2 + b, :]
                        dve.tensor_scalar(p[:, 0:T], p[:, 0:T], rinv[:, b, 1:2], None, ALU.mult).then_inc(fox_probs, 1)
                        dve.tensor_scalar(p[:, T:384], p[:, T:384], rinv[:, b, 0:1], None, ALU.mult)\
                            .then_inc(fox_probs, 1)
                    elif stage == "fox_c" and h % 2:
                        dve.wait_ge(fox_out, h + 1)
                        dve.tensor_copy(yT[:, 0, h // 2, :], OB[(h // 2) % 2][:, 0:T]).then_inc(fox_y, 1)
                    elif stage == "ssd_x":
                        dve.wait_ge(ssd_turned, h + 1)
                        dve.tensor_tensor(
                            xdt[:, :, P * h:P * h + P].rearrange("p t (a d) -> p t a d", a=2),
                            (TR, OB[0])[h % 2][:, 0:T].rearrange("p (t a d) -> p t a d", t=NT, a=2),
                            dtt[:, :, 2 * h:2 * h + 2, None].to_broadcast([P, NT, 2, 64]), ALU.mult).then_inc(ssd_x, 1)
                    elif stage == "ssd_cb":
                        dve.wait_ge(ssd_cb, h + 1)
                        dve.tensor_tensor(cbm[:, h, :], OB[1][:, 0:384], mask01[:, :], ALU.mult).then_inc(ssd_cbm, 1)
                    elif stage == "ssd_a":
                        b = h % 2
                        dve.wait_ge(ssd_bc, h + 1)
                        if h >= 2:
                            dve.wait_ge(ssd_exp, h - 1)
                        dve.tensor_scalar(work[:, b, 0:T], SC[b][:, 0:T], cum[:, 0, 16 + h:17 + h], 0.0,
                                          ALU.subtract, ALU.min).then_inc(ssd_seg, 1)
                        dve.tensor_scalar(work[:, b, T:384], SC[b][:, P:T], cum[:, 1, 16 + h:17 + h], 0.0,
                                          ALU.subtract, ALU.min).then_inc(ssd_seg, 1)
                    elif stage == "ssd_w":
                        ssd_weights(h)
                    elif stage == "ssd_c" and h % 2:
                        c = h // 2
                        dve.wait_ge(ssd_out, h + 1)
                        dve.wait_ge(conv_out, 16)
                        dve.wait_ge(z_out, 8)
                        dve.scalar_tensor_tensor(yT[:, 1, c, :], xbcT[:, c, :], dsk[:, c:c + 1],
                                                 OB[c % 2][:, 0:T], ALU.mult, ALU.add).then_inc(ssd_y, 1)
                        dve.wait_ge(ssd_y, 2 * c + 1)
                        dve.scalar_tensor_tensor(yT[:, 1, c, :], yT[:, 1, c, :], 0.5, zu[:, c, :], ALU.mult, ALU.mult)\
                            .then_inc(ssd_y, 1)
                    elif stage == "norm_y":
                        k, g = divmod(h, 4)
                        dve.wait_ge(nrm_rt, h + 1)
                        step(dve.reciprocal(root[h % 4], root[h % 4]))
                        for c in (2 * g, 2 * g + 1):
                            wcol = pc[:, 0, (88 if k == 0 else 96) + c:(89 if k == 0 else 97) + c]
                            y = yT[:, 1 + k, c, :]
                            if k == 0:
                                dve.scalar_tensor_tensor(y, y, wcol, root[h % 4], ALU.mult, ALU.mult)\
                                    .then_inc(nrm_y, 1)
                            else:
                                step(dve.scalar_tensor_tensor(y, y, wcol, root[h % 4], ALU.mult, ALU.mult))
                                dve.scalar_tensor_tensor(y, moT[:, c, :], 1.0, y, ALU.add, ALU.mult)\
                                    .then_inc(nrm_y, 1)
                    elif stage == "ml_a":
                        dve.wait_ge(ml_scores, h + 1)
                        if h == 0:
                            dve.wait_ge(ssd_exp, 16)
                        dve.tensor_tensor_reduce(work[:, 0, 0:T], SC[1][:, 0:T], mneg[:, :], 1.0, -3e38,
                                                 ALU.add, ALU.max, mls[:, 0, 1:2]).then_inc(ml_neg, 1)
                        dve.tensor_tensor_reduce(work[:, 0, T:384], SC[1][:, 0:P], mneg[:, P:T], 1.0, -3e38,
                                                 ALU.add, ALU.max, mls[:, 0, 0:1]).then_inc(ml_neg, 1)
                        dve.wait_ge(ml_neg, ML_NEG * h + 2)
                        dve.tensor_scalar(mls[:, 1, :], mls[:, 0, :], 0.0, -1.0, ALU.max, ALU.mult).then_inc(ml_neg, 1)
                        dve.wait_ge(ml_neg, ML_NEG * h + 3)
                        dve.tensor_tensor(mls[:, 2, :], mls[:, 1, :], cum[:, :, 32 + h], ALU.subtract).then_inc(ml_neg, 1)
                    elif stage == "ml_w":
                        w = work[:, 2, :]
                        b0 = ML_W * h
                        if h:
                            dve.wait_ge(ml_turned, h)
                        dve.wait_ge(ml_exp, 3 * h + 3)
                        dve.tensor_tensor_reduce(w[:, 0:T], work[:, 1, 0:T], SC[0][:, 0:T], 256 ** -0.5, 0.0,
                                                 ALU.mult, ALU.add, mls[:, 4, 1:2]).then_inc(ml_w, 1)
                        dve.tensor_tensor_reduce(w[:, T:384], work[:, 1, T:384], SC[0][:, T:384], 256 ** -0.5, 0.0,
                                                 ALU.mult, ALU.add, mls[:, 4, 0:1]).then_inc(ml_w, 1)
                        dve.wait_ge(ml_w, b0 + 2)
                        step(dve.scalar_tensor_tensor(mls[:, 5, :], mls[:, 4, :], -1.0, mls[:, 4, :], ALU.mult, ALU.max))
                        step(dve.tensor_tensor(mls[:, 5, :], mls[:, 5, :], mls[:, 3, :], ALU.max))
                        step(dve.reciprocal(mls[:, 5, :], mls[:, 5, :]))
                        dve.tensor_scalar(w[:, 0:T], w[:, 0:T], mls[:, 5, 1:2], None, ALU.mult).then_inc(ml_w, 1)
                        dve.tensor_scalar(w[:, T:384], w[:, T:384], mls[:, 5, 0:1], None, ALU.mult).then_inc(ml_w, 1)
                    elif stage == "ml_c":
                        for i in range(2):
                            dve.wait_ge(ml_out, 2 * h + i + 1)
                            dve.tensor_copy(yT[:, 2, 2 * h + i, :], OB[i][:, 0:T]).then_inc(ml_y, 1)

            route(dve.tensor_tensor(tally[:, :], tally[:, :], OB[1][:, 3 * NE:4 * NE], ALU.add))
            route(dve.tensor_tensor(cnt8[:, :, :], tally[:, :, None].to_broadcast([P, NE, 8]), first_blk, ALU.is_gt))
            route(dve.tensor_reduce(nbk[:, 0, :], cnt8[:, :, :], AX_X, ALU.add))
            route(dve.tensor_tensor_scan(nbk[:, 1, :], ones[:, 0:NE], nbk[:, 0, :], 0.0, ALU.mult, ALU.add))
            route(dve.tensor_scalar(nbk[:, 2, :], nbk[:, 1, :], pidx[:, :], None, ALU.is_le))
            route(dve.tensor_reduce(itc[:, 1:2], nbk[:, 2, :], AX_X, ALU.add))
            route(dve.scalar_tensor_tensor(nbk[:, 0, :], nbk[:, 0, :], -float(SLOT), gcst, ALU.mult, ALU.add))
            route(dve.tensor_tensor_reduce(nbk[:, 0, :], nbk[:, 2, :], nbk[:, 0, :], 1.0, 0.0, ALU.mult, ALU.add,
                                           itc[:, 2:3]))
            dve.tensor_tensor(itc[:, 0:1], itc[:, 2:3], place0[:, :], ALU.add).then_inc(item_cols, 1)
            dve.wait_ge(gathered, 1)
            dve.tensor_tensor(xg, GAB[:, :].rearrange("p (c s) -> p c s", c=KC),
                              n2[:, :, None].to_broadcast([P, KC, 64]), ALU.mult).then_inc(xg_ready, 1)
            route(dve.tensor_scalar(npf[:, :], halfc[:, :], nbk[:, 1, NE - 1:NE], 0.5, ALU.add, ALU.mult))
            route(dve.tensor_scalar(base[:, :], iota[:, :], npf[:, 0:1], None, ALU.is_le))
            route(dve.tensor_reduce(npf[:, 0:1], base[:, :], AX_X, ALU.add))
            route(dve.tensor_scalar(base[:, :], iota[:, :], npf[:, 1:2], None, ALU.is_le))
            route(dve.tensor_reduce(npf[:, 1:2], base[:, :], AX_X, ALU.add))
            route(dve.tensor_scalar(npair[:, :], npf[:, :], -1.0, None, ALU.add))
            dve.wait_ge(item_rows, 1)
            route(dve.tensor_copy(base[:, :], OB[1][:, 256:384]))
            dve.tensor_copy(eint[:, :], OB[1][:, 384:512]).then_inc(items_ready, 1)
            route(dve.tensor_tensor(pe8[:, :, :], lg[:, :, 0:NG], top[:, :, 0:1].to_broadcast([P, NT, NG]),
                                    ALU.subtract))
            dve.tensor_tensor(rt[:, 3, :], tope[:, :, 1], tope[:, :, 0], ALU.subtract).then_inc(grp_sub, 1)
            dve.wait_ge(grp_exp, 2)
            route(dve.tensor_reduce(rt[:, 1, :], pe8[:, :, :], AX_X, ALU.add))
            route(dve.tensor_scalar(rt[:, 5, :], rt[:, 4, :], 1.0, None, ALU.add))
            route(dve.tensor_tensor(rt[:, 6, :], rt[:, 5, :], rt[:, 1, :], ALU.mult))
            route(dve.reciprocal(wtok[:, :, 0], rt[:, 6, :]))
            dve.wait_ge(r_v, rv)
            dve.tensor_tensor(wtok[:, :, 1], wtok[:, :, 0], rt[:, 4, :], ALU.mult).then_inc(weighed, 1)

            def pick_pair(cols, first):
                k = first
                dve.tensor_copy(bnxt[:, :], cols).then_inc(pick_v, 1)
                dve.wait_ge(pick_v, k + 1)
                dve.tensor_tensor(tgt.rearrange("p (j s) -> p j s", j=2), iota[:, None, 0:SLOT].to_broadcast([P, 2, SLOT]),
                                  bnxt[:, :, None].to_broadcast([P, 2, SLOT]), ALU.add).then_inc(pick_v, 1)
                dve.wait_ge(pick_v, k + 2)
                for t in range(NT):
                    dve.tensor_scalar(pick[:, t, :], tgt, pos[:, 2 * t:2 * t + 1], None, ALU.is_equal)\
                        .then_inc(pick_v, 1)
                dve.wait_ge(pick_v, k + 4)
                dve.scalar_tensor_tensor(pick[:, 0, :], tgt, pos[:, 1:2], pick[:, 0, :], ALU.is_equal, ALU.add)\
                    .then_inc(pick_v, 1)
                dve.wait_ge(pick_v, k + 5)
                dve.scalar_tensor_tensor(pick[:, 1, :], tgt, pos[:, 3:4], pick[:, 1, :], ALU.is_equal, ALU.add)\
                    .then_inc(picked, 1)

            def pair_weights(i, cols):
                dve.tensor_copy(bcur[:, :], cols)\
                    .then_inc(comb_v, 1)
                dve.wait_ge(comb_v, 4 * i + 1)
                dve.tensor_scalar(scol[:, :], bcur[:, :], pmod[:, :], None, ALU.add).then_inc(comb_v, 1)
                dve.wait_ge(comb_v, 4 * i + 2)
                dve.wait_ge(comb_done, 2 * i + 1)
                for j in range(2):
                    dve.scalar_tensor_tensor(combt, posb, scol[:, j:j + 1], wb, ALU.is_equal, ALU.mult)\
                        .then_inc(comb_v, 1)
                    dve.wait_ge(comb_v, 4 * i + (3 + j))
                    dve.tensor_tensor(comb[:, j, :], combt[:, 0:T], combt[:, T:2 * T], ALU.add).then_inc(combined, 1)
                    dve.wait_ge(combined, 2 * i + (j + 1))

            def hidden(i, j):
                tr = TRB[:, T * j:T * j + T].rearrange("p (i s) -> p i s", i=2)
                dve.wait_ge(hid_tanh, 2 * i + (j + 1))
                dve.scalar_tensor_tensor(gt1[:, j, :, :], tht[:, j, :, :], 1.0, tr[:, :, 0:64], ALU.add, ALU.mult)\
                    .then_inc(hid_v, 1)
                dve.wait_ge(hid_v, 4 * i + (2 * j + 1))
                dve.scalar_tensor_tensor(actT[:, j, :, :], gt1[:, j, :, :], 0.5, tr[:, :, 64:128],
                                         ALU.mult, ALU.mult).then_inc(hid_v, 1)

            def keep_gathered(i):
                dve.wait_ge(gathered, i + 2)
                dve.wait_ge(gu_done, 2 * i + 2)
                dve.tensor_tensor(xg, GAB[:, :].rearrange("p (c s) -> p c s", c=KC),
                                  n2[:, :, None].to_broadcast([P, KC, 64]), ALU.mult).then_inc(xg_ready, 1)

            hidden(0, 0)
            pick_pair(base[:, 2:4], 0)
            dve.wait_ge(rows_copied, 2)
            pair_weights(0, base[:, 0:2])
            hidden(0, 1)
            keep_gathered(0)
            pairs = dve.value_load(npair[0:1, 0:1], min_val=1, max_val=P // 2 - 1)
            whole = dve.value_load(npair[0:1, 1:2], min_val=0, max_val=P // 2 - 2) + 1
            with dve.If(whole > 1):
                with dve.Fori(1, whole) as i:
                    dve.wait_ge(gathered, i + 1)
                    pick_pair(base[:, bass.ds(2 * i + 2, 2)], 5 * i)
                    pair_weights(i, base[:, bass.ds(2 * i, 2)])
                    hidden(i, 0)
                    hidden(i, 1)
                    keep_gathered(i)
            with dve.If(pairs > whole):
                pair_weights(whole, base[:, bass.ds(2 * whole, 2)])
                hidden(whole, 0)

            dve.wait_ge(fw_in, 16)
            dve.wait_ge(fin_root, 1)
            dve.reciprocal(ss[:, 4:6], ss[:, 2:4]).then_inc(fin_rstd, 1)
            dve.wait_ge(fin_rstd, 1)
            for t in range(NT):
                dve.scalar_tensor_tensor(xs[:, t, :].rearrange("p (b n) -> p b n", b=4), acc4[:, :, T * t:T * t + T],
                                         ss[:, 4 + t:5 + t], fw.rearrange("p (b n) -> p b n", b=4),
                                         ALU.mult, ALU.mult).then_inc(fin_out, 1)


_INS = ["x", "norm1_w", "w_in", "att_f_bias", "ssd_conv_w", "ssd_conv_b", "ssd_dt_bias", "ssd_a_log", "ssd_d",
        "ssd_norm_w", "ml_conv_w", "ml_conv_b", "ml_i_bias", "ml_f_bias", "ml_norm_w", "gate_bias", "w_branch",
        "w_out", "norm2_w", "w_group", "b_group", "w_expert_router", "b_expert_router", "w_gate", "w_up", "w_down",
        "final_norm_w"]


def kernel(**inputs):
    import numpy as np
    import concourse.bacc as bacc
    from concourse.bass_utils import run_bass_kernel_spmd

    nc = bacc.Bacc("TRN2", target_bir_lowering=False, num_devices=1)
    arrays, args = {}, []
    for name in _INS:
        a = np.ascontiguousarray(inputs[name])
        arrays[f"in_{name}"] = a
        args.append(nc.dram_tensor(f"in_{name}", a.shape, mybir.dt.from_np(a.dtype), kind="ExternalInput").ap())
    args.append(nc.dram_tensor("out_0", inputs["x"].shape, F32, kind="ExternalOutput").ap())
    build_trunk(nc, *args)
    r = run_bass_kernel_spmd(nc, [arrays], core_ids=[0])
    return r.results[0]["out_0"]
```
